# Optimizing a Trainium2 kernel written in Bass

```python
import math
import jax, jax.numpy as jnp
from jax import lax
import numpy as np

"""Two layers of a hybrid diffusion/flow-matching backbone over latent tokens with a context prefix.

Inputs: x (BATCH, SEQ, D_MODEL) latent tokens on a flattened grid of width GRID_W; c (BATCH, D_MODEL)
conditioning vector; ctx (BATCH, CTX_LEN, D_MODEL) context tokens; c_ctx (D_MODEL,) learned context
modulation vector; per-layer weights stacked along a leading DEPTH axis.
Output: latent stream (BATCH, SEQ, D_MODEL).

Each layer: adaLN modulation -> one combined input projection partitioned into four parallel mixer
branches (multi-head latent attention, chunked spatial-gating MLP, differential attention,
bidirectional gated DeltaNet) each with its own SiLU gate path -> per-branch projection to D_MODEL ->
per-channel sigmoid merge gates -> output projection -> DeepNorm post-LayerNorm residual.
"""

D_MODEL = 1024
BATCH = 1
SEQ = 1024
DEPTH = 2

GRID_W = 64
CTX_LEN = 256
N_BRANCH = 4
BR_WIDTH = 256
MLA_HEADS = 4
MLA_NOPE = 64
MLA_ROPE = 32
MLA_V = 64
MLA_Q_LORA = 256
MLA_KV_LORA = 128
GMLP_GROUPS = 4
GMLP_CHUNK = 128
DIFF_HEADS = 4
DIFF_D = 32
DN_HEADS = 4
DN_DK = 64
DN_DV = 64
DN_CONV = 3
DN_CHUNK = 64

Q_BLOCK = 128
ROPE_BASE = 10000.0
LN_EPS = 1e-6
DEEPNORM_ALPHA = (2 * DEPTH) ** 0.25
DEEPNORM_BETA = (8 * DEPTH) ** -0.25

MLA_COLS = MLA_Q_LORA + MLA_KV_LORA + MLA_ROPE
GMLP_COLS = 2 * BR_WIDTH
DIFF_COLS = 3 * DIFF_HEADS * 2 * DIFF_D
DN_COLS = 3 * BR_WIDTH + 4 * DN_HEADS
GATE_COLS = N_BRANCH * BR_WIDTH
IN_COLS = MLA_COLS + GMLP_COLS + DIFF_COLS + DN_COLS + GATE_COLS
IN_SPLITS = [MLA_COLS, MLA_COLS + GMLP_COLS, MLA_COLS + GMLP_COLS + DIFF_COLS,
             MLA_COLS + GMLP_COLS + DIFF_COLS + DN_COLS]

kernel_name = "hybrid_mla_gmlp_diff_deltanet_prefix"

def layer_norm(x):
    xf = x.astype(jnp.float32)
    mu = jnp.mean(xf, -1, keepdims=True)
    var = jnp.mean(jnp.square(xf - mu), -1, keepdims=True)
    return ((xf - mu) * lax.rsqrt(var + LN_EPS)).astype(x.dtype)

def rms_norm(x, g):
    xf = x.astype(jnp.float32)
    return (xf * lax.rsqrt(jnp.mean(xf * xf, -1, keepdims=True) + LN_EPS)).astype(x.dtype) * g

def l2_normalize(x):
    xf = x.astype(jnp.float32)
    return (xf * lax.rsqrt(jnp.sum(xf * xf, -1, keepdims=True) + LN_EPS)).astype(x.dtype)

def axial_angles(n, rot_dim):
    rows = n // GRID_W
    row = jnp.repeat(jnp.arange(rows, dtype=jnp.float32), GRID_W)
    col = jnp.tile(jnp.arange(GRID_W, dtype=jnp.float32), rows)
    axis_dim = rot_dim // 2
    inv_freq = ROPE_BASE ** (-jnp.arange(0, axis_dim, 2, dtype=jnp.float32) / axis_dim)
    return row[:, None] * inv_freq, col[:, None] * inv_freq

def rope_1d(x, ang):
    cos = jnp.cos(ang)[None, :, None, :].astype(x.dtype)
    sin = jnp.sin(ang)[None, :, None, :].astype(x.dtype)
    x1, x2 = jnp.split(x, 2, axis=-1)
    return jnp.concatenate([x1 * cos - x2 * sin, x2 * cos + x1 * sin], -1)

def rope_2d(x, angles):
    ang_row, ang_col = angles
    xr, xc = jnp.split(x, 2, axis=-1)
    return jnp.concatenate([rope_1d(xr, ang_row), rope_1d(xc, ang_col)], -1)

def sweep_query_blocks(fn, *qs):
    b, t = qs[0].shape[:2]
    nb = t // Q_BLOCK
    blocks = tuple(jnp.swapaxes(q.reshape(b, nb, Q_BLOCK, *q.shape[2:]), 0, 1) for q in qs)
    out = lax.map(lambda blk: fn(*blk), blocks)
    return jnp.swapaxes(out, 0, 1).reshape(b, t, *out.shape[3:])

def softmax_probs(q, k, scale):
    s = jnp.einsum('bqhd,bkhd->bhqk', q, k).astype(jnp.float32) * scale
    return jax.nn.softmax(s, axis=-1)

def mla_project(p, q_norm, w_uq, kv_norm, w_ukv, angles):
    b, t = p.shape[:2]
    cq, ckv, kr = jnp.split(p, [MLA_Q_LORA, MLA_Q_LORA + MLA_KV_LORA], -1)
    q = (rms_norm(cq, q_norm) @ w_uq).reshape(b, t, MLA_HEADS, MLA_NOPE + MLA_ROPE)
    q_nope, q_rope = jnp.split(q, [MLA_NOPE], -1)
    kv = (rms_norm(ckv, kv_norm) @ w_ukv).reshape(b, t, MLA_HEADS, MLA_NOPE + MLA_V)
    k_nope, v = jnp.split(kv, [MLA_NOPE], -1)
    kr = kr[:, :, None, :]
    if angles is not None:
        q_rope = rope_2d(q_rope, angles)
        kr = rope_2d(kr, angles)
    q = jnp.concatenate([q_nope, q_rope], -1)
    k = jnp.concatenate([k_nope, jnp.broadcast_to(kr, (b, t, MLA_HEADS, MLA_ROPE))], -1)
    return q, k, v

def mla_branch(px, pc, angles, q_norm, w_uq, kv_norm, w_ukv, need_ctx):
    b, t = px.shape[:2]
    qx, kx, vx = mla_project(px, q_norm, w_uq, kv_norm, w_ukv, angles)
    qc, kc, vc = mla_project(pc, q_norm, w_uq, kv_norm, w_ukv, None)
    scale = (MLA_NOPE + MLA_ROPE) ** -0.5

    def attend(k, v):
        def block(qb):
            p = softmax_probs(qb, k, scale).astype(v.dtype)
            return jnp.einsum('bhqk,bkhd->bqhd', p, v)
        return block

    k_all = jnp.concatenate([kx, kc], 1)
    v_all = jnp.concatenate([vx, vc], 1)
    yx = sweep_query_blocks(attend(k_all, v_all), qx).reshape(b, t, BR_WIDTH)
    yc = sweep_query_blocks(attend(kc, vc), qc).reshape(b, pc.shape[1], BR_WIDTH) if need_ctx else None
    return yx, yc

def gmlp_branch(p, ln_g, w_s, b_s):
    b, t = p.shape[:2]
    z = jax.nn.gelu(p)
    u, v = jnp.split(z, 2, -1)
    v = layer_norm(v) * ln_g
    v = v.reshape(b, t // GMLP_CHUNK, GMLP_CHUNK, GMLP_GROUPS, BR_WIDTH // GMLP_GROUPS)
    v = jnp.einsum('gpq,bnqgc->bnpgc', w_s, v) + b_s.T[:, :, None]
    return u * v.reshape(b, t, BR_WIDTH)

def diff_project(p, angles):
    b, t = p.shape[:2]
    q, k, v = jnp.split(p, [2 * DIFF_HEADS * DIFF_D, 4 * DIFF_HEADS * DIFF_D], -1)
    q = q.reshape(b, t, DIFF_HEADS, 2, DIFF_D)
    k = k.reshape(b, t, DIFF_HEADS, 2, DIFF_D)
    q1, q2, k1, k2 = q[..., 0, :], q[..., 1, :], k[..., 0, :], k[..., 1, :]
    if angles is not None:
        q1, q2, k1, k2 = (rope_2d(a, angles) for a in (q1, q2, k1, k2))
    return q1, q2, k1, k2, v.reshape(b, t, DIFF_HEADS, 2 * DIFF_D)

def diff_branch(px, pc, angles, lq1, lk1, lq2, lk2, norm_g, lam_init, need_ctx):
    b, t = px.shape[:2]
    lam = (jnp.exp(jnp.sum((lq1 * lk1).astype(jnp.float32)))
           - jnp.exp(jnp.sum((lq2 * lk2).astype(jnp.float32))) + lam_init)
    scale = DIFF_D ** -0.5
    q1x, q2x, k1x, k2x, vx = diff_project(px, angles)
    q1c, q2c, k1c, k2c, vc = diff_project(pc, None)

    def attend(k1, k2, v):
        def block(q1b, q2b):
            p = softmax_probs(q1b, k1, scale) - lam * softmax_probs(q2b, k2, scale)
            return jnp.einsum('bhqk,bkhd->bqhd', p.astype(v.dtype), v)
        return block

    def finish(o):
        return (rms_norm(o, norm_g) * (1.0 - lam_init)).reshape(o.shape[0], o.shape[1], BR_WIDTH)

    k1_all = jnp.concatenate([k1x, k1c], 1)
    k2_all = jnp.concatenate([k2x, k2c], 1)
    v_all = jnp.concatenate([vx, vc], 1)
    yx = finish(sweep_query_blocks(attend(k1_all, k2_all, v_all), q1x, q2x))
    yc = finish(sweep_query_blocks(attend(k1c, k2c, vc), q1c, q2c)) if need_ctx else None
    return yx, yc

def short_conv(x, w):
    t = x.shape[1]
    pad = DN_CONV // 2
    xp = jnp.pad(x, ((0, 0), (pad, pad), (0, 0)))
    y = xp[:, 0:t] * w[0]
    for i in range(1, DN_CONV):
        y = y + xp[:, i:i + t] * w[i]
    return y

def dn_prep(p, conv_w, a_log, dt_bias):
    b, t = p.shape[:2]
    qkv, a, bb = jnp.split(p, [3 * BR_WIDTH, 3 * BR_WIDTH + 2 * DN_HEADS], -1)
    qkv = jax.nn.silu(short_conv(qkv, conv_w))
    q, k, v = jnp.split(qkv, 3, -1)
    q = l2_normalize(q.reshape(b, t, DN_HEADS, DN_DK)) * (DN_DK ** -0.5)
    k = l2_normalize(k.reshape(b, t, DN_HEADS, DN_DK))
    v = v.reshape(b, t, DN_HEADS, DN_DV)
    a = a.reshape(b, t, 2, DN_HEADS).astype(jnp.float32)
    bb = bb.reshape(b, t, 2, DN_HEADS).astype(jnp.float32)
    g = -jnp.exp(a_log.astype(jnp.float32)) * jax.nn.softplus(a + dt_bias.astype(jnp.float32))
    beta = jax.nn.sigmoid(bb)
    return q, k, v, g, beta

def gated_delta_chunked(q, k, v, g, beta, s0):
    b, t, h, _ = q.shape
    dv = v.shape[-1]
    n = t // DN_CHUNK

    def chunked(a):
        a = a.astype(jnp.float32).reshape(b, n, DN_CHUNK, h, *a.shape[3:])
        return jnp.moveaxis(a, (1, 3), (0, 2))

    qc, kc, vc, gc, bc = chunked(q), chunked(k), chunked(v), chunked(g), chunked(beta)
    gam = jnp.cumsum(gc, -1)
    idx = jnp.arange(DN_CHUNK)
    incl = idx[:, None] >= idx[None, :]
    strict = idx[:, None] > idx[None, :]
    decay = jnp.exp(jnp.where(incl, gam[..., :, None] - gam[..., None, :], -jnp.inf))
    kb = kc * bc[..., None]
    a_mat = jnp.where(strict, jnp.einsum('nbhid,nbhjd->nbhij', kb, kc) * decay, 0.0)
    m = a_mat + jnp.eye(DN_CHUNK, dtype=jnp.float32)
    u = lax.linalg.triangular_solve(m, vc * bc[..., None], left_side=True, lower=True, unit_diagonal=True)
    w = lax.linalg.triangular_solve(m, kb * jnp.exp(gam)[..., None], left_side=True, lower=True,
                                    unit_diagonal=True)
    qk = jnp.where(incl, jnp.einsum('nbhid,nbhjd->nbhij', qc, kc) * decay, 0.0)
    q_dec = qc * jnp.exp(gam)[..., None]
    k_dec = kc * jnp.exp(gam[..., -1:] - gam)[..., None]
    last = jnp.exp(gam[..., -1])

    def step(s, xs):
        u_i, w_i, qk_i, qd_i, kd_i, last_i = xs
        v_new = u_i - jnp.einsum('bhcd,bhde->bhce', w_i, s)
        o_i = jnp.einsum('bhcd,bhde->bhce', qd_i, s) + jnp.einsum('bhij,bhje->bhie', qk_i, v_new)
        s = s * last_i[..., None, None] + jnp.einsum('bhcd,bhce->bhde', kd_i, v_new)
        return s, o_i

    s, o = lax.scan(step, s0.astype(jnp.float32), (u, w, qk, q_dec, k_dec, last))
    o = jnp.moveaxis(o, (0, 2), (1, 3)).reshape(b, t, h, dv)
    return o, s

def run_direction(q, k, v, g, beta, s0, d):
    if d == 0:
        return gated_delta_chunked(q, k, v, g[:, :, 0], beta[:, :, 0], s0)
    fl = lambda a: jnp.flip(a, 1)
    o, s = gated_delta_chunked(fl(q), fl(k), fl(v), fl(g[:, :, 1]), fl(beta[:, :, 1]), s0)
    return fl(o), s

def deltanet_branch(px, pc, conv_w, a_log, dt_bias, norm_g, need_ctx):
    b, t = px.shape[:2]
    qx, kx, vx, gx, bx = dn_prep(px, conv_w, a_log, dt_bias)
    qc, kc, vc, gcx, bcx = dn_prep(pc, conv_w, a_log, dt_bias)
    s0 = jnp.zeros((b, DN_HEADS, DN_DK, DN_DV), jnp.float32)
    oc_f, sc_f = run_direction(qc, kc, vc, gcx, bcx, s0, 0)
    oc_b, sc_b = run_direction(qc, kc, vc, gcx, bcx, s0, 1)
    ox_f, _ = run_direction(qx, kx, vx, gx, bx, sc_f, 0)
    ox_b, _ = run_direction(qx, kx, vx, gx, bx, sc_b, 1)

    def finish(o):
        return rms_norm(o.astype(px.dtype), norm_g).reshape(o.shape[0], o.shape[1], BR_WIDTH)

    yx = finish(ox_f + ox_b)
    yc = finish(oc_f + oc_b) if need_ctx else None
    return yx, yc

def setup_inputs(seed: int = 0) -> dict:
    key = jax.random.key(seed)
    ks = iter(jax.random.split(key, 40))
    L, D = DEPTH, D_MODEL

    def nrm(shape, scale):
        return jax.random.normal(next(ks), shape, jnp.float32) * scale

    def gain(shape):
        return 1.0 + nrm(shape, 0.05)

    x = nrm((BATCH, SEQ, D), 1.0)
    c = nrm((BATCH, D), 1.0)
    ctx = nrm((BATCH, CTX_LEN, D), 1.0)
    c_ctx = nrm((D,), 1.0)
    w_mod = nrm((L, D, 3 * D), 0.5 * D ** -0.5)
    b_mod = nrm((L, 3 * D), 0.01)
    w_in = nrm((L, D, IN_COLS), D ** -0.5)
    mla_q_norm = gain((L, MLA_Q_LORA))
    mla_w_uq = nrm((L, MLA_Q_LORA, MLA_HEADS * (MLA_NOPE + MLA_ROPE)), MLA_Q_LORA ** -0.5)
    mla_kv_norm = gain((L, MLA_KV_LORA))
    mla_w_ukv = nrm((L, MLA_KV_LORA, MLA_HEADS * (MLA_NOPE + MLA_V)), MLA_KV_LORA ** -0.5)
    gmlp_ln_g = gain((L, BR_WIDTH))
    gmlp_w_s = nrm((L, GMLP_GROUPS, GMLP_CHUNK, GMLP_CHUNK), GMLP_CHUNK ** -0.5)
    gmlp_b_s = 1.0 + nrm((L, GMLP_GROUPS, GMLP_CHUNK), 0.05)
    diff_lq1 = nrm((L, DIFF_D), 0.1)
    diff_lk1 = nrm((L, DIFF_D), 0.1)
    diff_lq2 = nrm((L, DIFF_D), 0.1)
    diff_lk2 = nrm((L, DIFF_D), 0.1)
    diff_norm_g = gain((L, 2 * DIFF_D))
    dn_conv_w = nrm((L, DN_CONV, 3 * BR_WIDTH), DN_CONV ** -0.5)
    dn_a_log = jnp.log(jax.random.uniform(next(ks), (L, 2, DN_HEADS), jnp.float32, 1.0, 16.0))
    dt = jnp.exp(jax.random.uniform(next(ks), (L, 2, DN_HEADS), jnp.float32,
                                    math.log(1e-3), math.log(1e-1)))
    dn_dt_bias = dt + jnp.log(-jnp.expm1(-dt))
    dn_norm_g = gain((L, DN_DV))
    w_gate = nrm((L, N_BRANCH, D, D), D ** -0.5)
    w_branch = nrm((L, N_BRANCH, BR_WIDTH, D), DEEPNORM_BETA * BR_WIDTH ** -0.5)
    w_out = nrm((L, D, D), DEEPNORM_BETA * D ** -0.5)
    ln_g = gain((L, D))
    ln_b = nrm((L, D), 0.01)
    return {"x": x, "c": c, "ctx": ctx, "c_ctx": c_ctx, "w_mod": w_mod, "b_mod": b_mod, "w_in": w_in,
            "mla_q_norm": mla_q_norm, "mla_w_uq": mla_w_uq, "mla_kv_norm": mla_kv_norm,
            "mla_w_ukv": mla_w_ukv, "gmlp_ln_g": gmlp_ln_g, "gmlp_w_s": gmlp_w_s, "gmlp_b_s": gmlp_b_s,
            "diff_lq1": diff_lq1, "diff_lk1": diff_lk1, "diff_lq2": diff_lq2, "diff_lk2": diff_lk2,
            "diff_norm_g": diff_norm_g, "dn_conv_w": dn_conv_w, "dn_a_log": dn_a_log,
            "dn_dt_bias": dn_dt_bias, "dn_norm_g": dn_norm_g, "w_gate": w_gate, "w_branch": w_branch,
            "w_out": w_out, "ln_g": ln_g, "ln_b": ln_b}

def reference(x, c, ctx, c_ctx, w_mod, b_mod, w_in, mla_q_norm, mla_w_uq, mla_kv_norm, mla_w_ukv,
              gmlp_ln_g, gmlp_w_s, gmlp_b_s, diff_lq1, diff_lk1, diff_lq2, diff_lk2, diff_norm_g,
              dn_conv_w, dn_a_log, dn_dt_bias, dn_norm_g, w_gate, w_branch, w_out, ln_g, ln_b):
    n = x.shape[1]
    ang_mla = axial_angles(n, MLA_ROPE)
    ang_diff = axial_angles(n, DIFF_D)
    for l in range(DEPTH):
        need_ctx = l < DEPTH - 1
        lam_init = 0.8 - 0.6 * math.exp(-0.3 * l)
        mod_x = jax.nn.silu(c) @ w_mod[l] + b_mod[l]
        mod_c = jax.nn.silu(c_ctx) @ w_mod[l] + b_mod[l]
        sh_x, sc_x, gt_x = jnp.split(mod_x[:, None, :], 3, -1)
        sh_c, sc_c, gt_c = jnp.split(mod_c, 3, -1)
        hx = layer_norm(x) * (1.0 + sc_x) + sh_x
        hc = layer_norm(ctx) * (1.0 + sc_c) + sh_c
        px_a, px_b, px_c, px_d, px_g = jnp.split(hx @ w_in[l], IN_SPLITS, -1)
        pc_a, pc_b, pc_c, pc_d, pc_g = jnp.split(hc @ w_in[l], IN_SPLITS, -1)

        ya_x, ya_c = mla_branch(px_a, pc_a, ang_mla, mla_q_norm[l], mla_w_uq[l], mla_kv_norm[l],
                                mla_w_ukv[l], need_ctx)
        yb_x = gmlp_branch(px_b, gmlp_ln_g[l], gmlp_w_s[l], gmlp_b_s[l])
        yb_c = gmlp_branch(pc_b, gmlp_ln_g[l], gmlp_w_s[l], gmlp_b_s[l]) if need_ctx else None
        yc_x, yc_c = diff_branch(px_c, pc_c, ang_diff, diff_lq1[l], diff_lk1[l], diff_lq2[l], diff_lk2[l],
                                 diff_norm_g[l], lam_init, need_ctx)
        yd_x, yd_c = deltanet_branch(px_d, pc_d, dn_conv_w[l], dn_a_log[l], dn_dt_bias[l], dn_norm_g[l],
                                     need_ctx)

        def merge(h, branches, pgate):
            silu_gates = jnp.split(jax.nn.silu(pgate), N_BRANCH, -1)
            acc = None
            for i in range(N_BRANCH):
                term = jax.nn.sigmoid(h @ w_gate[l, i]) * ((branches[i] * silu_gates[i]) @ w_branch[l, i])
                acc = term if acc is None else acc + term
            return acc @ w_out[l]

        out_x = merge(hx, (ya_x, yb_x, yc_x, yd_x), px_g)
        x_new = layer_norm(DEEPNORM_ALPHA * x + gt_x * out_x) * ln_g[l] + ln_b[l]
        if need_ctx:
            out_c = merge(hc, (ya_c, yb_c, yc_c, yd_c), pc_g)
            ctx = layer_norm(DEEPNORM_ALPHA * ctx + gt_c * out_c) * ln_g[l] + ln_b[l]
        x = x_new
    return x


_drawn_inputs = setup_inputs


def setup_inputs(seed=0):
    import zlib

    import numpy as np

    out = dict(_drawn_inputs(seed))
    spreads = {}
    factors = {'ctx': 8.0,
     'c_ctx': 8.0,
     'b_mod': 8.0,
     'mla_q_norm': 8.0,
     'mla_w_uq': 8.0,
     'mla_kv_norm': 8.0,
     'mla_w_ukv': 7.922,
     'gmlp_ln_g': 8.0,
     'gmlp_w_s': 2.799,
     'gmlp_b_s': 8.0,
     'diff_lq1': 8.0,
     'diff_lk1': 8.0,
     'diff_lq2': 8.0,
     'diff_lk2': 8.0,
     'diff_norm_g': 8.0,
     'dn_a_log': 8.0,
     'dn_dt_bias': 6.681,
     'dn_norm_g': 8.0,
     'w_gate': 3.101,
     'ln_b': 3.987}
    for name, (base, spread) in spreads.items():
        noise = np.random.default_rng([zlib.crc32(name.encode()), seed]).standard_normal(out[name].shape)
        drawn = base * np.exp(spread * noise) if base else spread * noise
        out[name] = __import__('jax').numpy.asarray(drawn.astype(out[name].dtype))
    for name, factor in factors.items():
        out[name] = (out[name] * factor).astype(out[name].dtype)
    return out
```

```python
from contextlib import ExitStack, contextmanager

import concourse.bass as bass
from concourse import mybir

F32 = mybir.dt.float32
F32R = mybir.dt.float32r
ALU = mybir.AluOpType
ACT = mybir.ActivationFunctionType
AX = mybir.AxisListType
ds = bass.ds

P = 128
D = 1024
KD = D // P
CTX, SEQ = 256, 1024
ROWS = CTX + SEQ
NT = ROWS // P
CT = CTX // P
DEPTH = 2
BR = 256
HEADS = 4
NOPE, ROPE = 64, 32
QK = NOPE + ROPE
HD = 64
MAPS = 2 * HEADS
EPS = 1e-6
ALPHA = (2 * DEPTH) ** 0.25
CHUNKS = [(0, CTX), (CTX, 512), (CTX + 512, 512)]
T_MLA, T_DIFF, T_DN, T_GATE = 0, 4, 8, 14
R_GMLP, R_DV, R_AB, R_COLS = 0, 512, 768, 784
V_BMOD, V_QN, V_KVN, V_CONV, V_COLS = 0, 24, 26, 27, 45
B_LNG, B_LNB, B_GLN, B_DFN, B_DNN, B_LAM, B_ALOG, B_DTB, B_COLS = 0, 1024, 2048, 2304, 2368, 2432, 2560, 2568, 2576
C_ID, C_ONE, C_PERM, C_BLK, C_TRIF, C_TRIB, C_LVF, C_LVB, C_REP, C_N = 0, 1, 2, 3, 4, 5, 6, 13, 20, 28
LEVELS = 7


class Tally:

    def __init__(self, sem, base=0, i=None, per=0):
        self.sem, self.base, self.i, self.per, self.k = sem, base, i, per, 0

    def did(self, ins):
        self.k += 1
        ins.then_inc(self.sem, 1)

    def wait(self, eng):
        start = self.base if self.i is None else self.i * self.per + self.base
        eng.wait_ge(self.sem, start + self.k)

    def then(self, eng, ins):
        self.did(ins)
        self.wait(eng)

    def close(self):
        assert self.k == self.per, (self.k, self.per)


PHASES = []


@contextmanager
def phase(nc, *names):
    PHASES.append(names)
    sems = [nc.alloc_semaphore(f"{n}_{len(PHASES)}") for n in names]
    with nc.Block() as block:
        yield (block, *sems)
    nc.clear_and_free_semaphores(sems)
    nc.all_engine_barrier()


class Mem:
    pass


def split_products(pe, out, w_hi, w_lo, x_hi, x_lo, first, last):
    pe.matmul(out, w_hi, x_hi, start=first, stop=False)
    pe.matmul(out, w_hi, x_lo, start=False, stop=False)
    return pe.matmul(out, w_lo, x_hi, start=False, stop=last)


def modulation(nc, m, l):
    RING = 4
    with ExitStack() as st:
        sb = lambda n, s, d=F32: st.enter_context(nc.sbuf_tensor(f"{n}_mod{l}", s, d))
        w = sb("w", [P, RING, KD, P])
        c = sb("c", [P, KD, 2])
        sc = sb("sc", [P, KD, 2])
        gt = sb("gt", [16, P])
        ph = phase(nc, "c_in", "silu", "mod_done", "mod_added", "gate_t", "gate_copied", "gate_out",
                   *[f"w_in{s}" for s in range(RING)], "w_used")
        with ph as (block, c_in, silu, mod_done, mod_added, gate_t, gate_copied, gate_out, *rest):
            w_in, w_used = rest[:RING], rest[RING]
            GROUPS = 24 // RING

            @block.sync
            def _(sp):
                sp.dma_start(c[:], m.cvec).then_inc(c_in, 16)
                sp.dma_start(m.vec[:], m.d_vec[l]).then_inc(c_in, 16)
                for s in range(RING):
                    sp.dma_start(w[:, s], m.d_wmod[l, s]).then_inc(w_in[s], 16)
                with sp.Fori(1, GROUPS) as g:
                    for s in range(RING):
                        sp.wait_ge(w_used, g * RING + (s + 1 - RING))
                        sp.dma_start(w[:, s], m.d_wmod[l, g * RING + s]).then_inc(w_in[s], 16)
                sp.wait_ge(gate_copied, 1)
                sp.dma_start(m.d_gate, gt[:]).then_inc(gate_out, 16)
                sp.wait_ge(gate_out, 16)

            @block.scalar
            def _(act):
                act.wait_ge(c_in, 32)
                act.activation(sc[:], c[:], ACT.Silu).then_inc(silu, 1)

            @block.tensor
            def _(pe):
                pe.wait_ge(silu, 1)
                with pe.Fori(0, GROUPS) as g:
                    for s in range(RING):
                        pe.wait_ge(w_in[s], g * 16 + 16)
                        for k in range(KD):
                            mm = pe.matmul(m.ps[:, 0, ds((g * RING + s) * 2, 2)], w[:, s, k], sc[:, k],
                                           start=k == 0, stop=k == KD - 1)
                        mm.then_inc(w_used, 1)
                pe.drain().then_inc(mod_done, 1)
                pe.wait_ge(mod_added, 1)
                pe.transpose(m.ps[0:16, 1, 0:P], m.gate_c[:], m.ident).then_inc(gate_t, 1)

            @block.vector
            def _(dve):
                dve.wait_ge(c_in, 32)
                dve.wait_ge(mod_done, 1)
                dve.wait_ge(w_used, 24)
                mod = m.ps[:, 0, 0:48].rearrange("p (t c) -> p t c", c=2)
                bias = m.vec[:, V_BMOD:V_BMOD + 24].rearrange("p (t a) -> p t a", a=1)
                dve.tensor_tensor(m.gate_c[:].rearrange("p (c t) -> p t c", c=2), mod[:, 16:24],
                                  bias[:, 16:24].to_broadcast([P, 8, 2]), ALU.add).then_inc(mod_added, 1)
                dve.tensor_tensor(m.shift[:], mod[:, 0:8], bias[:, 0:8].to_broadcast([P, 8, 2]), ALU.add)
                dve.scalar_tensor_tensor(out=m.scale[:], in0=mod[:, 8:16], scalar=1.0,
                                         in1=bias[:, 8:16].to_broadcast([P, 8, 2]), op0=ALU.add, op1=ALU.add)
                dve.wait_ge(gate_t, 1)
                dve.tensor_copy(gt[:], m.ps[0:16, 1, 0:P]).then_inc(gate_copied, 1)


def normalise_rows(nc, m, l):
    SLOTS = 3
    src = m.d_x if l == 0 else m.d_x1
    with ExitStack() as st:
        sb = lambda n, s, d=F32: st.enter_context(nc.sbuf_tensor(f"{n}_ln{l}", s, d))
        x = sb("x", [P, SLOTS, D])
        h = sb("h", [P, 2, KD, P])
        stats = sb("stats", [P, NT, 2, 6])
        mv = sb("mv", [P, NT, 2])
        std = sb("std", [P, NT])
        rstd = sb("rstd", [P, NT])
        ph = phase(nc, *[f"x_in{s}" for s in range(SLOTS)], "var_done", "std_done", "dve_step", "xhat",
                   "turned", "scaled_d", "scaled_a", "high", "low")
        with ph as (block, *sems):
            x_in = sems[:SLOTS]
            var_done, std_done, dve_step, xhat, turned, scaled_d, scaled_a, high, low = sems[SLOTS:]

            @block.sync
            def _(sp):
                for t in range(NT):
                    if t >= SLOTS:
                        sp.wait_ge(turned, t - SLOTS + 1)
                    sp.dma_start(x[:, t % SLOTS], src[t * P:(t + 1) * P, :]).then_inc(x_in[t % SLOTS], 16)

            @block.vector
            def _(dve):
                step = Tally(dve_step)

                def part(t):
                    dve.wait_ge(turned, t + 1)
                    if t >= 2:
                        dve.wait_ge(high, t - 1)
                        dve.wait_ge(low, t - 1)
                    g = 0 if t >= CT else 1
                    for k in range(4):
                        ins = dve.tensor_scalar(h[:, t % 2, k], m.ps[:, 2 * (t % 2), k * P:(k + 1) * P],
                                                m.scale[:, k, g:g + 1], m.shift[:, k, g:g + 1], ALU.mult, ALU.add)
                    ins.then_inc(scaled_d, 1)
                    dve.wait_ge(high, t + 1)
                    dve.wait_ge(scaled_a, t + 1)
                    dve.tensor_tensor(m.hl[:, :, t * P:(t + 1) * P], h[:, t % 2],
                                      m.hh[:, :, t * P:(t + 1) * P].bitcast(F32), ALU.subtract).then_inc(low, 1)

                for t in range(NT):
                    xs = x[:, t % SLOTS]
                    dve.wait_ge(x_in[t % SLOTS], 16 * (t // SLOTS + 1))
                    for j in range(2):
                        ins = dve.bn_stats(stats[:, t, j], xs[:, 512 * j:512 * j + 512])
                    step.then(dve, ins)
                    dve.bn_aggr(mv[:, t], stats[:, t]).then_inc(var_done, 1)
                    dve.wait_ge(std_done, t + 1)
                    step.then(dve, dve.reciprocal(rstd[:, t:t + 1], std[:, t:t + 1]))
                    dve.tensor_scalar(xs, xs, mv[:, t, 0:1], rstd[:, t:t + 1], ALU.subtract, ALU.mult).then_inc(xhat, 1)
                    if t >= 1:
                        part(t - 1)
                part(NT - 1)

            @block.tensor
            def _(pe):
                for t in range(NT):
                    pe.wait_ge(xhat, t + 1)
                    if t >= 2:
                        pe.wait_ge(scaled_d, t - 1)
                        pe.wait_ge(scaled_a, t - 1)
                    for k in range(KD):
                        mm = pe.transpose(m.ps[:, 2 * (t % 2) + k // 4, (k % 4) * P:(k % 4 + 1) * P],
                                          x[:, t % SLOTS, k * P:(k + 1) * P], m.ident)
                    mm.then_inc(turned, 1)

            @block.scalar
            def _(act):
                def part(t):
                    act.wait_ge(turned, t + 1)
                    if t >= 2:
                        act.wait_ge(low, t - 1)
                    g = 0 if t >= CT else 1
                    for k in range(4, KD):
                        ins = act.activation(h[:, t % 2, k], m.ps[:, 2 * (t % 2) + 1, (k - 4) * P:(k - 3) * P],
                                             ACT.Identity, bias=m.shift[:, k, g:g + 1], scale=m.scale[:, k, g:g + 1])
                    ins.then_inc(scaled_a, 1)
                    act.wait_ge(scaled_a, t + 1)
                    act.wait_ge(scaled_d, t + 1)
                    act.activation(m.hh[:, :, t * P:(t + 1) * P], h[:, t % 2], ACT.Copy).then_inc(high, 1)

                for t in range(NT):
                    act.wait_ge(var_done, t + 1)
                    act.activation(std[:, t:t + 1], mv[:, t, 1:2], ACT.Sqrt, bias=m.eps[:, 0:1]).then_inc(std_done, 1)
                    if t >= 1:
                        part(t - 1)
                part(NT - 1)


def project(nc, m, l, first, tiles, out, chunks, name):
    with ExitStack() as st:
        sb = lambda n, s, d=F32: st.enter_context(nc.sbuf_tensor(f"{n}_{name}{l}", s, d))
        w = sb("w", [P, 2, KD, P])
        wh = sb("wh", [P, 2, KD, P], F32R)
        wl = sb("wl", [P, 2, KD, P], F32R)
        n = len(chunks)
        ph = phase(nc, "w_in0", "w_in1", "w_high", "w_low", "made", "free_a", "free_d")
        with ph as (block, w_in0, w_in1, w_high, w_low, made, free_a, free_d):
            w_in = [w_in0, w_in1]
            per = [sum((s * n + c) % 2 == e for s in range(2) for c in range(n)) for e in range(2)]
            order = [(s, c) for s in range(2) for c in range(n)]

            def nth(s, c):
                return sum((a * n + b) % 2 == (s * n + c) % 2 for a, b in order[:order.index((s, c))])

            @block.sync
            def _(sp):
                for s in range(2):
                    sp.dma_start(w[:, s], m.d_win[l, first + s]).then_inc(w_in[s], 16)
                if tiles > 2:
                    with sp.Fori(1, tiles // 2) as i:
                        for s in range(2):
                            sp.wait_ge(w_low, i * 2 + (s - 1))
                            sp.dma_start(w[:, s], m.d_win[l, i * 2 + (first + s)]).then_inc(w_in[s], 16)

            def moves(eng, e, copy):
                eng.sem_inc(free_a if e == 0 else free_d, per[e])

                def cut(i, s):
                    eng.wait_ge(w_in[s], i * 16 + 16)
                    if e == 0:
                        eng.wait_ge(made, i * (2 * n) + (s + 1) * n)
                        eng.activation(wh[:, s], w[:, s], ACT.Copy).then_inc(w_high, 1)
                    else:
                        eng.wait_ge(w_high, i * 2 + (s + 1))
                        eng.tensor_tensor(wl[:, s], w[:, s], wh[:, s].bitcast(F32), ALU.subtract).then_inc(w_low, 1)

                def body(i, last):
                    for s in range(2):
                        for c, (at, width) in enumerate(chunks):
                            if c == 1 and not (last and s == 1):
                                cut(i + s, 1 - s)
                            if (s * n + c) % 2 == e:
                                eng.wait_ge(made, i * (2 * n) + (2 * n + s * n + c + 1))
                                ins = copy(out[:, i * 2 + s, at:at + width], m.ps[:, s * n + c, 0:width])
                                ins.then_inc(free_a if e == 0 else free_d, 1)

                cut(0, 0)
                if tiles > 2:
                    with eng.Fori(0, tiles // 2 - 1) as i:
                        body(i, False)
                body(tiles // 2 - 1, True)

            @block.scalar
            def _(act):
                moves(act, 0, lambda o, i: act.activation(o, i, ACT.Copy))

            @block.vector
            def _(dve):
                moves(dve, 1, lambda o, i: dve.tensor_copy(o, i))

            @block.tensor
            def _(pe):
                pe.sem_inc(made, 2 * n)
                with pe.Fori(0, tiles // 2) as i:
                    for s in range(2):
                        pe.wait_ge(w_low, i * 2 + (s + 1))
                        for c, (at, width) in enumerate(chunks):
                            e = (s * n + c) % 2
                            pe.wait_ge(free_d if e else free_a, i * per[e] + (nth(s, c) + 1))
                            for k in range(KD):
                                mm = split_products(pe, m.ps[:, s * n + c, 0:width], wh[:, s, k], wl[:, s, k],
                                                    m.hh[:, k, at:at + width], m.hl[:, k, at:at + width],
                                                    k == 0, k == KD - 1)
                            mm.then_inc(made, 1)


def turn_out(nc, m, l, branch, y_rows, y_t, tiles, y_ready, turned, copied, stored):
    def tensor(pe):
        for n, t in enumerate(tiles):
            pe.wait_ge(y_ready, n + 1)
            if n >= 2:
                pe.wait_ge(copied, n - 1)
            for b in range(2):
                mm = pe.transpose(m.ps[:, 6 + n % 2, b * P:(b + 1) * P], y_rows(t)[:, b * P:(b + 1) * P], m.ident)
            mm.then_inc(turned, 1)

    def vector(dve, n, t):
        dve.wait_ge(turned, n + 1)
        dve.tensor_copy(y_t[:, :, t * P:(t + 1) * P],
                        m.ps[:, 6 + n % 2, 0:BR].rearrange("p (b c) -> p b c", b=2)).then_inc(copied, 1)

    def store(sp):
        at = tiles[0] * P
        sp.wait_ge(copied, len(tiles))
        sp.dma_start(m.d_y[:, 2 * branch:2 * branch + 2, at:ROWS], y_t[:, :, at:ROWS]).then_inc(stored, 16)
        sp.wait_ge(stored, 16)
    return tensor, vector, store


def gating_mlp(nc, m, l):
    tiles = range(0 if l < DEPTH - 1 else CT, NT)
    with ExitStack() as st:
        sb = lambda n, s, d=F32: st.enter_context(nc.sbuf_tensor(f"{n}_gm{l}", s, d))
        w = sb("w", [P, 2, R_COLS])
        wh = sb("wh", [P, KD, R_COLS], F32R)
        wl = sb("wl", [P, KD, R_COLS], F32R)
        z = sb("z", [P, NT, 2, BR])
        ws = sb("ws", [P, HEADS, P])
        bs = sb("bs", [P, HEADS])
        g = sb("g", [P, BR])
        y_t = sb("y_t", [P, 2, ROWS])
        stats = sb("stats", [P, NT, 6])
        mv = sb("mv", [P, NT, 2])
        std = sb("std", [P, NT])
        rstd = sb("rstd", [P, NT])
        ph = phase(nc, "w_in0", "w_in1", "small_in", "w_high", "w_low", "made", "gelu", "kept", "stat", "std_done",
                   "dve_step", "v_ready", "mixed", "y_ready", "turned", "copied", "stored")
        with ph as (block, w_in0, w_in1, small_in, w_high, w_low, made, gelu, kept, stat, std_done,
                    dve_step, v_ready, mixed, y_ready, turned, copied, stored):
            w_in = [w_in0, w_in1]
            turn, copy_turned, store = turn_out(nc, m, l, 1, lambda t: z[:, t, 1], y_t, tiles,
                                                y_ready, turned, copied, stored)

            @block.sync
            def _(sp):
                sp.dma_start(ws[:], m.d_ws[l]).then_inc(small_in, 16)
                sp.dma_start(bs[:], m.d_bs[l]).then_inc(small_in, 16)
                sp.dma_start(g[:], m.d_bvec[l:l + 1, B_GLN:B_GLN + BR].to_broadcast([P, BR])).then_inc(small_in, 16)
                for k in range(KD):
                    if k >= 2:
                        sp.wait_ge(w_low, k - 1)
                    sp.dma_start(w[:, k % 2], m.d_winr[l, k]).then_inc(w_in[k % 2], 16)
                store(sp)

            @block.scalar
            def _(act):
                for k in range(KD):
                    act.wait_ge(w_in[k % 2], 16 * (k // 2 + 1))
                    act.activation(wh[:, k], w[:, k % 2], ACT.Copy).then_inc(w_high, 1)
                for n, t in enumerate(tiles):
                    act.wait_ge(made, t + 1)
                    act.activation(z[:, t], m.ps[:, 2 * (t % 2), 0:512].rearrange("p (a b) -> p a b", a=2),
                                   ACT.Gelu_apprx_tanh).then_inc(gelu, 1)
                act.wait_ge(stat, 1)
                act.activation(std[:, tiles[0]:], mv[:, tiles[0]:, 1], ACT.Sqrt, bias=m.eps[:, 0:1]).then_inc(std_done, 1)

            @block.tensor
            def _(pe):
                pe.wait_ge(w_low, KD)
                for t in range(NT):
                    if t >= 2:
                        pe.wait_ge(kept, t - 1)
                        if t - 2 in tiles:
                            pe.wait_ge(gelu, t - 1 - tiles[0])
                    for b, (at, width) in enumerate(((R_GMLP, 512), (R_DV, R_COLS - R_DV))):
                        if b == 0 and t not in tiles:
                            continue
                        for k in range(KD):
                            h = [x[:, k, t * P:(t + 1) * P] for x in (m.hh, m.hl)]
                            mm = split_products(pe, m.ps[:, 2 * (t % 2) + b, 0:width], *h,
                                                wh[:, k, at:at + width], wl[:, k, at:at + width], k == 0, k == KD - 1)
                    mm.then_inc(made, 1)
                pe.wait_ge(small_in, 48)
                for n, t in enumerate(tiles):
                    pe.wait_ge(v_ready, n + 1)
                    if n >= 2:
                        pe.wait_ge(y_ready, n - 1)
                    for h in range(HEADS):
                        mm = pe.matmul(m.ps[:, 4 + n % 2, h * HD:(h + 1) * HD], ws[:, h],
                                       z[:, t, 1, h * HD:(h + 1) * HD], start=True, stop=True)
                    mm.then_inc(mixed, 1)
                turn(pe)

            @block.vector
            def _(dve):
                step = Tally(dve_step)
                for k in range(KD):
                    dve.wait_ge(w_high, k + 1)
                    dve.tensor_tensor(wl[:, k], w[:, k % 2], wh[:, k].bitcast(F32), ALU.subtract).then_inc(w_low, 1)
                for t in range(NT):
                    dve.wait_ge(made, t + 1)
                    dve.tensor_copy(m.dv[:, t], m.ps[:, 2 * (t % 2) + 1, 0:BR])
                    dve.tensor_copy(m.ab[:, t], m.ps[:, 2 * (t % 2) + 1, BR:BR + 16]).then_inc(kept, 1)
                    if t in tiles:
                        dve.wait_ge(gelu, t + 1 - tiles[0])
                        step.then(dve, dve.bn_stats(stats[:, t], z[:, t, 1]))
                        ins = dve.bn_aggr(mv[:, t], stats[:, t])
                ins.then_inc(stat, 1)
                dve.wait_ge(std_done, 1)
                step.then(dve, dve.reciprocal(rstd[:, tiles[0]:], std[:, tiles[0]:]))
                dve.wait_ge(small_in, 48)
                for n, t in enumerate(tiles):
                    v = z[:, t, 1]
                    step.then(dve, dve.tensor_scalar(v, v, mv[:, t, 0:1], rstd[:, t:t + 1], ALU.subtract, ALU.mult))
                    dve.tensor_tensor(v, v, g[:], ALU.mult).then_inc(v_ready, 1)
                for n, t in enumerate(tiles):
                    dve.wait_ge(mixed, n + 1)
                    for h in range(HEADS):
                        part = slice(h * HD, (h + 1) * HD)
                        ins = dve.scalar_tensor_tensor(out=z[:, t, 1, part], in0=m.ps[:, 4 + n % 2, part],
                                                       scalar=bs[:, h:h + 1], in1=z[:, t, 0, part],
                                                       op0=ALU.add, op1=ALU.mult)
                    ins.then_inc(y_ready, 1)
                for n, t in enumerate(tiles):
                    copy_turned(dve, n, t)


def normalise_columns(nc, m, l, name, out, tiles, ones, factor, mean, gain, chunks=CHUNKS):
    with ExitStack() as st:
        sb = lambda n, s, d=F32: st.enter_context(nc.sbuf_tensor(f"{n}_{name}{l}", s, d))
        steps = [(grp, c) for grp in tiles for c in range(len(chunks))]
        wide = max(len(g) for g in tiles)
        sq = sb("sq", [P, 2, wide, 512])
        std = sb("std", [P, 2, 512])
        inv = sb("inv", [P, 2, 512])
        with phase(nc, "squared", "summed", "rooted", "inverted", "scaled") as (
                block, squared, summed, rooted, inverted, scaled):
            @block.gpsimd
            def _(pool):
                for n, (grp, c) in enumerate(steps):
                    at, width = chunks[c]
                    if n >= 2:
                        pool.wait_ge(summed, n - 1)
                    for a, j in enumerate(grp):
                        x = out[:, j, at:at + width]
                        ins = pool.tensor_tensor(sq[:, n % 2, a, 0:width], x, x, ALU.mult)
                    ins.then_inc(squared, 1)

            @block.tensor
            def _(pe):
                for n, (grp, c) in enumerate(steps):
                    width = chunks[c][1]
                    pe.wait_ge(squared, n + 1)
                    if n >= 2:
                        pe.wait_ge(rooted, n - 1)
                    for a in range(len(grp)):
                        mm = pe.matmul(m.ps[:, n % 2, 0:width], ones, sq[:, n % 2, a, 0:width],
                                       start=a == 0, stop=a == len(grp) - 1)
                    mm.then_inc(summed, 1)

            @block.scalar
            def _(act):
                for n, (grp, c) in enumerate(steps):
                    width = chunks[c][1]
                    act.wait_ge(summed, n + 1)
                    if n >= 2:
                        act.wait_ge(inverted, n - 1)
                    act.activation(std[:, n % 2, 0:width], m.ps[:, n % 2, 0:width], ACT.Sqrt, bias=m.eps[:, 0:1],
                                   scale=1.0 / mean(grp)).then_inc(rooted, 1)

            @block.vector
            def _(dve):
                for n, (grp, c) in enumerate(steps):
                    at, width = chunks[c]
                    dve.wait_ge(rooted, n + 1)
                    dve.reciprocal(inv[:, n % 2, 0:width], std[:, n % 2, 0:width]).then_inc(inverted, 1)
                    dve.wait_ge(inverted, n + 1)
                    dve.wait_ge(squared, n + 1)
                    for j in grp:
                        x = out[:, j, at:at + width]
                        f = gain(j) if gain else factor(j)
                        ins = dve.scalar_tensor_tensor(out=x, in0=x, scalar=f, in1=inv[:, n % 2, 0:width],
                                                       op0=ALU.mult, op1=ALU.mult)
                    ins.then_inc(scaled, 1)


def rotate_columns(nc, m, l, name, items):
    steps = [(x, c) for x in items for c in (1, 2)]
    with ExitStack() as st:
        sb = lambda n, s, d=F32: st.enter_context(nc.sbuf_tensor(f"{n}_{name}{l}", s, d))
        cos = sb("cos", [P, 2, SEQ])
        a = sb("a", [P, 2, 512])
        b = sb("b", [P, 2, 512])
        perm = sb("perm", [P, P])
        with phase(nc, "table_in", "swapped", "with_sin", "with_cos", "rotated") as (
                block, table_in, swapped, with_sin, with_cos, rotated):
            @block.sync
            def _(sp):
                sp.dma_start(cos[:], m.d_rope).then_inc(table_in, 16)
                sp.dma_start(perm[:], m.d_const[:, C_PERM]).then_inc(table_in, 16)

            @block.tensor
            def _(pe):
                pe.wait_ge(table_in, 32)
                for n, (x, c) in enumerate(steps):
                    at, width = CHUNKS[c]
                    q = x.shape[0]
                    if n >= 2:
                        pe.wait_ge(with_sin, n - 1)
                    pe.matmul(m.ps[0:q, n % 2, 0:width], perm[0:q, 0:q], x[:, at:at + width],
                              start=True, stop=True).then_inc(swapped, 1)

            @block.gpsimd
            def _(pool):
                pool.wait_ge(table_in, 32)
                for n, (x, c) in enumerate(steps):
                    at, width = CHUNKS[c]
                    q = x.shape[0]
                    if n >= 2:
                        pool.wait_ge(rotated, n - 1)
                    pool.tensor_tensor(b[0:q, n % 2], x[:, at:at + width], cos[0:q, 0, at - CTX:at - CTX + width],
                                       ALU.mult).then_inc(with_cos, 1)

            @block.vector
            def _(dve):
                dve.wait_ge(table_in, 32)
                for n, (x, c) in enumerate(steps):
                    at, width = CHUNKS[c]
                    q = x.shape[0]
                    dve.wait_ge(swapped, n + 1)
                    dve.tensor_tensor(a[0:q, n % 2], m.ps[0:q, n % 2, 0:width],
                                      cos[0:q, 1, at - CTX:at - CTX + width], ALU.mult).then_inc(with_sin, 1)
                    dve.wait_ge(with_sin, n + 1)
                    dve.wait_ge(with_cos, n + 1)
                    dve.tensor_tensor(x[:, at:at + width], a[0:q, n % 2], b[0:q, n % 2], ALU.add).then_inc(rotated, 1)


def expand_latents(nc, m, l, raw, q, k, v, qr):
    with ExitStack() as st:
        sb = lambda n, s, d=F32: st.enter_context(nc.sbuf_tensor(f"{n}_ex{l}", s, d))
        wq = sb("wq", [P, 2, HEADS * QK])
        wkv = sb("wkv", [P, 2 * HEADS * HD])
        jobs = []
        for at, width in CHUNKS:
            cols = slice(at, at + width)
            jobs.append((qr[:, cols], P, width, [(wq[:, j, 0:P], raw[:, j, cols]) for j in range(2)]))
            for h in range(HEADS):
                own = slice(P + h * NOPE, P + (h + 1) * NOPE)
                jobs.append((q[0:NOPE, h, cols], NOPE, width, [(wq[:, j, own], raw[:, j, cols]) for j in range(2)]))
                jobs.append((k[0:NOPE, h, cols], NOPE, width,
                             [(wkv[:, h * NOPE:(h + 1) * NOPE], raw[:, 2, cols])]))
        for t in range(NT):
            jobs.append((v[:, t], P, BR, [(raw[:, 2, t * P:(t + 1) * P], wkv[:, HEADS * NOPE:])]))
        with phase(nc, "w_in", "made", "moved_a", "moved_d") as (block, w_in, made, moved_a, moved_d):
            @block.sync
            def _(sp):
                sp.dma_start(wq[:], m.d_wuq[l]).then_inc(w_in, 16)
                sp.dma_start(wkv[:], m.d_wukv[l]).then_inc(w_in, 16)

            @block.tensor
            def _(pe):
                pe.wait_ge(w_in, 32)
                for n, (_, rows, width, pairs) in enumerate(jobs):
                    if n >= 4:
                        pe.wait_ge(moved_d if n % 2 else moved_a, (n - 4) // 2 + 1)
                    for a, (lhs, rhs) in enumerate(pairs):
                        mm = pe.matmul(m.ps[0:rows, n % 4, 0:width], lhs, rhs, start=a == 0, stop=a == len(pairs) - 1)
                    mm.then_inc(made, 1)

            @block.scalar
            def _(act):
                for n in range(0, len(jobs), 2):
                    out, rows, width, _ = jobs[n]
                    act.wait_ge(made, n + 1)
                    act.activation(out, m.ps[0:rows, n % 4, 0:width], ACT.Copy).then_inc(moved_a, 1)

            @block.vector
            def _(dve):
                for n in range(1, len(jobs), 2):
                    out, rows, width, _ = jobs[n]
                    dve.wait_ge(made, n + 1)
                    dve.tensor_copy(out, m.ps[0:rows, n % 4, 0:width]).then_inc(moved_d, 1)


def place_rotated(nc, m, l, raw, q, k, qr):
    with phase(nc, "done") as (block, done):
        @block.gpsimd
        def _(pool):
            for h in range(HEADS):
                pool.tensor_copy(k[NOPE:QK, h], raw[0:ROPE, 3])

        @block.vector
        def _(dve):
            for h in range(HEADS):
                dve.tensor_copy(q[NOPE:QK, h], qr[h * ROPE:(h + 1) * ROPE, :])


def attention(nc, m, l, name, q_part, k_all, v, y, qs, key_tiles, t0, t1, scale, maps, neg_lam, e=None):
    keys = key_tiles * P
    pieces = [(at, min(512, keys - at)) for at in range(0, keys, 512)]
    groups = [(0, 4), (4, 2), (6, 4)] if key_tiles == NT else [(0, CT)]
    G = len(groups)
    n_tiles = t1 - t0
    on_act = [g for g in range(G) if g % 2 == 1 or maps == 2]
    on_dve = [g for g in range(G) if g not in on_act]
    SL = 2 // maps
    LAG = 2
    copies = len(q_part(0, 0))
    with ExitStack() as st:
        sb = lambda n, s, d=F32: st.enter_context(nc.sbuf_tensor(f"{n}_{name}{l}_{t0}", s, d))
        if e is None:
            e = sb("e", [P, 2, maps, keys])
        pt = sb("pt", [P, 2, key_tiles, P])
        mx = sb("mx", [P, HEADS, maps])
        nmx = sb("nmx", [P, HEADS, maps])
        total = sb("total", [P, HEADS, maps])
        inv = sb("inv", [P, HEADS, maps])
        own = sb("own", [P, HEADS])
        with phase(nc, "staged", "scored", "maximum", "bias", "exp_done", "inverse", "mixed",
                   "turned", "moved_a", "moved_d", "valued", "y_done", "dve_step", "mixing", "kept") as (
                block, staged, scored, maximum, bias, exp_done, inverse, mixed,
                turned, moved_a, moved_d, valued, y_done, dve_step, mixing, kept):

            def bank(h, a):
                return 3 * (h % 2 if maps == 1 else a)

            def turn_bank(g, count):
                return m.ps[:, 7, BR:BR + count * P] if g == 1 else m.ps[:, 6, 0:count * P]

            def loop(eng, body, tail):
                body(0, False)
                with eng.Fori(1, n_tiles) as i:
                    body(i, True)
                tail(n_tiles)

            @block.gpsimd
            def _(pool):
                def body(i, prior):
                    for h in range(HEADS):
                        if prior:
                            pool.wait_ge(scored, i * (HEADS * maps) + (h - HEADS + 1) * maps)
                        for slot, src in q_part(h, i + t0):
                            pool.tensor_copy(slot, src).then_inc(staged, 1)
                loop(pool, body, lambda i: None)

            @block.tensor
            def _(pe):
                def turn(i, h, g):
                    at, count = groups[g]
                    u = i * HEADS + h
                    if maps == 1:
                        pe.wait_ge(exp_done, u + 1)
                    else:
                        pe.wait_ge(mixed, u + 1)
                    first = isinstance(i, int) and u == 0
                    if g == 1:
                        if h == 0 and not first:
                            pe.wait_ge(y_done, i + 0)
                    elif g == 2 or not first:
                        back, g_last = (0, 0) if g == 2 else (1, G - 1)
                        movers, moved = (on_act, moved_a) if g_last in on_act else (on_dve, moved_d)
                        pe.wait_ge(moved, (u - back) * len(movers) + (movers.index(g_last) + 1))
                    for b in range(count):
                        src = e[:, h % 2, maps - 1, (at + b) * P:(at + b + 1) * P]
                        mm = pe.transpose(turn_bank(g, count)[:, b * P:(b + 1) * P], src, m.ident)
                    mm.then_inc(turned, 1)

                def value(i, h):
                    u = i * HEADS + h
                    if on_act:
                        pe.wait_ge(moved_a, (u + 1) * len(on_act))
                    if on_dve:
                        pe.wait_ge(moved_d, (u + 1) * len(on_dve))
                    if h == 0 and not (isinstance(i, int) and i == 0):
                        pe.wait_ge(y_done, i + 0)
                    for b in range(key_tiles):
                        mm = pe.matmul(m.ps[:, 7, h * HD:(h + 1) * HD], pt[:, h % 2, b],
                                       v[:, b, h * HD:(h + 1) * HD], start=b == 0, stop=b == key_tiles - 1)
                    mm.then_inc(valued, 1)

                def body(i, prior):
                    for h in range(HEADS):
                        before = (i, h - LAG) if h >= LAG else (i - 1, h - LAG + HEADS)
                        has_before = prior or h >= LAG
                        pe.wait_ge(staged, (i * HEADS + (h + 1)) * copies)
                        g = 0
                        for a in range(maps):
                            if prior or h >= SL:
                                pe.wait_ge(exp_done, (i * HEADS + (h - SL)) * maps + (a + 1))
                            for at, width in pieces:
                                mm = pe.matmul(m.ps[:, bank(h, a) + at // 512, 0:width], qs(h, a),
                                               k_all(h, a)[:, at:at + width], start=True, stop=True)
                                if at + width == keys:
                                    mm.then_inc(scored, 1)
                                if has_before and g < G and (maps == 1 or at + width == keys):
                                    turn(*before, g)
                                    g += 1
                        while has_before and g < G:
                            turn(*before, g)
                            g += 1
                        if has_before:
                            value(*before)

                def tail(i):
                    for h in range(HEADS - LAG, HEADS):
                        for g in range(G):
                            turn(i - 1, h, g)
                        value(i - 1, h)
                loop(pe, body, tail)

            @block.vector
            def _(dve):
                def move(i, h, gs):
                    u = i * HEADS + h
                    for g in gs:
                        at, count = groups[g]
                        dve.wait_ge(turned, u * G + (g + 1))
                        if g == 0 and not (isinstance(i, int) and i * HEADS + h < 2):
                            dve.wait_ge(valued, u - 1)
                        dve.tensor_copy(pt[:, h % 2, at:at + count],
                                        turn_bank(g, count).rearrange("p (b c) -> p b c", b=count)
                                        ).then_inc(moved_d, 1)

                def invert(h):
                    dve.reciprocal(inv[:, h], total[:, h]).then_inc(inverse, 1)

                def finish(i):
                    dve.wait_ge(valued, (i + 1) * HEADS)
                    o = m.ps[:, 7, 0:BR].rearrange("p (h c) -> p h c", h=HEADS)
                    out = y[:, ds(i + t0, 1), :].rearrange("p a (h c) -> p (a h) c", h=HEADS)
                    dve.wait_ge(kept, i + 1)
                    dve.tensor_tensor(out, o, own[:].rearrange("p (h a) -> p h a", a=1).to_broadcast([P, HEADS, HD]), ALU.mult
                                      ).then_inc(y_done, 1)

                def keep(i):
                    dve.wait_ge(inverse, (i + 1) * HEADS)
                    if not (isinstance(i, int) and i == 0):
                        dve.wait_ge(y_done, i + 0)
                    dve.tensor_copy(own[:], inv[:, :, 0]).then_inc(kept, 1)

                def mix(i, h):
                    u = i * HEADS + h
                    dve.wait_ge(exp_done, (u + 1) * maps)
                    dve.reciprocal(inv[:, h], total[:, h]).then_inc(mixing, 1)
                    dve.wait_ge(mixing, u + 1)
                    dve.scalar_tensor_tensor(out=mx[:, h, 1:2], in0=inv[:, h, 1:2], scalar=total[:, h, 0:1], in1=neg_lam,
                                             op0=ALU.mult, op1=ALU.mult).then_inc(inverse, 1)
                    dve.wait_ge(inverse, u + 1)
                    dve.scalar_tensor_tensor(out=e[:, h % 2, 1], in0=e[:, h % 2, 1], scalar=mx[:, h, 1:2],
                                             in1=e[:, h % 2, 0], op0=ALU.mult, op1=ALU.add).then_inc(mixed, 1)

                def body(i, prior):
                    step = Tally(dve_step, 0, i, HEADS * maps)
                    for h in range(HEADS):
                        before = (i, h - LAG) if h >= LAG else (i - 1, h - LAG + HEADS)
                        has_before = prior or h >= LAG
                        if has_before:
                            move(*before, on_dve)
                            if maps == 1:
                                invert(before[1])
                        if maps == 1 and prior and h == LAG - 1:
                            keep(i - 1)
                            finish(i - 1)
                        for a in range(maps):
                            dve.wait_ge(scored, i * (HEADS * maps) + (h * maps + a + 1))
                            s = m.ps[:, bank(h, a):bank(h, a) + 3, :].rearrange("p b c -> p (b c)")[:, 0:keys]
                            step.then(dve, dve.reduce_max(mx[:, h, a:a + 1], s, AX.X))
                            dve.tensor_scalar(nmx[:, h, a:a + 1], mx[:, h, a:a + 1], -scale, None,
                                              ALU.mult).then_inc(maximum, 1)
                            if a == 0 and maps == 2 and (prior or h > 0):
                                mix(*((i, h - 1) if h else (i - 1, HEADS - 1)))
                                if h == 0:
                                    keep(i - 1)
                        if maps == 2 and prior and h == LAG - 1:
                            finish(i - 1)

                def tail(i):
                    if maps == 2:
                        mix(i - 1, HEADS - 1)
                        keep(i - 1)
                    for h in range(HEADS - LAG, HEADS):
                        move(i - 1, h, on_dve)
                        if maps == 1:
                            invert(h)
                    if maps == 1:
                        keep(i - 1)
                    finish(i - 1)
                loop(dve, body, tail)

            @block.scalar
            def _(act):
                def move(i, h, gs):
                    u = i * HEADS + h
                    for g in gs:
                        at, count = groups[g]
                        act.wait_ge(turned, u * G + (g + 1))
                        if g == 0 and not (isinstance(i, int) and i * HEADS + h < 2):
                            act.wait_ge(valued, u - 1)
                        act.activation(pt[:, h % 2, at:at + count],
                                       turn_bank(g, count).rearrange("p (b c) -> p b c", b=count),
                                       ACT.Copy).then_inc(moved_a, 1)

                def body(i, prior):
                    for h in range(HEADS):
                        before = (i, h - LAG) if h >= LAG else (i - 1, h - LAG + HEADS)
                        has_before = prior or h >= LAG
                        if has_before:
                            move(*before, on_act if maps == 1 else on_act[:1])
                        for a in range(maps):
                            if has_before and a == 1:
                                move(*before, on_act[1:])
                            act.wait_ge(maximum, i * (HEADS * maps) + (h * maps + a + 1))
                            if prior or h >= 2:
                                if a == maps - 1:
                                    act.wait_ge(turned, (i * HEADS + (h - 1)) * G)
                                else:
                                    act.wait_ge(mixed, i * HEADS + (h - 1))
                            if prior:
                                act.wait_ge(inverse, i * HEADS + (h - HEADS + 1))
                            s = m.ps[:, bank(h, a):bank(h, a) + 3, :].rearrange("p b c -> p (b c)")[:, 0:keys]
                            act.activation(e[:, h % 2, a], s, ACT.Exp, bias=nmx[:, h, a:a + 1], scale=scale,
                                           accum_out=total[:, h, a:a + 1]).then_inc(exp_done, 1)
                loop(act, body, lambda i: [move(i - 1, h, on_act) for h in range(HEADS - LAG, HEADS)])


def latent_attention(nc, m, l):
    tiles = range(0 if l < DEPTH - 1 else CT, NT)
    with ExitStack() as st:
        sb = lambda n, s, d=F32: st.enter_context(nc.sbuf_tensor(f"{n}_la{l}", s, d))
        y = sb("y", [P, NT, BR])
        v = sb("v", [P, NT, BR])
        q = sb("q", [QK, HEADS, ROWS])
        k = sb("k", [QK, HEADS, ROWS])
        with ExitStack() as st2:
            raw = st2.enter_context(nc.sbuf_tensor(f"raw_la{l}", [P, 4, ROWS], F32))
            project(nc, m, l, T_MLA, 4, raw, CHUNKS, "pa")
            normalise_columns(nc, m, l, "na", raw, [[0, 1], [2]], m.ones, None, lambda g: P * len(g),
                              lambda j: m.vec[:, V_QN + j:V_QN + j + 1])
            qr = y[:, 0:5].rearrange("p t c -> p (t c)")
            expand_latents(nc, m, l, raw, q, k, v, qr)
            rotate_columns(nc, m, l, "ra", [qr, raw[0:ROPE, 3]])
            place_rotated(nc, m, l, raw, q, k, qr)
        qs = sb("qs", [QK, HEADS, P])
        for key_tiles, t0, t1 in ((CT, 0, CT), (NT, CT, NT))[l == DEPTH - 1:]:
            attention(nc, m, l, "a", lambda h, t: [(qs[:, h], q[:, h, ds(t * P, P)])], lambda h, a: k[:, h],
                      v, y, lambda h, a: qs[:, h], key_tiles, t0, t1, QK ** -0.5, 1, None)
        store_rows(nc, m, l, 0, y, tiles)


def store_rows(nc, m, l, branch, y, tiles):
    with nc.sbuf_tensor(f"y_t{branch}_{l}", [P, 2, ROWS], F32) as y_t, phase(
            nc, "y_ready", "turned", "copied", "stored") as (block, y_ready, turned, copied, stored):
        turn, copy_turned, store = turn_out(nc, m, l, branch, lambda t: y[:, t], y_t, tiles,
                                            y_ready, turned, copied, stored)

        @block.sync
        def _(sp):
            store(sp)

        @block.tensor
        def _(pe):
            turn(pe)

        @block.vector
        def _(dve):
            dve.sem_inc(y_ready, len(tiles))
            for n, t in enumerate(tiles):
                copy_turned(dve, n, t)


def stack_keys(nc, m, l, qk, rep, kk, qh, ql, vecs, lam, prod, lam_init):
    pieces = [(j, at, min(512, ROWS - at)) for j in range(MAPS) for at in range(0, ROWS, 512)]
    kl = ql
    with nc.sbuf_tensor(f"kh_{l}", [P, 2, ROWS], F32R) as kh, nc.sbuf_tensor(f"rep_{l}", [P, MAPS, P], F32) as rep_raw:
        with phase(nc, "vecs_in", "rep_in", "dve_step", "lam_exp", "rep_cut", "k_high", "k_low", "q_high", "stacked",
                   "moved_a", "moved_d") as (block, vecs_in, rep_in, dve_step, lam_exp, rep_cut, k_high, k_low,
                                             q_high, stacked, moved_a, moved_d):
            @block.sync
            def _(sp):
                sp.dma_start(rep_raw[:], m.d_const[:, C_REP:C_REP + MAPS]).then_inc(rep_in, 16)
                sp.dma_start(vecs[:, 0:HD], m.d_bvec[l:l + 1, B_DFN:B_DFN + HD].to_broadcast([P, HD])
                             ).then_inc(vecs_in, 16)
                sp.dma_start(vecs[:, HD:], m.d_bvec[l:l + 1, B_LAM:B_LAM + 4 * ROPE].to_broadcast([P, 4 * ROPE])
                             ).then_inc(vecs_in, 16)

            def move(eng, e, moved, copy):
                for n, (j, at, width) in enumerate(pieces):
                    if n % 2 == e:
                        eng.wait_ge(stacked, n + 1)
                        copy(kk[:, j, at:at + width], m.ps[:, n % 8, 0:width]).then_inc(moved, 1)

            @block.tensor
            def _(pe):
                pe.wait_ge(rep_cut, 1)
                for n, (j, at, width) in enumerate(pieces):
                    if at == 0 and j % 4 == 0:
                        pe.wait_ge(k_low, j // 4 + 1)
                    if n >= 8:
                        pe.wait_ge((moved_a, moved_d)[n % 2], (n - 8) // 2 + 1)
                    pe.matmul(m.ps[:, n % 8, 0:width], rep[:, j % 4], kh[:, j // 4, at:at + width],
                              start=True, stop=False)
                    pe.matmul(m.ps[:, n % 8, 0:width], rep[:, 4 + j % 4], kl[:, j // 4, at:at + width],
                              start=False, stop=True
                              ).then_inc(stacked, 1)

            @block.scalar
            def _(act):
                for j in range(2):
                    act.activation(kh[:, j], qk[:, 2 + j], ACT.Copy).then_inc(k_high, 1)
                    if j == 0:
                        act.wait_ge(rep_in, 16)
                        act.activation(rep[:], rep_raw[:], ACT.Copy).then_inc(rep_cut, 1)
                move(act, 0, moved_a, lambda o, i: act.activation(o, i, ACT.Copy))
                for j in range(2):
                    act.activation(qh[:, j], qk[:, j], ACT.Copy).then_inc(q_high, 1)
                act.wait_ge(dve_step, 2)
                act.activation(lam[:], lam[:], ACT.Exp).then_inc(lam_exp, 1)

            @block.vector
            def _(dve):
                for j in range(2):
                    dve.wait_ge(k_high, j + 1)
                    dve.tensor_tensor(kl[:, j], qk[:, 2 + j], kh[:, j].bitcast(F32), ALU.subtract
                                      ).then_inc(k_low, 1)
                move(dve, 1, moved_d, lambda o, i: dve.tensor_copy(o, i))
                step = Tally(dve_step)
                dve.wait_ge(vecs_in, 32)
                pairs = vecs[:, HD:].rearrange("p (a b c) -> p a b c", a=2, b=2)
                step.then(dve, dve.tensor_tensor(prod[:], pairs[:, :, 0], pairs[:, :, 1], ALU.mult))
                step.then(dve, dve.reduce_sum(lam[:], prod[:], AX.X))
                for j in range(2):
                    dve.wait_ge(q_high, j + 1)
                    dve.wait_ge(stacked, len(pieces))
                    dve.tensor_tensor(ql[:, j], qk[:, j], qh[:, j].bitcast(F32), ALU.subtract)
                dve.wait_ge(lam_exp, 1)
                step.then(dve, dve.tensor_scalar(lam[:, 1:2], lam[:, 1:2], lam[:, 0:1], -lam_init,
                                                 ALU.subtract, ALU.add))
                dve.tensor_scalar(vecs[:, 0:HD], vecs[:, 0:HD], 1.0 - lam_init, None, ALU.mult)


def differential_attention(nc, m, l):
    import math
    lam_init = 0.8 - 0.6 * math.exp(-0.3 * l)
    tiles = range(0 if l < DEPTH - 1 else CT, NT)
    n_t = len(tiles)
    with ExitStack() as st:
        sb = lambda n, s, d=F32: st.enter_context(nc.sbuf_tensor(f"{n}_da{l}", s, d))
        y = sb("y", [P, NT, BR])
        qk = sb("qk", [P, 4, ROWS])
        vecs = sb("vecs", [P, HD + 4 * ROPE])
        lam = sb("lam", [P, 2])
        prod = sb("prod", [P, 2, ROPE])
        project(nc, m, l, T_DIFF, 4, qk, CHUNKS, "pd")
        rotate_columns(nc, m, l, "rd", [qk[:, j] for j in range(4)])
        qs = sb("qs", [P, MAPS, P], F32R)
        kk = sb("kk", [P, MAPS, ROWS], F32R)
        qh = sb("qh", [P, 2, ROWS], F32R)
        ql = sb("ql", [P, 2, ROWS], F32R)
        stack_keys(nc, m, l, qk, qs, kk, qh, ql, vecs, lam, prod, lam_init)

        def q_part(h, t):
            out = []
            for j in (2 * h, 2 * h + 1):
                rows = slice(32 * (j % 4), 32 * (j % 4) + 32)
                out += [(qs[32 * a:32 * a + 32, j], (qh, ql)[a // 2][rows, j // 4, ds(t * P, P)]) for a in range(4)]
            return out
        e = qk[:].rearrange("p (s a) c -> p s a c", s=2)
        for key_tiles, t0, t1 in ((CT, 0, CT), (NT, CT, NT))[l == DEPTH - 1:]:
            attention(nc, m, l, "d", q_part, lambda h, a: kk[:, 2 * h + a], m.dv, y,
                      lambda h, a: qs[:, 2 * h + a], key_tiles, t0, t1, ROPE ** -0.5, 2, lam[:, 1:2],
                      e[:, :, :, 0:key_tiles * P])
        normalise_heads(nc, m, l, "nd", y, tiles, vecs[:, 0:HD])
        store_rows(nc, m, l, 2, y, tiles)


def normalise_heads(nc, m, l, name, y, tiles, gain):
    with ExitStack() as st:
        sb = lambda n, s, d=F32: st.enter_context(nc.sbuf_tensor(f"{n}_{name}{l}", s, d))
        sq = sb("sq", [P, NT, BR])
        ssq = sb("ssq", [P, NT * HEADS])
        std = sb("std", [P, NT * HEADS])
        inv = sb("inv", [P, NT * HEADS])
        a, b = tiles[0], NT
        n = (b - a) * HEADS
        heads = lambda x: x[:, a:b].rearrange("p t (h c) -> p (t h) c", h=HEADS)
        with phase(nc, "dve_step", "rooted") as (block, dve_step, rooted):
            @block.vector
            def _(dve):
                step = Tally(dve_step)
                step.then(dve, dve.tensor_tensor(sq[:, a:b], y[:, a:b], y[:, a:b], ALU.mult))
                step.then(dve, dve.reduce_sum(ssq[:, 0:n], heads(sq), AX.X))
                dve.wait_ge(rooted, 1)
                step.then(dve, dve.reciprocal(inv[:, 0:n], std[:, 0:n]))
                by = inv[:, 0:n].rearrange("p (n a) -> p n a", a=1).to_broadcast([P, n, HD])
                step.then(dve, dve.tensor_tensor(heads(y), heads(y), by, ALU.mult))
                dve.tensor_tensor(heads(y), heads(y), gain.rearrange("p (a c) -> p a c", a=1).to_broadcast([P, n, HD]),
                                  ALU.mult)

            @block.scalar
            def _(act):
                act.wait_ge(dve_step, 2)
                act.activation(std[:, 0:n], ssq[:, 0:n], ACT.Sqrt, bias=m.eps[:, 0:1], scale=1.0 / HD).then_inc(rooted, 1)


def convolve(nc, m, l, qkv):
    with nc.sbuf_tensor(f"acc_cv{l}", [P, 2, ROWS], F32) as acc, phase(nc, "convolved", "dve_step", "silu") as (
            block, convolved, dve_step, silu):
        @block.vector
        def _(dve):
            step = Tally(dve_step)
            for j in range(6):
                a = acc[:, j % 2]
                tap = [m.vec[:, V_CONV + 6 * i + j:V_CONV + 6 * i + j + 1] for i in range(3)]
                if j >= 2:
                    dve.wait_ge(silu, j - 1)
                step.then(dve, dve.tensor_scalar(a, qkv[:, j], tap[1], None, ALU.mult))
                for n, (lo, hi) in enumerate(((0, CTX), (CTX, ROWS))):
                    ins = dve.scalar_tensor_tensor(out=a[:, lo + 1:hi], in0=qkv[:, j, lo:hi - 1], scalar=tap[0],
                                                   in1=a[:, lo + 1:hi], op0=ALU.mult, op1=ALU.add)
                step.then(dve, ins)
                for n, (lo, hi) in enumerate(((0, CTX), (CTX, ROWS))):
                    ins = dve.scalar_tensor_tensor(out=a[:, lo:hi - 1], in0=qkv[:, j, lo + 1:hi], scalar=tap[2],
                                                   in1=a[:, lo:hi - 1], op0=ALU.mult, op1=ALU.add)
                ins.then_inc(convolved, 1)

        @block.scalar
        def _(act):
            for j in range(6):
                act.wait_ge(convolved, j + 1)
                act.activation(qkv[:, j], acc[:, j % 2], ACT.Silu).then_inc(silu, 1)


def turn_keys(nc, m, l, qkv, kv):
    with phase(nc, "turned", "moved_a", "moved_d") as (block, turned, moved_a, moved_d):
        @block.tensor
        def _(pe):
            for t in range(NT):
                if t >= 4:
                    pe.wait_ge(moved_d if t % 2 else moved_a, (t - 4) // 2 + 1)
                for j in range(4):
                    mm = pe.transpose(m.ps[:, t % 4, j * P:(j + 1) * P], qkv[:, 2 + j, t * P:(t + 1) * P], m.ident)
                mm.then_inc(turned, 1)

        @block.scalar
        def _(act):
            for t in range(0, NT, 2):
                act.wait_ge(turned, t + 1)
                act.activation(kv[:, t], m.ps[:, t % 4], ACT.Copy).then_inc(moved_a, 1)

        @block.vector
        def _(dve):
            for t in range(1, NT, 2):
                dve.wait_ge(turned, t + 1)
                dve.tensor_copy(kv[:, t], m.ps[:, t % 4]).then_inc(moved_d, 1)


def decay_gates(nc, m, l, g):
    TERMS = 9
    G_DONE = 2 + 5 + (TERMS - 1) + 4
    with ExitStack() as st:
        sb = lambda n, s, d=F32: st.enter_context(nc.sbuf_tensor(f"{n}_dg{l}", s, d))
        vecs = sb("vecs", [P, 16])
        tri = sb("tri", [P, 2, P])
        x = sb("x", [P, NT, MAPS])
        y = sb("y", [P, NT, MAPS])
        z = sb("z", [P, NT, MAPS])
        z2 = sb("z2", [P, NT, MAPS])
        r = sb("r", [P, NT, MAPS])
        gl = sb("gl", [P, NT, MAPS])
        last = sb("last", [P, NT, MAPS])
        bc = lambda v: v.rearrange("p (a c) -> p a c", a=1).to_broadcast([P, NT, MAPS])
        with phase(nc, "loaded", "dve_step", "act_step", "pe_step") as (block, loaded, dve_step, act_step, pe_step):
            @block.sync
            def _(sp):
                sp.dma_start(vecs[:], m.d_bvec[l:l + 1, B_ALOG:B_ALOG + 16].to_broadcast([P, 16])).then_inc(loaded, 16)
                sp.dma_start(tri[:], m.d_const[:, C_TRIF:C_TRIF + 2]).then_inc(loaded, 16)

            @block.vector
            def _(dve):
                step = Tally(dve_step)
                then = lambda ins: step.then(dve, ins)
                dve.wait_ge(loaded, 32)
                then(dve.tensor_tensor(x[:], m.ab[:, :, 0:8], bc(vecs[:, 8:16]), ALU.add))
                then(dve.scalar_tensor_tensor(out=y[:], in0=x[:], scalar=-1.0, in1=x[:], op0=ALU.mult, op1=ALU.min))
                dve.wait_ge(act_step, 1)
                then(dve.tensor_scalar(z[:], y[:], 2.0, None, ALU.add))
                then(dve.reciprocal(z[:], z[:]))
                then(dve.tensor_tensor(z[:], z[:], y[:], ALU.mult))
                then(dve.tensor_tensor(z2[:], z[:], z[:], ALU.mult))
                then(dve.tensor_scalar(r[:], z2[:], 1.0 / (2 * TERMS + 1), None, ALU.mult))
                for n in range(TERMS - 1, 0, -1):
                    then(dve.scalar_tensor_tensor(out=r[:], in0=r[:], scalar=1.0 / (2 * n + 1), in1=z2[:],
                                                  op0=ALU.add, op1=ALU.mult))
                then(dve.scalar_tensor_tensor(out=r[:], in0=r[:], scalar=1.0, in1=z[:], op0=ALU.add, op1=ALU.mult))
                then(dve.tensor_scalar(x[:], x[:], 0.0, None, ALU.max))
                then(dve.scalar_tensor_tensor(out=r[:], in0=r[:], scalar=2.0, in1=x[:], op0=ALU.mult, op1=ALU.add))
                then(dve.scalar_tensor_tensor(out=gl[:], in0=r[:], scalar=-1.0, in1=bc(vecs[:, 0:8]),
                                              op0=ALU.mult, op1=ALU.mult))
                dve.wait_ge(pe_step, 1)
                for d in range(2):
                    dve.tensor_copy(g.gam[:, :, 4 * d:4 * d + 4],
                                    m.ps[:, d, 0:NT * 4].rearrange("p (t h) -> p t h", h=4))
                then(dve.tensor_copy(last[:], m.ps[:, 2, 0:NT * 8].rearrange("p (t h) -> p t h", h=8)))
                then(dve.tensor_tensor(g.kd[:], last[:], g.gam[:], ALU.subtract))
                dve.wait_ge(act_step, 4)
                dve.tensor_tensor(g.be[:], g.beta[:], g.eg[:], ALU.mult)
                for par in range(2):
                    rows = slice(64 * par, 64 * par + 64)
                    for d in range(2):
                        dve.tensor_copy(g.last[rows, :, d], last[rows, :, 4 * d + par:4 * d + 4:2])

            @block.scalar
            def _(act):
                act.wait_ge(dve_step, 2)
                act.activation(vecs[:, 0:8], vecs[:, 0:8], ACT.Exp)
                act.activation(y[:], y[:], ACT.Exp).then_inc(act_step, 1)
                act.wait_ge(dve_step, G_DONE + 2)
                act.activation(last[:], last[:], ACT.Exp).then_inc(act_step, 1)
                act.activation(g.kd[:], g.kd[:], ACT.Exp)
                act.activation(g.eg[:], g.gam[:], ACT.Exp).then_inc(act_step, 1)
                act.activation(g.beta[:], m.ab[:, :, 8:16], ACT.Sigmoid).then_inc(act_step, 1)

            @block.tensor
            def _(pe):
                pe.wait_ge(dve_step, G_DONE)
                for d in range(2):
                    pe.matmul(m.ps[:, d, 0:NT * 4], tri[:, d], gl[:, :, 4 * d:4 * d + 4], start=True, stop=True)
                pe.matmul(m.ps[:, 2, 0:NT * 8], m.ones, gl[:], start=True, stop=True).then_inc(pe_step, 1)


def delta_rule(nc, m, l, qkv, kv, o, g):
    with ExitStack() as st:
        sb = lambda n, s, d=F32: st.enter_context(nc.sbuf_tensor(f"{n}_dr{l}", s, d))
        lv = sb("lv", [P, 2, LEVELS, P])
        inc = sb("inc", [P, 2, P])
        quad = lambda n: [sb(f"{n}{d}", [P, HEADS, P]) for d in range(2)]
        staged_t, joins, E, A, AT, T, TT, V, PT = (quad(n) for n in (
            "st", "joins", "E", "A", "AT", "T", "TT", "V", "PT"))
        EG = V
        half = lambda n: [sb(f"{n}{d}", [P, HEADS, HD]) for d in range(2)]
        xk, xv, kdec, vn = (half(n) for n in ("xk", "xv", "kdec", "vn"))
        qd = [sb(f"qd{d}", [P, 2, P]) for d in range(2)]
        wt = [sb(f"wt{d}", [P, 2, P]) for d in range(2)]
        kz = [sb(f"kz{d}", [P, HEADS, P]) for d in range(2)]
        S = [sb(f"S{d}", [P, 2, 2, HD]) for d in range(2)]
        names = ("staged", "kz_ready", "diag", "grams", "e_in", "e_exp", "eg_done", "a_ready", "pt_ready", "at_turned", "at_ready",
                 "t_ready", "join_ready", "v_made", "v_ready", "x_made", "t_new", "rows_ready", "w_made", "w_ready",
                 "qd_ready", "vn_made", "vn_ready", "o_made", "o_added", "s_made", "s_new", "dve_step")
        all_names = [f"{n}{'fb'[d]}" for n in names for d in range(2)]
        SEGMENTS = ((0, CT, 0, l < DEPTH - 1), (CT, NT - CT, CT, True))
        with phase(nc, "loaded", "cleared", *all_names) as (block, loaded, cleared, *rest):
            sem = {n: rest[2 * a:2 * a + 2] for a, n in enumerate(names)}
            bank = lambda d, b: m.ps[:, 4 * d + b]
            wide = lambda x: x.rearrange("p (h c) -> p h c", h=HEADS)
            own = lambda h: slice(64 * (h % 2), 64 * (h % 2) + 64)
            LV = LEVELS - 1

            def steps(eng, body):
                for t0, n, s0, wants in SEGMENTS:
                    with eng.Fori(0, n) as i:
                        body(i + s0, [eng.snap(i + t0), eng.snap(i * -1 + (t0 + n - 1))], wants)

            def per_head(x, tile, d, width):
                v = x[:, ds(tile, 1), 4 * d:4 * d + 4].rearrange("p t h -> p h t")
                return v.to_broadcast([P, HEADS, width])

            @block.sync
            def _(sp):
                sp.dma_start(lv[:], m.d_const[:, C_LVF:C_LVF + 2 * LEVELS].rearrange(
                    "p (d v) c -> p d v c", d=2)).then_inc(loaded, 16)
                sp.dma_start(inc[:], m.d_const[:, C_TRIF:C_TRIF + 2]).then_inc(loaded, 16)

            @block.gpsimd
            def _(pool):
                pool.wait_ge(loaded, 32)

                def body(s, tiles, wants):
                    for d in range(2):
                        pool.wait_ge(sem["s_made"][d], s + 1)
                        t = tiles[d]
                        pool.tensor_copy(staged_t[d][:], qkv[:, 0:4, ds(t * P, P)]).then_inc(sem["staged"][d], 1)
                        pool.tensor_tensor(joins[d][:], m.ident.rearrange("p (a c) -> p a c", a=1).to_broadcast(
                            [P, HEADS, P]), per_head(g.gam, t, d, P), ALU.mult).then_inc(sem["diag"][d], 1)
                    for d in range(2):
                        t = tiles[d]
                        k = wide(kv[:, ds(t, 1), 0:BR].rearrange("p a c -> p (a c)"))
                        v = wide(kv[:, ds(t, 1), BR:2 * BR].rearrange("p a c -> p (a c)"))
                        pool.tensor_tensor(xk[d][:], k, per_head(g.be, t, d, HD), ALU.mult)
                        pool.tensor_tensor(xv[d][:], v, per_head(g.beta, t, d, HD), ALU.mult)
                        pool.tensor_tensor(kdec[d][:], k, per_head(g.kd, t, d, HD), ALU.mult
                                           ).then_inc(sem["rows_ready"][d], 1)
                    for b in range(LV):
                        for d in range(2):
                            if b == 0:
                                pool.wait_ge(sem["at_ready"][d], s + 1)
                            else:
                                pool.wait_ge(sem["v_made"][d], s * LV + b)
                            pool.tensor_tensor(joins[d][:], AT[d][:], lv[:, 1 - d, b + 1:b + 2].to_broadcast(
                                [P, HEADS, P]), ALU.mult).then_inc(sem["join_ready"][d], 1)
                steps(pool, body)

            @block.tensor
            def _(pe):
                for d in range(2):
                    pe.sem_inc(sem["s_made"][d], 1)
                    pe.sem_inc(sem["grams"][d], 1)
                pe.wait_ge(cleared, 5)

                def body(s, tiles, wants):
                    for d in range(2):
                        pe.wait_ge(sem["staged"][d], s + 1)
                        pe.wait_ge(sem["kz_ready"][d], s + 1)
                        pe.wait_ge(sem["diag"][d], s + 1)
                        pe.wait_ge(sem["s_new"][d], s + 1)
                        pe.wait_ge(sem["o_added"][d], s + 1)
                        for h in range(HEADS):
                            k = kz[d][:, h]
                            pe.matmul(bank(d, 0)[:, h * P:(h + 1) * P], k, staged_t[d][:, 2 + h // 2],
                                      start=True, stop=True)
                            pe.matmul(bank(d, 1)[:, h * P:(h + 1) * P], k, staged_t[d][:, h // 2],
                                      start=True, stop=True)
                        pe.matmul(bank(d, 2), m.ones, joins[d][:], start=True, stop=True).then_inc(sem["grams"][d], 1)
                    for d in range(2):
                        pe.wait_ge(sem["a_ready"][d], s + 1)
                        for h in range(HEADS):
                            mm = pe.transpose(bank(d, 3)[:, h * P:(h + 1) * P], A[d][:, h], m.ident)
                        mm.then_inc(sem["at_turned"][d], 1)
                    for b in range(LV):
                        for d in range(2):
                            if b == 0:
                                pe.wait_ge(sem["t_ready"][d], s + 1)
                            else:
                                pe.wait_ge(sem["t_new"][d], s * LV + b)
                            pe.wait_ge(sem["join_ready"][d], s * LV + (b + 1))
                            for h in range(HEADS):
                                mm = pe.matmul(bank(d, 3)[:, h * P:(h + 1) * P], joins[d][:, h], T[d][:, h],
                                               start=True, stop=True)
                            mm.then_inc(sem["v_made"][d], 1)
                        for d in range(2):
                            pe.wait_ge(sem["v_ready"][d], s * LV + (b + 1))
                            for h in range(HEADS):
                                cols = slice(h * P, (h + 1) * P)
                                if b < LV - 1:
                                    pe.matmul(bank(d, 0)[:, cols], TT[d][:, h], V[d][:, h], start=True, stop=True)
                                mm = pe.matmul(bank(d, 1)[:, cols], V[d][:, h], TT[d][:, h], start=True, stop=True)
                            mm.then_inc(sem["x_made"][d], 1)
                    for d in range(2):
                        pe.wait_ge(sem["t_new"][d], s * LV + LV)
                        pe.wait_ge(sem["rows_ready"][d], s + 1)
                        for h in range(HEADS):
                            mm = pe.matmul(bank(d, 2)[own(h), (h // 2) * P:(h // 2 + 1) * P], xk[d][:, h], TT[d][:, h],
                                           start=True, stop=True)
                        mm.then_inc(sem["w_made"][d], 1)
                    for d in range(2):
                        pe.wait_ge(sem["w_ready"][d], s + 1)
                        for hp in range(2):
                            cols = slice(hp * P, (hp + 1) * P)
                            pe.matmul(bank(d, 3)[:, cols], wt[d][:, hp], S[d][:, hp], start=True, stop=True,
                                      skip_group_check=True)
                            for h in (2 * hp, 2 * hp + 1):
                                cols = slice(h * HD, (h + 1) * HD)
                                mm = pe.matmul(bank(d, 3)[:, cols], TT[d][:, h], xv[d][:, h], start=False,
                                               stop=True, skip_group_check=True)
                        mm.then_inc(sem["vn_made"][d], 1)
                    for d in range(2):
                        pe.wait_ge(sem["vn_ready"][d], s + 1)
                        pe.wait_ge(sem["qd_ready"][d], s + 1)
                        pe.wait_ge(sem["pt_ready"][d], s + 1)
                        if wants:
                            for hp in range(2):
                                cols = slice(hp * P, (hp + 1) * P)
                                pe.matmul(bank(d, 0)[:, cols], qd[d][:, hp], S[d][:, hp], start=True, stop=True,
                                      skip_group_check=True)
                                for h in (2 * hp, 2 * hp + 1):
                                    cols = slice(h * HD, (h + 1) * HD)
                                    mm = pe.matmul(bank(d, 0)[:, cols], PT[d][:, h], vn[d][:, h], start=False,
                                                   stop=True, skip_group_check=True)
                            mm.then_inc(sem["o_made"][d], 1)
                        else:
                            pe.sem_inc(sem["o_made"][d], 1)
                        for h in range(HEADS):
                            mm = pe.matmul(bank(d, 1)[own(h), (h // 2) * HD:(h // 2 + 1) * HD], kdec[d][:, h],
                                           vn[d][:, h], start=True, stop=True)
                        mm.then_inc(sem["s_made"][d], 1)
                steps(pe, body)

            @block.scalar
            def _(act):
                act.wait_ge(cleared, 5)

                def body(s, tiles, wants):
                    for d in range(2):
                        act.wait_ge(sem["grams"][d], s + 1)
                        for par in range(2):
                            rows = slice(64 * par, 64 * par + 64)
                            ins = act.activation(kz[d][rows, par:HEADS:2], qkv[rows, 2:4, ds(tiles[d] * P, P)], ACT.Copy)
                        ins.then_inc(sem["kz_ready"][d], 1)
                    for d in range(2):
                        act.wait_ge(sem["e_in"][d], s + 1)
                        act.activation(E[d][:], E[d][:], ACT.Exp).then_inc(sem["e_exp"][d], 1)
                        act.activation(EG[d][:], wide(bank(d, 2)), ACT.Exp).then_inc(sem["eg_done"][d], 1)
                    for d in range(2):
                        act.wait_ge(sem["at_turned"][d], s + 1)
                        act.activation(AT[d][:], wide(bank(d, 3)), ACT.Copy).then_inc(sem["at_ready"][d], 1)
                    for b in range(LV):
                        for d in range(2):
                            act.wait_ge(sem["v_made"][d], s * LV + (b + 1))
                            if b == 0:
                                act.wait_ge(sem["qd_ready"][d], s + 1)
                            act.activation(V[d][:], wide(bank(d, 3)), ACT.Copy).then_inc(sem["v_ready"][d], 1)
                    for d in range(2):
                        act.wait_ge(sem["w_made"][d], s + 1)
                        act.activation(wt[d][:], bank(d, 2)[:, 0:2 * P].rearrange("p (h c) -> p h c", h=2), ACT.Copy,
                                       scale=-1.0).then_inc(sem["w_ready"][d], 1)
                    for d in range(2):
                        act.wait_ge(sem["vn_made"][d], s + 1)
                        act.activation(vn[d][:], wide(bank(d, 3)[:, 0:BR]), ACT.Copy).then_inc(sem["vn_ready"][d], 1)
                steps(act, body)

            @block.vector
            def _(dve):
                for x in (S[0][:], S[1][:], kz[0][:], kz[1][:], o):
                    dve.memset(x, 0.0).then_inc(cleared, 1)
                for d in range(2):
                    dve.sem_inc(sem["s_new"][d], 1)
                    dve.sem_inc(sem["o_added"][d], 1)
                dve.wait_ge(loaded, 32)
                dve.wait_ge(cleared, 5)
                PER = 6
                ident4 = m.ident.rearrange("p (a c) -> p a c", a=1).to_broadcast([P, HEADS, P])

                def body(s, tiles, wants):
                    step = [Tally(sem["dve_step"][d], 0, s, PER) for d in range(2)]
                    for d in range(2):
                        dve.wait_ge(sem["grams"][d], s + 2)
                        ins = dve.tensor_tensor(E[d][:], wide(bank(d, 2)), per_head(g.gam, tiles[d], d, P), ALU.subtract)
                        step[d].did(ins)
                    for d in range(2):
                        step[d].wait(dve)
                        dve.scalar_tensor_tensor(out=E[d][:], in0=E[d][:], scalar=-1.0, in1=E[d][:], op0=ALU.mult,
                                                 op1=ALU.min).then_inc(sem["e_in"][d], 1)
                    for d in range(2):
                        dve.wait_ge(sem["e_exp"][d], s + 1)
                        step[d].did(dve.tensor_tensor(A[d][:], wide(bank(d, 0)), E[d][:], ALU.mult))
                        step[d].did(dve.tensor_tensor(PT[d][:], wide(bank(d, 1)), E[d][:], ALU.mult))
                    for d in range(2):
                        step[d].wait(dve)
                        dve.tensor_tensor(A[d][:], A[d][:], per_head(g.beta, tiles[d], d, P), ALU.mult
                                          ).then_inc(sem["a_ready"][d], 1)
                        dve.tensor_tensor(PT[d][:], PT[d][:], inc[:, d:d + 1].to_broadcast([P, HEADS, P]), ALU.mult
                                          ).then_inc(sem["pt_ready"][d], 1)
                    for d in range(2):
                        dve.wait_ge(sem["a_ready"][d], s + 1)
                        step[d].did(dve.tensor_tensor(T[d][:], A[d][:], lv[:, d, 0:1].to_broadcast([P, HEADS, P]), ALU.mult))
                    for d in range(2):
                        dve.wait_ge(sem["at_ready"][d], s + 1)
                        step[d].did(dve.tensor_tensor(TT[d][:], AT[d][:], lv[:, 1 - d, 0:1].to_broadcast([P, HEADS, P]),
                                                      ALU.mult))
                    for d in range(2):
                        step[d].wait(dve)
                        for x in (T, TT):
                            ins = dve.scalar_tensor_tensor(out=x[d][:], in0=x[d][:], scalar=-1.0, in1=ident4,
                                                           op0=ALU.mult, op1=ALU.add)
                        ins.then_inc(sem["t_ready"][d], 1)
                    for d in range(2):
                        dve.wait_ge(sem["eg_done"][d], s + 1)
                        dve.wait_ge(sem["staged"][d], s + 1)
                        for par in range(2):
                            rows = slice(64 * par, 64 * par + 64)
                            ins = dve.tensor_tensor(qd[d][rows], staged_t[d][rows, 0:2], EG[d][rows, par:HEADS:2],
                                                    ALU.mult)
                        ins.then_inc(sem["qd_ready"][d], 1)
                    for b in range(LV):
                        for d in range(2):
                            if b == 0:
                                dve.wait_ge(sem["t_ready"][d], s + 1)
                            else:
                                dve.wait_ge(sem["t_new"][d], s * LV + b)
                            dve.wait_ge(sem["x_made"][d], s * LV + (b + 1))
                            if b < LV - 1:
                                dve.tensor_tensor(T[d][:], T[d][:], wide(bank(d, 0)), ALU.subtract)
                            dve.tensor_tensor(TT[d][:], TT[d][:], wide(bank(d, 1)), ALU.subtract
                                              ).then_inc(sem["t_new"][d], 1)
                    for d in range(2):
                        dve.wait_ge(sem["s_made"][d], s + 2)
                        for par in range(2):
                            rows = slice(64 * par, 64 * par + 64)
                            by = g.last[rows, ds(tiles[d], 1), d].rearrange("p a h -> p h a").to_broadcast([64, 2, HD])
                            ins = dve.tensor_tensor(S[d][rows, :, par], S[d][rows, :, par], by, ALU.mult)
                        step[d].then(dve, ins)
                        for par in range(2):
                            rows = slice(64 * par, 64 * par + 64)
                            ins = dve.tensor_tensor(S[d][rows, :, par], S[d][rows, :, par],
                                                    bank(d, 1)[rows, 0:2 * HD].rearrange("p (h c) -> p h c", h=2), ALU.add)
                        ins.then_inc(sem["s_new"][d], 1)
                        if wants:
                            dve.wait_ge(sem["o_made"][d], s + 1)
                            row = o[:, ds(tiles[d], 1)].rearrange("p a c -> p (a c)")
                            ins = dve.tensor_tensor(row, row, bank(d, 0)[:, 0:BR], ALU.add)
                            ins.then_inc(sem["o_added"][d], 1)
                            dve.wait_ge(sem["o_added"][d], s + 2)
                        else:
                            dve.sem_inc(sem["o_added"][d], 1)
                    for d in range(2):
                        step[d].close()
                steps(dve, body)


class Gates:
    pass


def delta_net(nc, m, l):
    tiles = range(0 if l < DEPTH - 1 else CT, NT)
    with ExitStack() as st:
        sb = lambda n, s, d=F32: st.enter_context(nc.sbuf_tensor(f"{n}_dn{l}", s, d))
        g = Gates()
        g.gam, g.eg, g.kd, g.beta, g.be = (sb(n, [P, NT, MAPS]) for n in ("gam", "eg", "kd", "beta", "be"))
        g.last = sb("glast", [P, NT, 2, 2])
        vecs = sb("vecs", [P, HD])
        qkv = sb("qkv", [P, 6, ROWS])
        kv = sb("kv", [P, NT, 2 * BR])
        o = qkv[:, 4:6].rearrange("p j c -> p (j c)").rearrange("p (t c) -> p t c", t=NT)
        project(nc, m, l, T_DN, 6, qkv, CHUNKS, "pn")
        convolve(nc, m, l, qkv)
        normalise_columns(nc, m, l, "nn", qkv, [[0], [1], [2], [3]], m.blocks, lambda j: HD ** -0.5 if j < 2 else 1.0,
                          lambda g: 1, None)
        turn_keys(nc, m, l, qkv, kv)
        decay_gates(nc, m, l, g)
        delta_rule(nc, m, l, qkv, kv, o, g)
        with phase(nc, "loaded") as (block, loaded):
            @block.sync
            def _(sp):
                sp.dma_start(vecs[:], m.d_bvec[l:l + 1, B_DNN:B_DNN + HD].to_broadcast([P, HD])).then_inc(loaded, 16)
                sp.wait_ge(loaded, 16)
        normalise_heads(nc, m, l, "nh", o, tiles, vecs[:])
        store_rows(nc, m, l, 3, o, tiles)


def merge(nc, m, l):
    chunks = list(enumerate(CHUNKS))[0 if l < DEPTH - 1 else 1:]
    n_c = len(chunks)
    lo = chunks[0][1][0]
    with ExitStack() as st:
        sb = lambda n, s, d=F32: st.enter_context(nc.sbuf_tensor(f"{n}_mg{l}", s, d))
        y = sb("y", [P, 2 * 4, ROWS])
        with nc.sbuf_tensor(f"gate_mg{l}", [P, 2, ROWS], F32) as gate:
            own_chunks = [c for _, c in chunks]
            with phase(nc, "y_in") as (block, y_in):
                @block.sync
                def _(sp):
                    sp.dma_start(y[:, :, lo:], m.d_y[:, :, lo:]).then_inc(y_in, 16)
                    sp.wait_ge(y_in, 16)
            for j in range(0, 8, 2):
                project(nc, m, l, T_GATE + j, 2, gate, own_chunks, f"pg{j}")
                with phase(nc, "silu") as (block, silu):
                    @block.scalar
                    def _(act):
                        act.activation(gate[:, :, lo:], gate[:, :, lo:], ACT.Silu).then_inc(silu, 1)

                    @block.vector
                    def _(dve):
                        dve.wait_ge(silu, 1)
                        dve.tensor_tensor(y[:, j:j + 2, lo:], y[:, j:j + 2, lo:], gate[:, :, lo:], ALU.mult)
        w = sb("w", [P, 2, KD + 2, P])
        wh = sb("wh", [P, 2, KD, P], F32R)
        wl = sb("wl", [P, 2, KD, P], F32R)
        sg = sb("sg", [P, 2, 512])
        term = sb("term", [P, 2, 512])
        acc = sb("acc", [P, ROWS])
        N = 4 * n_c
        with phase(nc, "w_in0", "w_in1", "w_high", "w_low", "gated", "branched", "sigm",
                   "multiplied", "added", "stored") as (
                block, w_in0, w_in1, w_high, w_low, gated, branched, sigm, multiplied, added, stored):
            w_in = [w_in0, w_in1]

            @block.sync
            def _(sp):
                sp.sem_inc(stored, 16)
                for s in range(2):
                    sp.dma_start(w[:, s], m.d_wmerge[l, s]).then_inc(w_in[s], 16)

                def body(f, loads):
                    for b in range(loads):
                        s = b % 2
                        sp.wait_ge(branched, f * N + (b + 3) * n_c)
                        sp.dma_start(w[:, s], m.d_wmerge[l, f * 4 + (b + 2)]).then_inc(w_in[s], 16)
                    sp.wait_ge(added, f * N + N)
                    sp.dma_start(m.d_acc[:, ds(f, 1), lo:], acc[:, lo:].rearrange("p (a c) -> p a c", a=1)
                                 ).then_inc(stored, 16)
                with sp.Fori(0, KD - 1) as f:
                    body(f, 4)
                body(KD - 1, 2)
                sp.wait_ge(stored, 16 * KD + 16)

            @block.scalar
            def _(act):
                def cut(f, b):
                    act.wait_ge(w_in[b % 2], f * 32 + 16 * (b // 2 + 1))
                    act.wait_ge(branched, f * N + (b + 1) * n_c)
                    act.activation(wh[:, b % 2], w[:, b % 2, 0:KD], ACT.Copy).then_inc(w_high, 1)

                def body(f, last):
                    for b in range(4):
                        for n, (c, (at, width)) in enumerate(chunks):
                            if n == 1 and not (last and b == 3):
                                cut(f + b // 3, (b + 1) % 4)
                            u = b * n_c + n
                            act.wait_ge(gated, f * N + (u + 1))
                            act.wait_ge(multiplied, f * N + (u + 3))
                            act.activation(sg[:, u % 2, 0:width], m.ps[:, u % 4, 0:width], ACT.Sigmoid
                                           ).then_inc(sigm, 1)
                cut(0, 0)
                with act.Fori(0, KD - 1) as f:
                    body(f, False)
                body(KD - 1, True)

            @block.tensor
            def _(pe):
                pe.sem_inc(branched, 2 * n_c)
                with pe.Fori(0, KD) as f:
                    for b in range(4):
                        s = b % 2
                        pe.wait_ge(w_low, f * 4 + (b + 1))
                        for n, (c, (at, width)) in enumerate(chunks):
                            u = b * n_c + n
                            pe.wait_ge(multiplied, f * N + (u + 1))
                            for k in range(KD):
                                mm = split_products(pe, m.ps[:, u % 4, 0:width], wh[:, s, k], wl[:, s, k],
                                                    m.hh[:, k, at:at + width], m.hl[:, k, at:at + width],
                                                    k == 0, k == KD - 1)
                            mm.then_inc(gated, 1)
                            for k in range(2):
                                mm = pe.matmul(m.ps[:, 4 + u % 4, 0:width], w[:, s, KD + k], y[:, 2 * b + k, at:at + width],
                                               start=k == 0, stop=k == 1)
                            mm.then_inc(branched, 1)

            @block.vector
            def _(dve):
                dve.sem_inc(multiplied, 4)

                def cut(f, b):
                    dve.wait_ge(w_high, f * 4 + (b + 1))
                    dve.tensor_tensor(wl[:, b % 2], w[:, b % 2, 0:KD], wh[:, b % 2].bitcast(F32), ALU.subtract
                                      ).then_inc(w_low, 1)

                def body(f, last):
                    for b in range(4):
                        for n, (c, (at, width)) in enumerate(chunks):
                            if n == 1 and not (last and b == 3):
                                cut(f + b // 3, (b + 1) % 4)
                            u = b * n_c + n
                            dve.wait_ge(sigm, f * N + (u + 1))
                            dve.wait_ge(branched, f * N + (u + 1 + 2 * n_c))
                            if b == 0:
                                if n == 0:
                                    dve.wait_ge(stored, f * 16 + 16)
                                dst = acc[:, at:at + width]
                            else:
                                dst = term[:, u % 2, 0:width]
                            dve.tensor_tensor(dst, sg[:, u % 2, 0:width], m.ps[:, 4 + u % 4, 0:width], ALU.mult
                                              ).then_inc(multiplied, 1)
                            dve.wait_ge(multiplied, f * N + (u + 5))
                            if b:
                                dve.tensor_tensor(acc[:, at:at + width], acc[:, at:at + width], dst, ALU.add
                                                  ).then_inc(added, 1)
                                dve.wait_ge(added, f * N + (u + 1))
                            else:
                                dve.sem_inc(added, 1)
                cut(0, 0)
                with dve.Fori(0, KD - 1) as f:
                    body(f, False)
                body(KD - 1, True)


def output(nc, m, l, out):
    tiles = range(0 if l < DEPTH - 1 else CT, NT)
    src = m.d_x if l == 0 else m.d_x1
    wo_h, wo_l = m.hh[:, :, 0:D], m.hl[:, :, 0:D]
    with ExitStack() as st:
        sb = lambda n, s, d=F32: st.enter_context(nc.sbuf_tensor(f"{n}_ou{l}", s, d))
        w = sb("w", [P, 2, D])
        x = sb("x", [P, 2, D])
        r = sb("r", [P, 2, D])
        acc = sb("acc", [P, 2, KD, P])
        ah = sb("ah", [P, 2, KD, P], F32R)
        al = sb("al", [P, 2, KD, P], F32R)
        gate = sb("gate", [P, 2, D])
        lng = sb("lng", [P, 2, D])
        stats = sb("stats", [P, NT, 2, 6])
        mv = sb("mv", [P, NT, 2])
        std = sb("std", [P, NT])
        rstd = sb("rstd", [P, NT])
        with phase(nc, "small_in", "w_in0", "w_in1", "w_high", "w_low", "a_in0", "a_in1", "a_high", "a_low", "made",
                   "x_in0", "x_in1", "var_done", "std_done", "dve_step", "row_done", "stored0", "stored1", "used") as (
                block, small_in, w_in0, w_in1, w_high, w_low, a_in0, a_in1, a_high, a_low, made,
                x_in0, x_in1, var_done, std_done, dve_step, row_done, stored0, stored1, used):
            w_in, a_in, x_in, stored = [w_in0, w_in1], [a_in0, a_in1], [x_in0, x_in1], [stored0, stored1]

            def rows_out(t):
                if l < DEPTH - 1:
                    return m.d_x1[t * P:(t + 1) * P, :]
                return out[(t - CT) * P:(t - CT + 1) * P, :]

            @block.sync
            def _(sp):
                sp.dma_start(gate[:], m.d_gate.rearrange("(c t) p -> c (t p)", c=2).rearrange(
                    "(a c) n -> a c n", a=1).to_broadcast([P, 2, D])).then_inc(small_in, 16)
                sp.dma_start(lng[:], m.d_bvec[l:l + 1, 0:2 * D].rearrange("a (c n) -> a c n", c=2
                                                                          ).to_broadcast([P, 2, D])).then_inc(small_in, 16)
                for k in range(KD):
                    if k >= 2:
                        sp.wait_ge(w_low, k - 1)
                    sp.dma_start(w[:, k % 2], m.d_wout[l, k]).then_inc(w_in[k % 2], 16)
                for n, t in enumerate(tiles):
                    s = n % 2
                    if n >= 2:
                        sp.wait_ge(a_low, n - 1)
                        sp.wait_ge(used, n - 1)
                    sp.dma_start(acc[:, s], m.d_acc[:, :, t * P:(t + 1) * P]).then_inc(a_in[s], 16)
                    sp.dma_start(x[:, s], src[t * P:(t + 1) * P, :]).then_inc(x_in[s], 16)
                    if n >= 1:
                        sp.wait_ge(row_done, n)
                        sp.dma_start(rows_out(tiles[n - 1]), r[:, (n - 1) % 2]).then_inc(stored[(n - 1) % 2], 16)
                n = len(tiles)
                sp.wait_ge(row_done, n)
                sp.dma_start(rows_out(tiles[-1]), r[:, (n - 1) % 2]).then_inc(stored[(n - 1) % 2], 16)
                for s in range(2):
                    sp.wait_ge(stored[s], 16 * len(range(s, n, 2)))

            @block.scalar
            def _(act):
                for k in range(KD):
                    act.wait_ge(w_in[k % 2], 16 * (k // 2 + 1))
                    act.activation(wo_h[:, k], w[:, k % 2], ACT.Copy).then_inc(w_high, 1)
                for n, t in enumerate(tiles):
                    act.wait_ge(a_in[n % 2], 16 * (n // 2 + 1))
                    if n >= 2:
                        act.wait_ge(made, n - 1)
                    act.activation(ah[:, n % 2], acc[:, n % 2], ACT.Copy).then_inc(a_high, 1)
                    if n >= 1:
                        act.wait_ge(var_done, n)
                        act.activation(std[:, n - 1:n], mv[:, n - 1, 1:2], ACT.Sqrt, bias=m.eps[:, 0:1]
                                       ).then_inc(std_done, 1)
                n = len(tiles)
                act.wait_ge(var_done, n)
                act.activation(std[:, n - 1:n], mv[:, n - 1, 1:2], ACT.Sqrt, bias=m.eps[:, 0:1]).then_inc(std_done, 1)

            @block.tensor
            def _(pe):
                pe.wait_ge(w_low, KD)
                for n, t in enumerate(tiles):
                    pe.wait_ge(a_low, n + 1)
                    if n >= 2:
                        pe.wait_ge(used, n - 1)
                    for c in range(2):
                        for k in range(KD):
                            mm = split_products(pe, m.ps[:, 2 * (n % 2) + c], ah[:, n % 2, k], al[:, n % 2, k],
                                                wo_h[:, k, 512 * c:512 * c + 512], wo_l[:, k, 512 * c:512 * c + 512],
                                                k == 0, k == KD - 1)
                    mm.then_inc(made, 1)

            @block.vector
            def _(dve):
                step = Tally(dve_step)
                then = lambda ins: step.then(dve, ins)
                for k in range(KD):
                    dve.wait_ge(w_high, k + 1)
                    dve.tensor_tensor(wo_l[:, k], w[:, k % 2], wo_h[:, k].bitcast(F32), ALU.subtract).then_inc(w_low, 1)

                def low(n):
                    dve.wait_ge(a_high, n + 1)
                    dve.tensor_tensor(al[:, n % 2], acc[:, n % 2], ah[:, n % 2].bitcast(F32), ALU.subtract
                                      ).then_inc(a_low, 1)
                low(0)
                dve.wait_ge(small_in, 32)
                for n, t in enumerate(tiles):
                    s = n % 2
                    if n + 1 < len(tiles):
                        low(n + 1)
                    g = 0 if t >= CT else 1
                    dve.wait_ge(made, n + 1)
                    dve.wait_ge(x_in[s], 16 * (n // 2 + 1))
                    if n >= 2:
                        dve.wait_ge(stored[s], 16 * (n // 2))
                    row = r[:, s].rearrange("p (c n) -> p c n", c=2)
                    then(dve.tensor_tensor(row, m.ps[:, 2 * s:2 * s + 2], gate[:, g].rearrange("p (c n) -> p c n", c=2),
                                           ALU.mult))
                    ins = dve.scalar_tensor_tensor(out=r[:, s], in0=x[:, s], scalar=ALPHA, in1=r[:, s], op0=ALU.mult,
                                                   op1=ALU.add)
                    ins.then_inc(used, 1)
                    dve.wait_ge(used, n + 1)
                    for j in range(2):
                        ins = dve.bn_stats(stats[:, n, j], r[:, s, 512 * j:512 * j + 512])
                    then(ins)
                    dve.bn_aggr(mv[:, n], stats[:, n]).then_inc(var_done, 1)
                    dve.wait_ge(std_done, n + 1)
                    then(dve.reciprocal(rstd[:, n:n + 1], std[:, n:n + 1]))
                    then(dve.tensor_scalar(r[:, s], r[:, s], mv[:, n, 0:1], rstd[:, n:n + 1], ALU.subtract, ALU.mult))
                    then(dve.tensor_tensor(r[:, s], r[:, s], lng[:, 0], ALU.mult))
                    dve.tensor_tensor(r[:, s], r[:, s], lng[:, 1], ALU.add).then_inc(row_done, 1)


def build(nc, d_x, d_c, d_const, d_rope, d_vec, d_bvec, d_wmod, d_win, d_winr, d_ws, d_bs, d_wuq, d_wukv,
          d_wmerge, d_wout, out, only=None, kind="Internal"):
    m = Mem()
    m.d_x, m.cvec, m.d_const, m.d_rope, m.d_vec, m.d_bvec, m.d_wmod = d_x, d_c, d_const, d_rope, d_vec, d_bvec, d_wmod
    m.d_win, m.d_winr, m.d_ws, m.d_bs, m.d_wuq, m.d_wukv = d_win, d_winr, d_ws, d_bs, d_wuq, d_wukv
    m.d_wmerge, m.d_wout = d_wmerge, d_wout
    m.d_x1 = nc.dram_tensor("x1", [ROWS, D], F32, kind=kind).ap()
    m.d_gate = nc.dram_tensor("gate_rows", [16, P], F32, kind=kind).ap()
    m.d_y = nc.dram_tensor("branches", [P, 8, ROWS], F32, kind=kind).ap()
    m.d_acc = nc.dram_tensor("merged", [P, KD, ROWS], F32, kind=kind).ap()
    with ExitStack() as st:
        sb = lambda n, s, d=F32: st.enter_context(nc.sbuf_tensor(n, s, d))
        m.ps = st.enter_context(nc.psum_tensor("ps", [P, 8, 512], F32))
        const = sb("const", [P, 3, P])
        m.ident, m.ones, m.blocks = const[:, 0], const[:, 1], const[:, 2]
        m.eps = sb("eps", [P, 1])
        m.vec = sb("vec", [P, V_COLS])
        m.shift = sb("shift", [P, KD, 2])
        m.scale = sb("scale", [P, KD, 2])
        m.gate_c = sb("gate_c", [P, 16])
        m.dv = sb("dv", [P, NT, BR])
        m.ab = sb("ab", [P, NT, 16])
        m.hh = sb("hh", [P, KD, ROWS], F32R)
        m.hl = sb("hl", [P, KD, ROWS], F32R)
        with phase(nc, "loaded") as (block, loaded):
            @block.sync
            def _(sp):
                sp.dma_start(const[:, 0:2], d_const[:, C_ID:C_ID + 2]).then_inc(loaded, 16)
                sp.dma_start(const[:, 2], d_const[:, C_BLK]).then_inc(loaded, 16)
                sp.wait_ge(loaded, 32)

            @block.vector
            def _(dve):
                dve.memset(m.eps[:], EPS)
        for l in range(DEPTH):
            for name, part in (("mod", modulation), ("ln", normalise_rows), ("gmlp", gating_mlp),
                               ("mla", latent_attention), ("diff", differential_attention), ("dn", delta_net),
                               ("merge", merge)):
                if only is None or (l, name) in only:
                    part(nc, m, l)
            if only is None or (l, "out") in only:
                output(nc, m, l, out)
        return m


def layouts(x, c, ctx, c_ctx, w_mod, b_mod, w_in, mla_q_norm, mla_w_uq, mla_kv_norm, mla_w_ukv, gmlp_ln_g, gmlp_w_s,
            gmlp_b_s, diff_lq1, diff_lk1, diff_lq2, diff_lk2, diff_norm_g, dn_conv_w, dn_a_log, dn_dt_bias, dn_norm_g,
            w_gate, w_branch, w_out, ln_g, ln_b):
    import numpy as np
    L = DEPTH
    A = np.asarray
    w_in, w_mod, w_gate, w_branch = A(w_in), A(w_mod), A(w_gate), A(w_branch)

    def blocks(w):
        n, k, c = w.shape
        return np.ascontiguousarray(w.reshape(n, k // P, P, c // P, P).transpose(0, 3, 2, 1, 4))

    def columns(v):
        return v.reshape(L, -1, P).transpose(0, 2, 1)

    dn0 = 416 + 512 + 768
    zero = np.zeros((L, D, P - ROPE), np.float32)
    w_t = np.concatenate([w_in[:, :, 0:416], zero, w_in[:, :, 928:928 + 512], w_in[:, :, dn0:dn0 + 768],
                          w_in[:, :, dn0 + 784:]], axis=2)
    w_r = np.concatenate([w_in[:, :, 416:928], w_in[:, :, 928 + 512:928 + 768],
                          w_in[:, :, dn0 + 768:dn0 + 784]], axis=2)
    uq = A(mla_w_uq).reshape(L, 2, P, HEADS, QK)
    uq = np.concatenate([uq[..., NOPE:].reshape(L, 2, P, HEADS * ROPE), uq[..., :NOPE].reshape(L, 2, P, HEADS * NOPE)],
                        axis=3).transpose(0, 2, 1, 3)
    ukv = A(mla_w_ukv).reshape(L, P, HEADS, 2, HD).transpose(0, 1, 3, 2, 4).reshape(L, P, 2 * HEADS * HD)
    gate_t = np.stack([blocks(w_gate[:, b]) for b in range(4)], axis=2)
    branch_t = np.stack([blocks(w_branch[:, b]) for b in range(4)], axis=2)
    merge_t = np.concatenate([gate_t, branch_t], axis=4).reshape(L, KD * 4, P, KD + 2, P)
    pad = np.zeros((L, 2, P, KD + 2, P), np.float32)
    conv = A(dn_conv_w).reshape(L, 3, 6, P).transpose(0, 3, 1, 2).reshape(L, P, 18)
    vec = np.concatenate([columns(A(b_mod)), columns(A(mla_q_norm)), columns(A(mla_kv_norm)), conv], axis=2)
    bvec = np.concatenate([A(ln_g), A(ln_b), A(gmlp_ln_g), A(diff_norm_g), A(dn_norm_g), A(diff_lq1), A(diff_lk1),
                           A(diff_lq2), A(diff_lk2), A(dn_a_log).reshape(L, 8), A(dn_dt_bias).reshape(L, 8)], axis=1)
    const = np.zeros((C_N, P, P), np.float32)
    i, j = np.arange(P)[:, None], np.arange(P)[None, :]
    const[C_ID] = i == j
    const[C_ONE] = 1
    const[C_PERM] = (i ^ 8) == j
    const[C_BLK] = i // HD == j // HD
    const[C_TRIF] = i <= j
    const[C_TRIB] = i >= j
    for r in range(4):
        source, high = i == 32 * r + j % 32, j // 32 % 2 == 0
        const[C_REP + r], const[C_REP + 4 + r] = source & high, source & ~high
    for v in range(LEVELS):
        b = 1 << v
        joins = (i // (2 * b) == j // (2 * b)) & (i // b % 2 == 1) & (j // b % 2 == 0)
        const[C_LVF + v], const[C_LVB + v] = joins, joins.T
    at = np.arange(SEQ, dtype=np.float32)
    line, col = np.floor(at / 64).astype(np.float32), at % 64
    freq = (np.float32(10000.0) ** (-np.arange(0, 16, 2, dtype=np.float32) / np.float32(16))).astype(np.float32)
    angle = np.concatenate([np.tile(freq[:, None] * line[None], (2, 1)), np.tile(freq[:, None] * col[None], (2, 1))])
    sign = np.where(np.arange(32) % 16 < 8, -1.0, 1.0).astype(np.float32)[:, None]
    rope = np.stack([np.tile(np.cos(angle), (4, 1)), np.tile(np.sin(angle) * sign, (4, 1))], axis=1)
    f = lambda a: np.ascontiguousarray(a, dtype=np.float32)
    cv = np.stack([A(c)[0], A(c_ctx)], axis=1).reshape(KD, P, 2).transpose(1, 0, 2)
    return {
        "d_x": f(np.concatenate([A(ctx)[0], A(x)[0]], axis=0)), "d_c": f(cv), "d_const": f(const.transpose(1, 0, 2)),
        "d_rope": f(rope), "d_vec": f(vec), "d_bvec": f(bvec), "d_wmod": f(blocks(w_mod)), "d_win": f(blocks(w_t)),
        "d_winr": f(w_r.reshape(L, KD, P, R_COLS)), "d_ws": f(A(gmlp_w_s).transpose(0, 3, 1, 2)),
        "d_bs": f(A(gmlp_b_s).transpose(0, 2, 1)), "d_wuq": f(uq), "d_wukv": f(ukv),
        "d_wmerge": f(np.concatenate([merge_t, pad], axis=1)), "d_wout": f(A(w_out).reshape(L, KD, P, D)),
    }


def kernel(**inputs):
    import numpy as np
    import concourse.bacc as bacc
    from concourse.bass_utils import run_bass_kernel_spmd

    nc = bacc.Bacc("TRN2", target_bir_lowering=False, num_devices=1)
    arrays = layouts(**inputs)
    aps = {n: nc.dram_tensor(f"in_{n}", list(a.shape), mybir.dt.from_np(a.dtype), kind="ExternalInput").ap()
           for n, a in arrays.items()}
    out = nc.dram_tensor("out_x", [SEQ, D], F32, kind="ExternalOutput").ap()
    build(nc, out=out, **aps)
    r = run_bass_kernel_spmd(nc, [{f"in_{n}": a for n, a in arrays.items()}], core_ids=[0])
    return r.results[0]["out_x"].reshape(1, SEQ, D)
```

```python
from contextlib import ExitStack, contextmanager

import concourse.bass as bass
from concourse import mybir

F32 = mybir.dt.float32
F32R = mybir.dt.float32r
ALU = mybir.AluOpType
ACT = mybir.ActivationFunctionType
AX = mybir.AxisListType
ds = bass.ds

P = 128
D = 1024
KD = D // P
CTX, SEQ = 256, 1024
ROWS = CTX + SEQ
NT = ROWS // P
CT = CTX // P
DEPTH = 2
BR = 256
HEADS = 4
NOPE, ROPE = 64, 32
QK = NOPE + ROPE
HD = 64
MAPS = 2 * HEADS
EPS = 1e-6
ALPHA = (2 * DEPTH) ** 0.25
CHUNKS = [(0, CTX), (CTX, 512), (CTX + 512, 512)]
T_MLA, T_DIFF, T_DN, T_GATE = 0, 4, 8, 14
R_GMLP, R_DV, R_AB, R_COLS = 0, 512, 768, 784
V_BMOD, V_QN, V_KVN, V_CONV, V_COLS = 0, 24, 26, 27, 45
B_LNG, B_LNB, B_GLN, B_DFN, B_DNN, B_LAM, B_ALOG, B_DTB, B_COLS = 0, 1024, 2048, 2304, 2368, 2432, 2560, 2568, 2576
C_ID, C_ONE, C_PERM, C_BLK, C_TRIF, C_TRIB, C_LVF, C_LVB, C_REP, C_N = 0, 1, 2, 3, 4, 5, 6, 13, 20, 28
LEVELS = 7


class Tally:

    def __init__(self, sem, base=0, i=None, per=0):
        self.sem, self.base, self.i, self.per, self.k = sem, base, i, per, 0

    def did(self, ins):
        self.k += 1
        ins.then_inc(self.sem, 1)

    def wait(self, eng):
        start = self.base if self.i is None else self.i * self.per + self.base
        eng.wait_ge(self.sem, start + self.k)

    def then(self, eng, ins):
        self.did(ins)
        self.wait(eng)

    def close(self):
        assert self.k == self.per, (self.k, self.per)


PHASES = []


@contextmanager
def phase(nc, *names):
    PHASES.append(names)
    sems = [nc.alloc_semaphore(f"{n}_{len(PHASES)}") for n in names]
    with nc.Block() as block:
        yield (block, *sems)
    nc.clear_and_free_semaphores(sems)
    nc.all_engine_barrier()


class Mem:
    pass


def split_products(pe, out, w_hi, w_lo, x_hi, x_lo, first, last):
    pe.matmul(out, w_hi, x_hi, start=first, stop=False)
    pe.matmul(out, w_hi, x_lo, start=False, stop=False)
    return pe.matmul(out, w_lo, x_hi, start=False, stop=last)


def modulation(nc, m, l):
    TOGETHER = 4
    LOADS = 24 // TOGETHER
    with ExitStack() as st:
        sb = lambda n, s, d=F32: st.enter_context(nc.sbuf_tensor(f"{n}_mod{l}", s, d))
        w = sb("w", [P, 24, KD, P])
        c = sb("c", [P, KD, 2])
        sc = sb("sc", [P, KD, 2])
        gt = sb("gt", [16, P])
        rows = sb("rows", [2, LOADS, TOGETHER * P])
        ph = phase(nc, "c_in", "silu", "rows_made", "rows_copied", "mod_done", "mod_added", "gate_t", "gate_copied", "gate_out",
                   *[f"w_in{s}" for s in range(LOADS)])
        with ph as (block, c_in, silu, rows_made, rows_copied, mod_done, mod_added, gate_t, gate_copied, gate_out, *w_in):

            @block.sync
            def _(sp):
                sp.dma_start(c[:], m.cvec).then_inc(c_in, 16)
                sp.dma_start(m.vec[:], m.d_vec[l]).then_inc(c_in, 16)
                for s in range(LOADS):
                    own = slice(s * TOGETHER, (s + 1) * TOGETHER)
                    sp.dma_start(w[:, own], m.d_wmod[l, own].rearrange("t p k c -> p t k c")).then_inc(w_in[s], 16)
                sp.wait_ge(gate_copied, 1)
                sp.dma_start(m.d_gate, gt[:]).then_inc(gate_out, 16)
                sp.wait_ge(gate_out, 16)

            @block.scalar
            def _(act):
                act.wait_ge(c_in, 32)
                act.activation(sc[:], c[:], ACT.Silu).then_inc(silu, 1)

            @block.tensor
            def _(pe):
                pe.wait_ge(silu, 1)

                def turn(s):
                    pe.wait_ge(rows_copied, s + 1)
                    for t in range(TOGETHER):
                        at = 2 * (s * TOGETHER + t)
                        mm = pe.transpose(m.ps[:, 7, at:at + 2], rows[:, s, t * P:(t + 1) * P], m.ident[0:2, 0:2])
                    return mm

                for s in range(LOADS):
                    pe.wait_ge(w_in[s], 16)
                    for k in range(KD):
                        mm = pe.matmul(m.ps[0:2, s, :], sc[:, k], w[:, s * TOGETHER:(s + 1) * TOGETHER, k],
                                       start=k == 0, stop=k == KD - 1)
                    mm.then_inc(rows_made, 1)
                    if s > 0:
                        turn(s - 1)
                mm = turn(LOADS - 1)
                mm.then_inc(mod_done, 1)
                pe.wait_ge(mod_added, 1)
                pe.transpose(m.ps[0:16, 1, 0:P], m.gate_c[:], m.ident).then_inc(gate_t, 1)

            @block.vector
            def _(dve):
                dve.wait_ge(c_in, 32)
                for s in range(LOADS):
                    dve.wait_ge(rows_made, s + 1)
                    dve.tensor_copy(rows[:, s], m.ps[0:2, s, :]).then_inc(rows_copied, 1)
                dve.wait_ge(mod_done, 1)
                mod = m.ps[:, 7, 0:48].rearrange("p (t c) -> p t c", c=2)
                bias = m.vec[:, V_BMOD:V_BMOD + 24].rearrange("p (t a) -> p t a", a=1)
                dve.tensor_tensor(m.gate_c[:].rearrange("p (c t) -> p t c", c=2), mod[:, 16:24],
                                  bias[:, 16:24].to_broadcast([P, 8, 2]), ALU.add).then_inc(mod_added, 1)
                dve.tensor_tensor(m.shift[:], mod[:, 0:8], bias[:, 0:8].to_broadcast([P, 8, 2]), ALU.add)
                dve.scalar_tensor_tensor(out=m.scale[:], in0=mod[:, 8:16], scalar=1.0,
                                         in1=bias[:, 8:16].to_broadcast([P, 8, 2]), op0=ALU.add, op1=ALU.add)
                dve.wait_ge(gate_t, 1)
                dve.tensor_copy(gt[:], m.ps[0:16, 1, 0:P]).then_inc(gate_copied, 1)


def normalise_rows(nc, m, l):
    SLOTS = 3
    src = m.d_x if l == 0 else m.d_x1
    with ExitStack() as st:
        sb = lambda n, s, d=F32: st.enter_context(nc.sbuf_tensor(f"{n}_ln{l}", s, d))
        x = sb("x", [P, SLOTS, D])
        h = sb("h", [P, 2, KD, P])
        stats = sb("stats", [P, NT, 2, 6])
        mv = sb("mv", [P, NT, 2])
        std = sb("std", [P, NT])
        rstd = sb("rstd", [P, NT])
        ph = phase(nc, *[f"x_in{s}" for s in range(SLOTS)], "var_done", "std_done", "dve_step", "xhat",
                   "turned", "scaled_d", "scaled_a", "high", "low")
        with ph as (block, *sems):
            x_in = sems[:SLOTS]
            var_done, std_done, dve_step, xhat, turned, scaled_d, scaled_a, high, low = sems[SLOTS:]

            @block.sync
            def _(sp):
                for t in range(NT):
                    if t >= SLOTS:
                        sp.wait_ge(turned, t - SLOTS + 1)
                    sp.dma_start(x[:, t % SLOTS], src[t * P:(t + 1) * P, :]).then_inc(x_in[t % SLOTS], 16)

            @block.vector
            def _(dve):
                step = Tally(dve_step)

                def part(t):
                    dve.wait_ge(turned, t + 1)
                    if t >= 2:
                        dve.wait_ge(high, t - 1)
                        dve.wait_ge(low, t - 1)
                    g = 0 if t >= CT else 1
                    for k in range(4):
                        ins = dve.tensor_scalar(h[:, t % 2, k], m.ps[:, 2 * (t % 2), k * P:(k + 1) * P],
                                                m.scale[:, k, g:g + 1], m.shift[:, k, g:g + 1], ALU.mult, ALU.add)
                    ins.then_inc(scaled_d, 1)

                def low_part(t):
                    dve.wait_ge(high, t + 1)
                    dve.wait_ge(scaled_a, t + 1)
                    dve.tensor_tensor(m.hl[:, :, t * P:(t + 1) * P], h[:, t % 2],
                                      m.hh[:, :, t * P:(t + 1) * P].bitcast(F32), ALU.subtract).then_inc(low, 1)

                for t in range(NT):
                    xs = x[:, t % SLOTS]
                    dve.wait_ge(x_in[t % SLOTS], 16 * (t // SLOTS + 1))
                    for j in range(2):
                        ins = dve.bn_stats(stats[:, t, j], xs[:, 512 * j:512 * j + 512])
                    step.then(dve, ins)
                    dve.bn_aggr(mv[:, t], stats[:, t]).then_inc(var_done, 1)
                    dve.wait_ge(std_done, t + 1)
                    step.then(dve, dve.reciprocal(rstd[:, t:t + 1], std[:, t:t + 1]))
                    dve.tensor_scalar(xs, xs, mv[:, t, 0:1], rstd[:, t:t + 1], ALU.subtract, ALU.mult).then_inc(xhat, 1)
                    if t >= 1:
                        part(t - 1)
                    if t >= 2:
                        low_part(t - 2)
                part(NT - 1)
                low_part(NT - 2)
                low_part(NT - 1)

            @block.tensor
            def _(pe):
                for t in range(NT):
                    pe.wait_ge(xhat, t + 1)
                    if t >= 2:
                        pe.wait_ge(scaled_d, t - 1)
                        pe.wait_ge(scaled_a, t - 1)
                    for k in range(KD):
                        mm = pe.transpose(m.ps[:, 2 * (t % 2) + k // 4, (k % 4) * P:(k % 4 + 1) * P],
                                          x[:, t % SLOTS, k * P:(k + 1) * P], m.ident)
                    mm.then_inc(turned, 1)

            @block.scalar
            def _(act):
                def part(t):
                    act.wait_ge(turned, t + 1)
                    if t >= 2:
                        act.wait_ge(low, t - 1)
                    g = 0 if t >= CT else 1
                    for k in range(4, KD):
                        ins = act.activation(h[:, t % 2, k], m.ps[:, 2 * (t % 2) + 1, (k - 4) * P:(k - 3) * P],
                                             ACT.Identity, bias=m.shift[:, k, g:g + 1], scale=m.scale[:, k, g:g + 1])
                    ins.then_inc(scaled_a, 1)
                    act.wait_ge(scaled_a, t + 1)
                    act.wait_ge(scaled_d, t + 1)
                    act.activation(m.hh[:, :, t * P:(t + 1) * P], h[:, t % 2], ACT.Copy).then_inc(high, 1)

                for t in range(NT):
                    act.wait_ge(var_done, t + 1)
                    act.activation(std[:, t:t + 1], mv[:, t, 1:2], ACT.Sqrt, bias=m.eps[:, 0:1]).then_inc(std_done, 1)
                    if t >= 1:
                        part(t - 1)
                part(NT - 1)


def project(nc, m, l, first, tiles, out, chunks, name):
    with ExitStack() as st:
        sb = lambda n, s, d=F32: st.enter_context(nc.sbuf_tensor(f"{n}_{name}{l}", s, d))
        w = sb("w", [P, 2, KD, P])
        wh = sb("wh", [P, 2, KD, P], F32R)
        wl = sb("wl", [P, 2, KD, P], F32R)
        n = len(chunks)
        ph = phase(nc, "w_in0", "w_in1", "w_high", "w_low", "made", "free_a", "free_d")
        with ph as (block, w_in0, w_in1, w_high, w_low, made, free_a, free_d):
            w_in = [w_in0, w_in1]
            per = [sum((s * n + c) % 2 == e for s in range(2) for c in range(n)) for e in range(2)]
            order = [(s, c) for s in range(2) for c in range(n)]

            def nth(s, c):
                return sum((a * n + b) % 2 == (s * n + c) % 2 for a, b in order[:order.index((s, c))])

            @block.sync
            def _(sp):
                for s in range(2):
                    sp.dma_start(w[:, s], m.d_win[l, first + s]).then_inc(w_in[s], 16)
                if tiles > 2:
                    with sp.Fori(1, tiles // 2) as i:
                        for s in range(2):
                            sp.wait_ge(w_low, i * 2 + (s - 1))
                            sp.dma_start(w[:, s], m.d_win[l, i * 2 + (first + s)]).then_inc(w_in[s], 16)

            def moves(eng, e, copy):
                eng.sem_inc(free_a if e == 0 else free_d, per[e])

                def cut(i, s):
                    eng.wait_ge(w_in[s], i * 16 + 16)
                    if e == 0:
                        eng.wait_ge(made, i * (2 * n) + (s + 1) * n)
                        eng.activation(wh[:, s], w[:, s], ACT.Copy).then_inc(w_high, 1)
                    else:
                        eng.wait_ge(w_high, i * 2 + (s + 1))
                        eng.tensor_tensor(wl[:, s], w[:, s], wh[:, s].bitcast(F32), ALU.subtract).then_inc(w_low, 1)

                def body(i, last):
                    for s in range(2):
                        for c, (at, width) in enumerate(chunks):
                            if c == 1 and not (last and s == 1):
                                cut(i + s, 1 - s)
                            if (s * n + c) % 2 == e:
                                eng.wait_ge(made, i * (2 * n) + (2 * n + s * n + c + 1))
                                ins = copy(out[:, i * 2 + s, at:at + width], m.ps[:, s * n + c, 0:width])
                                ins.then_inc(free_a if e == 0 else free_d, 1)

                cut(0, 0)
                if tiles > 2:
                    with eng.Fori(0, tiles // 2 - 1) as i:
                        body(i, False)
                body(tiles // 2 - 1, True)

            @block.scalar
            def _(act):
                moves(act, 0, lambda o, i: act.activation(o, i, ACT.Copy))

            @block.vector
            def _(dve):
                moves(dve, 1, lambda o, i: dve.tensor_copy(o, i))

            @block.tensor
            def _(pe):
                pe.sem_inc(made, 2 * n)
                with pe.Fori(0, tiles // 2) as i:
                    for s in range(2):
                        pe.wait_ge(w_low, i * 2 + (s + 1))
                        for c, (at, width) in enumerate(chunks):
                            e = (s * n + c) % 2
                            pe.wait_ge(free_d if e else free_a, i * per[e] + (nth(s, c) + 1))
                            for k in range(KD):
                                mm = split_products(pe, m.ps[:, s * n + c, 0:width], wh[:, s, k], wl[:, s, k],
                                                    m.hh[:, k, at:at + width], m.hl[:, k, at:at + width],
                                                    k == 0, k == KD - 1)
                            mm.then_inc(made, 1)


def turn_out(nc, m, l, branch, y_rows, y_t, tiles, y_ready, turned, copied, stored):
    def tensor(pe):
        for n, t in enumerate(tiles):
            pe.wait_ge(y_ready, n + 1)
            if n >= 2:
                pe.wait_ge(copied, n - 1)
            for b in range(2):
                mm = pe.transpose(m.ps[:, 6 + n % 2, b * P:(b + 1) * P], y_rows(t)[:, b * P:(b + 1) * P], m.ident)
            mm.then_inc(turned, 1)

    def vector(dve, n, t):
        dve.wait_ge(turned, n + 1)
        dve.tensor_copy(y_t[:, :, t * P:(t + 1) * P],
                        m.ps[:, 6 + n % 2, 0:BR].rearrange("p (b c) -> p b c", b=2)).then_inc(copied, 1)

    def store(sp):
        at = tiles[0] * P
        sp.wait_ge(copied, len(tiles))
        sp.dma_start(m.d_y[:, 2 * branch:2 * branch + 2, at:ROWS], y_t[:, :, at:ROWS]).then_inc(stored, 16)
        sp.wait_ge(stored, 16)
    return tensor, vector, store


def gating_mlp(nc, m, l):
    tiles = range(0 if l < DEPTH - 1 else CT, NT)
    with ExitStack() as st:
        sb = lambda n, s, d=F32: st.enter_context(nc.sbuf_tensor(f"{n}_gm{l}", s, d))
        w = sb("w", [P, KD, R_COLS])
        wh = sb("wh", [P, KD, R_COLS], F32R)
        wl = sb("wl", [P, KD, R_COLS], F32R)
        z = sb("z", [P, NT, 2, BR])
        ws = sb("ws", [P, HEADS, P])
        bs = sb("bs", [P, HEADS])
        g = sb("g", [P, BR])
        y_t = sb("y_t", [P, 2, ROWS])
        stats = sb("stats", [P, NT, 6])
        mv = sb("mv", [P, NT, 2])
        std = sb("std", [P, NT])
        rstd = sb("rstd", [P, NT])
        ph = phase(nc, "w_in0", "w_in1", "w_in2", "w_in3", "small_in", "w_high", "w_low", "made", "gelu", "kept", "stat", "std_done",
                   "dve_step", "v_ready", "mixed", "y_ready", "turned", "copied", "stored")
        with ph as (block, w_in0, w_in1, w_in2, w_in3, small_in, w_high, w_low, made, gelu, kept, stat, std_done,
                    dve_step, v_ready, mixed, y_ready, turned, copied, stored):
            w_in = [w_in0, w_in1, w_in2, w_in3]
            turn, copy_turned, store = turn_out(nc, m, l, 1, lambda t: z[:, t, 1], y_t, tiles,
                                                y_ready, turned, copied, stored)

            @block.sync
            def _(sp):
                for j in range(4):
                    sp.dma_start(w[:, 2 * j:2 * j + 2], m.d_winr[l, 2 * j:2 * j + 2].rearrange("k p c -> p k c")
                                 ).then_inc(w_in[j], 16)
                sp.dma_start(ws[:], m.d_ws[l]).then_inc(small_in, 16)
                sp.dma_start(bs[:], m.d_bs[l]).then_inc(small_in, 16)
                sp.dma_start(g[:], m.d_bvec[l:l + 1, B_GLN:B_GLN + BR].to_broadcast([P, BR])).then_inc(small_in, 16)
                store(sp)

            @block.scalar
            def _(act):
                for k in range(KD):
                    act.wait_ge(w_in[k // 2], 16)
                    act.activation(wh[:, k], w[:, k], ACT.Copy).then_inc(w_high, 1)
                for n, t in enumerate(tiles):
                    act.wait_ge(made, t + 1)
                    act.activation(z[:, t], m.ps[:, 2 * (t % 2), 0:512].rearrange("p (a b) -> p a b", a=2),
                                   ACT.Gelu_apprx_tanh).then_inc(gelu, 1)
                act.wait_ge(stat, 1)
                act.activation(std[:, tiles[0]:], mv[:, tiles[0]:, 1], ACT.Sqrt, bias=m.eps[:, 0:1]).then_inc(std_done, 1)

            @block.tensor
            def _(pe):
                for t in range(NT):
                    if t >= 2:
                        pe.wait_ge(kept, t - 1)
                        if t - 2 in tiles:
                            pe.wait_ge(gelu, t - 1 - tiles[0])
                    for b, (at, width) in enumerate(((R_GMLP, 512), (R_DV, R_COLS - R_DV))):
                        if b == 0 and t not in tiles:
                            continue
                        for k in range(KD):
                            if t == 0:
                                pe.wait_ge(w_low, k + 1)
                            h = [x[:, k, t * P:(t + 1) * P] for x in (m.hh, m.hl)]
                            mm = split_products(pe, m.ps[:, 2 * (t % 2) + b, 0:width], *h,
                                                wh[:, k, at:at + width], wl[:, k, at:at + width], k == 0, k == KD - 1)
                    mm.then_inc(made, 1)
                pe.wait_ge(small_in, 48)
                for n, t in enumerate(tiles):
                    pe.wait_ge(v_ready, n + 1)
                    if n >= 2:
                        pe.wait_ge(y_ready, n - 1)
                    for h in range(HEADS):
                        mm = pe.matmul(m.ps[:, 4 + n % 2, h * HD:(h + 1) * HD], ws[:, h],
                                       z[:, t, 1, h * HD:(h + 1) * HD], start=True, stop=True)
                    mm.then_inc(mixed, 1)
                turn(pe)

            @block.vector
            def _(dve):
                step = Tally(dve_step)
                for k in range(KD):
                    dve.wait_ge(w_high, k + 1)
                    dve.tensor_tensor(wl[:, k], w[:, k], wh[:, k].bitcast(F32), ALU.subtract).then_inc(w_low, 1)
                for t in range(NT):
                    dve.wait_ge(made, t + 1)
                    dve.tensor_copy(m.dv[:, t], m.ps[:, 2 * (t % 2) + 1, 0:BR])
                    dve.tensor_copy(m.ab[:, t], m.ps[:, 2 * (t % 2) + 1, BR:BR + 16]).then_inc(kept, 1)
                    if t in tiles:
                        dve.wait_ge(gelu, t + 1 - tiles[0])
                        step.then(dve, dve.bn_stats(stats[:, t], z[:, t, 1]))
                        ins = dve.bn_aggr(mv[:, t], stats[:, t])
                ins.then_inc(stat, 1)
                dve.wait_ge(std_done, 1)
                step.then(dve, dve.reciprocal(rstd[:, tiles[0]:], std[:, tiles[0]:]))
                dve.wait_ge(small_in, 48)
                for n, t in enumerate(tiles):
                    v = z[:, t, 1]
                    step.then(dve, dve.tensor_scalar(v, v, mv[:, t, 0:1], rstd[:, t:t + 1], ALU.subtract, ALU.mult))
                    dve.tensor_tensor(v, v, g[:], ALU.mult).then_inc(v_ready, 1)
                for n, t in enumerate(tiles):
                    dve.wait_ge(mixed, n + 1)
                    for h in range(HEADS):
                        part = slice(h * HD, (h + 1) * HD)
                        ins = dve.scalar_tensor_tensor(out=z[:, t, 1, part], in0=m.ps[:, 4 + n % 2, part],
                                                       scalar=bs[:, h:h + 1], in1=z[:, t, 0, part],
                                                       op0=ALU.add, op1=ALU.mult)
                    ins.then_inc(y_ready, 1)
                for n, t in enumerate(tiles):
                    copy_turned(dve, n, t)


def normalise_columns(nc, m, l, name, out, tiles, ones, factor, mean, gain, chunks=CHUNKS):
    with ExitStack() as st:
        sb = lambda n, s, d=F32: st.enter_context(nc.sbuf_tensor(f"{n}_{name}{l}", s, d))
        steps = [(grp, c) for grp in tiles for c in range(len(chunks))]
        wide = max(len(g) for g in tiles)
        sq = sb("sq", [P, 2, wide, 512])
        std = sb("std", [P, 2, 512])
        inv = sb("inv", [P, 2, 512])
        with phase(nc, "squared", "summed", "rooted", "inverted", "scaled") as (
                block, squared, summed, rooted, inverted, scaled):
            @block.gpsimd
            def _(pool):
                for n, (grp, c) in enumerate(steps):
                    at, width = chunks[c]
                    if n >= 2:
                        pool.wait_ge(summed, n - 1)
                    for a, j in enumerate(grp):
                        x = out[:, j, at:at + width]
                        ins = pool.tensor_tensor(sq[:, n % 2, a, 0:width], x, x, ALU.mult)
                    ins.then_inc(squared, 1)

            @block.tensor
            def _(pe):
                for n, (grp, c) in enumerate(steps):
                    width = chunks[c][1]
                    pe.wait_ge(squared, n + 1)
                    if n >= 2:
                        pe.wait_ge(rooted, n - 1)
                    for a in range(len(grp)):
                        mm = pe.matmul(m.ps[:, n % 2, 0:width], ones, sq[:, n % 2, a, 0:width],
                                       start=a == 0, stop=a == len(grp) - 1)
                    mm.then_inc(summed, 1)

            @block.scalar
            def _(act):
                for n, (grp, c) in enumerate(steps):
                    width = chunks[c][1]
                    act.wait_ge(summed, n + 1)
                    if n >= 2:
                        act.wait_ge(inverted, n - 1)
                    act.activation(std[:, n % 2, 0:width], m.ps[:, n % 2, 0:width], ACT.Sqrt, bias=m.eps[:, 0:1],
                                   scale=1.0 / mean(grp)).then_inc(rooted, 1)

            @block.vector
            def _(dve):
                for n, (grp, c) in enumerate(steps):
                    at, width = chunks[c]
                    dve.wait_ge(rooted, n + 1)
                    dve.reciprocal(inv[:, n % 2, 0:width], std[:, n % 2, 0:width]).then_inc(inverted, 1)
                    dve.wait_ge(inverted, n + 1)
                    dve.wait_ge(squared, n + 1)
                    for j in grp:
                        x = out[:, j, at:at + width]
                        f = gain(j) if gain else factor(j)
                        ins = dve.scalar_tensor_tensor(out=x, in0=x, scalar=f, in1=inv[:, n % 2, 0:width],
                                                       op0=ALU.mult, op1=ALU.mult)
                    ins.then_inc(scaled, 1)


def rotate_columns(nc, m, l, name, items):
    steps = [(x, c) for x in items for c in (1, 2)]
    with ExitStack() as st:
        sb = lambda n, s, d=F32: st.enter_context(nc.sbuf_tensor(f"{n}_{name}{l}", s, d))
        cos = sb("cos", [P, 2, SEQ])
        a = sb("a", [P, 2, 512])
        b = sb("b", [P, 2, 512])
        perm = sb("perm", [P, P])
        with phase(nc, "table_in", "swapped", "with_sin", "with_cos", "rotated") as (
                block, table_in, swapped, with_sin, with_cos, rotated):
            @block.sync
            def _(sp):
                sp.dma_start(cos[:], m.d_rope).then_inc(table_in, 16)
                sp.dma_start(perm[:], m.d_const[:, C_PERM]).then_inc(table_in, 16)

            @block.tensor
            def _(pe):
                pe.wait_ge(table_in, 32)
                for n, (x, c) in enumerate(steps):
                    at, width = CHUNKS[c]
                    q = x.shape[0]
                    if n >= 2:
                        pe.wait_ge(with_sin, n - 1)
                    pe.matmul(m.ps[0:q, n % 2, 0:width], perm[0:q, 0:q], x[:, at:at + width],
                              start=True, stop=True).then_inc(swapped, 1)

            @block.gpsimd
            def _(pool):
                pool.wait_ge(table_in, 32)
                for n, (x, c) in enumerate(steps):
                    at, width = CHUNKS[c]
                    q = x.shape[0]
                    if n >= 2:
                        pool.wait_ge(rotated, n - 1)
                    pool.tensor_tensor(b[0:q, n % 2], x[:, at:at + width], cos[0:q, 0, at - CTX:at - CTX + width],
                                       ALU.mult).then_inc(with_cos, 1)

            @block.vector
            def _(dve):
                dve.wait_ge(table_in, 32)
                for n, (x, c) in enumerate(steps):
                    at, width = CHUNKS[c]
                    q = x.shape[0]
                    dve.wait_ge(swapped, n + 1)
                    dve.tensor_tensor(a[0:q, n % 2], m.ps[0:q, n % 2, 0:width],
                                      cos[0:q, 1, at - CTX:at - CTX + width], ALU.mult).then_inc(with_sin, 1)
                    dve.wait_ge(with_sin, n + 1)
                    dve.wait_ge(with_cos, n + 1)
                    dve.tensor_tensor(x[:, at:at + width], a[0:q, n % 2], b[0:q, n % 2], ALU.add).then_inc(rotated, 1)


def expand_latents(nc, m, l, raw, q, k, v, qr):
    with ExitStack() as st:
        sb = lambda n, s, d=F32: st.enter_context(nc.sbuf_tensor(f"{n}_ex{l}", s, d))
        wq = sb("wq", [P, 2, HEADS * QK])
        wkv = sb("wkv", [P, 2 * HEADS * HD])
        jobs = []
        for at, width in CHUNKS:
            cols = slice(at, at + width)
            jobs.append((qr[:, cols], P, width, [(wq[:, j, 0:P], raw[:, j, cols]) for j in range(2)]))
            for h in range(HEADS):
                own = slice(P + h * NOPE, P + (h + 1) * NOPE)
                jobs.append((q[0:NOPE, h, cols], NOPE, width, [(wq[:, j, own], raw[:, j, cols]) for j in range(2)]))
                jobs.append((k[0:NOPE, h, cols], NOPE, width,
                             [(wkv[:, h * NOPE:(h + 1) * NOPE], raw[:, 2, cols])]))
        for t in range(NT):
            jobs.append((v[:, t], P, BR, [(raw[:, 2, t * P:(t + 1) * P], wkv[:, HEADS * NOPE:])]))
        with phase(nc, "w_in", "made", "moved_a", "moved_d") as (block, w_in, made, moved_a, moved_d):
            @block.sync
            def _(sp):
                sp.dma_start(wq[:], m.d_wuq[l]).then_inc(w_in, 16)
                sp.dma_start(wkv[:], m.d_wukv[l]).then_inc(w_in, 16)

            @block.tensor
            def _(pe):
                pe.wait_ge(w_in, 32)
                for n, (_, rows, width, pairs) in enumerate(jobs):
                    if n >= 4:
                        pe.wait_ge(moved_d if n % 2 else moved_a, (n - 4) // 2 + 1)
                    for a, (lhs, rhs) in enumerate(pairs):
                        mm = pe.matmul(m.ps[0:rows, n % 4, 0:width], lhs, rhs, start=a == 0, stop=a == len(pairs) - 1)
                    mm.then_inc(made, 1)

            @block.scalar
            def _(act):
                for n in range(0, len(jobs), 2):
                    out, rows, width, _ = jobs[n]
                    act.wait_ge(made, n + 1)
                    act.activation(out, m.ps[0:rows, n % 4, 0:width], ACT.Copy).then_inc(moved_a, 1)

            @block.vector
            def _(dve):
                for n in range(1, len(jobs), 2):
                    out, rows, width, _ = jobs[n]
                    dve.wait_ge(made, n + 1)
                    dve.tensor_copy(out, m.ps[0:rows, n % 4, 0:width]).then_inc(moved_d, 1)


def place_rotated(nc, m, l, raw, q, k, qr):
    with phase(nc, "done") as (block, done):
        @block.scalar
        def _(act):
            for h in range(HEADS):
                act.activation(k[NOPE:QK, h], raw[0:ROPE, 3], ACT.Copy)

        @block.vector
        def _(dve):
            for h in range(HEADS):
                dve.tensor_copy(q[NOPE:QK, h], qr[h * ROPE:(h + 1) * ROPE, :])


def attention(nc, m, l, name, q_part, k_all, v, y, qs, key_tiles, t0, t1, scale, maps, neg_lam, e=None):
    keys = key_tiles * P
    pieces = [(at, min(512, keys - at)) for at in range(0, keys, 512)]
    groups = [(0, 4), (4, 2), (6, 4)] if key_tiles == NT else [(0, CT)]
    G = len(groups)
    n_tiles = t1 - t0
    on_act = [g for g in range(G) if g % 2 == 1 or maps == 2]
    on_dve = [g for g in range(G) if g not in on_act]
    SL = 2 // maps
    value_at = pieces[-1][0] if maps == 2 or len(pieces) == 1 else pieces[-2][0]
    LAG = 2
    copies = len(q_part(0, 0))
    with ExitStack() as st:
        sb = lambda n, s, d=F32: st.enter_context(nc.sbuf_tensor(f"{n}_{name}{l}_{t0}", s, d))
        if e is None:
            e = sb("e", [P, 2, maps, keys])
        pt = sb("pt", [P, 2, key_tiles, P])
        mx = sb("mx", [P, HEADS, maps])
        nmx = sb("nmx", [P, HEADS, maps])
        total = sb("total", [P, HEADS, maps])
        inv = sb("inv", [P, HEADS, maps])
        own = sb("own", [P, HEADS])
        with phase(nc, "staged", "scored", "maximum", "exp_done", "inverse", "mixed",
                   "turned", "moved_a", "moved_d", "valued", "y_done", "dve_step", "mixing", "kept") as (
                block, staged, scored, maximum, exp_done, inverse, mixed,
                turned, moved_a, moved_d, valued, y_done, dve_step, mixing, kept):

            def bank(h, a):
                return 3 * (h % 2 if maps == 1 else a)

            def turn_bank(g, count):
                return m.ps[:, 7, BR:BR + count * P] if g == 1 else m.ps[:, 6, 0:count * P]

            def loop(eng, body, tail):
                body(0, False)
                with eng.Fori(1, n_tiles) as i:
                    body(i, True)
                tail(n_tiles)

            @block.gpsimd
            def _(pool):
                def body(i, prior):
                    for h in range(HEADS):
                        if prior:
                            pool.wait_ge(scored, i * (HEADS * maps) + (h - HEADS + 1) * maps)
                        for slot, src in q_part(h, i + t0):
                            pool.tensor_copy(slot, src).then_inc(staged, 1)
                loop(pool, body, lambda i: None)

            @block.tensor
            def _(pe):
                def turn(i, h, g):
                    at, count = groups[g]
                    u = i * HEADS + h
                    if maps == 1:
                        pe.wait_ge(exp_done, u + 1)
                    else:
                        pe.wait_ge(mixed, u + 1)
                    first = isinstance(i, int) and u == 0
                    if g == 1:
                        if h == 0 and not first:
                            pe.wait_ge(y_done, i + 0)
                    elif g == 2 or not first:
                        back, g_last = (0, 0) if g == 2 else (1, G - 1)
                        movers, moved = (on_act, moved_a) if g_last in on_act else (on_dve, moved_d)
                        pe.wait_ge(moved, (u - back) * len(movers) + (movers.index(g_last) + 1))
                    for b in range(count):
                        src = e[:, h % 2, maps - 1, (at + b) * P:(at + b + 1) * P]
                        mm = pe.transpose(turn_bank(g, count)[:, b * P:(b + 1) * P], src, m.ident)
                    mm.then_inc(turned, 1)

                def value(i, h):
                    u = i * HEADS + h
                    if on_act:
                        pe.wait_ge(moved_a, (u + 1) * len(on_act))
                    if on_dve:
                        pe.wait_ge(moved_d, (u + 1) * len(on_dve))
                    if h == 0 and not (isinstance(i, int) and i == 0):
                        pe.wait_ge(y_done, i + 0)
                    for b in range(key_tiles):
                        mm = pe.matmul(m.ps[:, 7, h * HD:(h + 1) * HD], pt[:, h % 2, b],
                                       v[:, b, h * HD:(h + 1) * HD], start=b == 0, stop=b == key_tiles - 1)
                    mm.then_inc(valued, 1)

                def body(i, prior):
                    for h in range(HEADS):
                        before = (i, h - LAG) if h >= LAG else (i - 1, h - LAG + HEADS)
                        has_before = prior or h >= LAG
                        pe.wait_ge(staged, (i * HEADS + (h + 1)) * copies)
                        valued_now = (i, h - LAG - 1) if h > LAG else (i - 1, h - LAG - 1 + HEADS)
                        has_valued = prior or h > LAG
                        g = 0
                        for a in range(maps):
                            if prior or h >= SL:
                                pe.wait_ge(exp_done, (i * HEADS + (h - SL)) * maps + (a + 1))
                            for at, width in pieces:
                                mm = pe.matmul(m.ps[:, bank(h, a) + at // 512, 0:width], qs(h, a),
                                               k_all(h, a)[:, at:at + width], start=True, stop=True)
                                if at + width == keys:
                                    mm.then_inc(scored, 1)
                                if a == 0 and has_valued and at == value_at:
                                    value(*valued_now)
                                if has_before and g < G and (at + width == keys or maps == 1 and at >= value_at):
                                    turn(*before, g)
                                    g += 1
                        while has_before and g < G:
                            turn(*before, g)
                            g += 1

                def tail(i):
                    value(i - 1, HEADS - LAG - 1)
                    for h in range(HEADS - LAG, HEADS):
                        for g in range(G):
                            turn(i - 1, h, g)
                        value(i - 1, h)
                loop(pe, body, tail)

            @block.vector
            def _(dve):
                def move(i, h, gs):
                    u = i * HEADS + h
                    for g in gs:
                        at, count = groups[g]
                        dve.wait_ge(turned, u * G + (g + 1))
                        if g == 0 and not (isinstance(i, int) and i * HEADS + h < 2):
                            dve.wait_ge(valued, u - 1)
                        dve.tensor_copy(pt[:, h % 2, at:at + count],
                                        turn_bank(g, count).rearrange("p (b c) -> p b c", b=count)
                                        ).then_inc(moved_d, 1)

                def invert(h):
                    dve.reciprocal(inv[:, h], total[:, h]).then_inc(inverse, 1)

                def finish(i):
                    dve.wait_ge(valued, (i + 1) * HEADS)
                    o = m.ps[:, 7, 0:BR].rearrange("p (h c) -> p h c", h=HEADS)
                    out = y[:, ds(i + t0, 1), :].rearrange("p a (h c) -> p (a h) c", h=HEADS)
                    dve.wait_ge(kept, i + 1)
                    dve.tensor_tensor(out, o, own[:].rearrange("p (h a) -> p h a", a=1).to_broadcast([P, HEADS, HD]), ALU.mult
                                      ).then_inc(y_done, 1)

                def keep(i):
                    dve.wait_ge(inverse, (i + 1) * HEADS)
                    if not (isinstance(i, int) and i == 0):
                        dve.wait_ge(y_done, i + 0)
                    dve.tensor_copy(own[:], inv[:, :, 0]).then_inc(kept, 1)

                def mix(i, h):
                    u = i * HEADS + h
                    dve.wait_ge(exp_done, (u + 1) * maps)
                    dve.reciprocal(inv[:, h], total[:, h]).then_inc(mixing, 1)
                    dve.wait_ge(mixing, u + 1)
                    dve.scalar_tensor_tensor(out=mx[:, h, 1:2], in0=inv[:, h, 1:2], scalar=total[:, h, 0:1], in1=neg_lam,
                                             op0=ALU.mult, op1=ALU.mult).then_inc(inverse, 1)
                    dve.wait_ge(inverse, u + 1)
                    dve.scalar_tensor_tensor(out=e[:, h % 2, 1], in0=e[:, h % 2, 1], scalar=mx[:, h, 1:2],
                                             in1=e[:, h % 2, 0], op0=ALU.mult, op1=ALU.add).then_inc(mixed, 1)

                def body(i, prior):
                    step = Tally(dve_step, 0, i, HEADS * maps)
                    for h in range(HEADS):
                        before = (i, h - LAG) if h >= LAG else (i - 1, h - LAG + HEADS)
                        has_before = prior or h >= LAG
                        if maps == 1 and prior and h == LAG:
                            finish(i - 1)
                        if has_before:
                            move(*before, on_dve)
                            if maps == 1:
                                invert(before[1])
                        if maps == 1 and prior and h == LAG - 1:
                            keep(i - 1)
                        for a in range(maps):
                            dve.wait_ge(scored, i * (HEADS * maps) + (h * maps + a + 1))
                            s = m.ps[:, bank(h, a):bank(h, a) + 3, :].rearrange("p b c -> p (b c)")[:, 0:keys]
                            step.then(dve, dve.reduce_max(mx[:, h, a:a + 1], s, AX.X))
                            dve.tensor_scalar(nmx[:, h, a:a + 1], mx[:, h, a:a + 1], -scale, None,
                                              ALU.mult).then_inc(maximum, 1)
                            if a == 0 and maps == 2 and (prior or h > 0):
                                mix(*((i, h - 1) if h else (i - 1, HEADS - 1)))
                                if h == 0:
                                    keep(i - 1)
                                if prior and h == LAG:
                                    finish(i - 1)

                def tail(i):
                    if maps == 2:
                        mix(i - 1, HEADS - 1)
                        keep(i - 1)
                    for h in range(HEADS - LAG, HEADS):
                        move(i - 1, h, on_dve)
                        if maps == 1:
                            invert(h)
                    if maps == 1:
                        keep(i - 1)
                    finish(i - 1)
                loop(dve, body, tail)

            @block.scalar
            def _(act):
                def move(i, h, gs):
                    u = i * HEADS + h
                    for g in gs:
                        at, count = groups[g]
                        act.wait_ge(turned, u * G + (g + 1))
                        if g == 0 and not (isinstance(i, int) and i * HEADS + h < 2):
                            act.wait_ge(valued, u - 1)
                        act.activation(pt[:, h % 2, at:at + count],
                                       turn_bank(g, count).rearrange("p (b c) -> p b c", b=count),
                                       ACT.Copy).then_inc(moved_a, 1)

                def body(i, prior):
                    for h in range(HEADS):
                        before = (i, h - LAG) if h >= LAG else (i - 1, h - LAG + HEADS)
                        has_before = prior or h >= LAG
                        if has_before:
                            move(*before, on_act if maps == 1 else on_act[:1])
                        for a in range(maps):
                            if has_before and a == 1:
                                move(*before, on_act[1:])
                            act.wait_ge(maximum, i * (HEADS * maps) + (h * maps + a + 1))
                            if prior or h >= 2:
                                if a == maps - 1:
                                    act.wait_ge(turned, (i * HEADS + (h - 1)) * G)
                                else:
                                    act.wait_ge(mixed, i * HEADS + (h - 1))
                            if prior:
                                act.wait_ge(inverse, i * HEADS + (h - HEADS + 1))
                            s = m.ps[:, bank(h, a):bank(h, a) + 3, :].rearrange("p b c -> p (b c)")[:, 0:keys]
                            act.activation(e[:, h % 2, a], s, ACT.Exp, bias=nmx[:, h, a:a + 1], scale=scale,
                                           accum_out=total[:, h, a:a + 1]).then_inc(exp_done, 1)
                loop(act, body, lambda i: [move(i - 1, h, on_act) for h in range(HEADS - LAG, HEADS)])


def latent_attention(nc, m, l):
    tiles = range(0 if l < DEPTH - 1 else CT, NT)
    with ExitStack() as st:
        sb = lambda n, s, d=F32: st.enter_context(nc.sbuf_tensor(f"{n}_la{l}", s, d))
        y = sb("y", [P, NT, BR])
        v = sb("v", [P, NT, BR])
        q = sb("q", [QK, HEADS, ROWS])
        k = sb("k", [QK, HEADS, ROWS])
        with ExitStack() as st2:
            raw = st2.enter_context(nc.sbuf_tensor(f"raw_la{l}", [P, 4, ROWS], F32))
            project(nc, m, l, T_MLA, 4, raw, CHUNKS, "pa")
            normalise_columns(nc, m, l, "na", raw, [[0, 1], [2]], m.ones, None, lambda g: P * len(g),
                              lambda j: m.vec[:, V_QN + j:V_QN + j + 1])
            qr = y[:, 0:5].rearrange("p t c -> p (t c)")
            expand_latents(nc, m, l, raw, q, k, v, qr)
            rotate_columns(nc, m, l, "ra", [qr, raw[0:ROPE, 3]])
            place_rotated(nc, m, l, raw, q, k, qr)
        qs = sb("qs", [QK, HEADS, P])
        for key_tiles, t0, t1 in ((CT, 0, CT), (NT, CT, NT))[l == DEPTH - 1:]:
            attention(nc, m, l, "a", lambda h, t: [(qs[:, h], q[:, h, ds(t * P, P)])], lambda h, a: k[:, h],
                      v, y, lambda h, a: qs[:, h], key_tiles, t0, t1, QK ** -0.5, 1, None)
        store_rows(nc, m, l, 0, y, tiles)


def store_rows(nc, m, l, branch, y, tiles):
    with nc.sbuf_tensor(f"y_t{branch}_{l}", [P, 2, ROWS], F32) as y_t, phase(
            nc, "y_ready", "turned", "copied", "stored") as (block, y_ready, turned, copied, stored):
        turn, copy_turned, store = turn_out(nc, m, l, branch, lambda t: y[:, t], y_t, tiles,
                                            y_ready, turned, copied, stored)

        @block.sync
        def _(sp):
            store(sp)

        @block.tensor
        def _(pe):
            turn(pe)

        @block.vector
        def _(dve):
            dve.sem_inc(y_ready, len(tiles))
            for n, t in enumerate(tiles):
                copy_turned(dve, n, t)


def stack_keys(nc, m, l, qk, rep, kk, qh, ql, vecs, lam, prod, lam_init):
    pieces = [(j, at, min(512, ROWS - at)) for j in range(MAPS) for at in range(0, ROWS, 512)]
    kl = ql
    with nc.sbuf_tensor(f"kh_{l}", [P, 2, ROWS], F32R) as kh, nc.sbuf_tensor(f"rep_{l}", [P, MAPS, P], F32) as rep_raw:
        with phase(nc, "vecs_in", "rep_in", "dve_step", "lam_exp", "rep_cut", "k_high", "k_low", "q_high", "stacked",
                   "moved_a", "moved_d") as (block, vecs_in, rep_in, dve_step, lam_exp, rep_cut, k_high, k_low,
                                             q_high, stacked, moved_a, moved_d):
            @block.sync
            def _(sp):
                sp.dma_start(rep_raw[:], m.d_const[:, C_REP:C_REP + MAPS]).then_inc(rep_in, 16)
                sp.dma_start(vecs[:, 0:HD], m.d_bvec[l:l + 1, B_DFN:B_DFN + HD].to_broadcast([P, HD])
                             ).then_inc(vecs_in, 16)
                sp.dma_start(vecs[:, HD:], m.d_bvec[l:l + 1, B_LAM:B_LAM + 4 * ROPE].to_broadcast([P, 4 * ROPE])
                             ).then_inc(vecs_in, 16)

            def move(eng, e, moved, copy):
                for n, (j, at, width) in enumerate(pieces):
                    if n % 2 == e:
                        eng.wait_ge(stacked, n + 1)
                        copy(kk[:, j, at:at + width], m.ps[:, n % 8, 0:width]).then_inc(moved, 1)

            @block.tensor
            def _(pe):
                pe.wait_ge(rep_cut, 1)
                for n, (j, at, width) in enumerate(pieces):
                    if at == 0 and j % 4 == 0:
                        pe.wait_ge(k_low, j // 4 + 1)
                    if n >= 8:
                        pe.wait_ge((moved_a, moved_d)[n % 2], (n - 8) // 2 + 1)
                    pe.matmul(m.ps[:, n % 8, 0:width], rep[:, j % 4], kh[:, j // 4, at:at + width],
                              start=True, stop=False)
                    pe.matmul(m.ps[:, n % 8, 0:width], rep[:, 4 + j % 4], kl[:, j // 4, at:at + width],
                              start=False, stop=True
                              ).then_inc(stacked, 1)

            @block.scalar
            def _(act):
                for j in range(2):
                    act.activation(kh[:, j], qk[:, 2 + j], ACT.Copy).then_inc(k_high, 1)
                    if j == 0:
                        act.wait_ge(rep_in, 16)
                        act.activation(rep[:], rep_raw[:], ACT.Copy).then_inc(rep_cut, 1)
                move(act, 0, moved_a, lambda o, i: act.activation(o, i, ACT.Copy))
                for j in range(2):
                    act.activation(qh[:, j], qk[:, j], ACT.Copy).then_inc(q_high, 1)
                act.wait_ge(dve_step, 2)
                act.activation(lam[:], lam[:], ACT.Exp).then_inc(lam_exp, 1)

            @block.vector
            def _(dve):
                for j in range(2):
                    dve.wait_ge(k_high, j + 1)
                    dve.tensor_tensor(kl[:, j], qk[:, 2 + j], kh[:, j].bitcast(F32), ALU.subtract
                                      ).then_inc(k_low, 1)
                move(dve, 1, moved_d, lambda o, i: dve.tensor_copy(o, i))
                step = Tally(dve_step)
                dve.wait_ge(vecs_in, 32)
                pairs = vecs[:, HD:].rearrange("p (a b c) -> p a b c", a=2, b=2)
                step.then(dve, dve.tensor_tensor(prod[:], pairs[:, :, 0], pairs[:, :, 1], ALU.mult))
                step.then(dve, dve.reduce_sum(lam[:], prod[:], AX.X))
                for j in range(2):
                    dve.wait_ge(q_high, j + 1)
                    dve.wait_ge(stacked, len(pieces))
                    dve.tensor_tensor(ql[:, j], qk[:, j], qh[:, j].bitcast(F32), ALU.subtract)
                dve.wait_ge(lam_exp, 1)
                step.then(dve, dve.tensor_scalar(lam[:, 1:2], lam[:, 1:2], lam[:, 0:1], -lam_init,
                                                 ALU.subtract, ALU.add))
                dve.tensor_scalar(vecs[:, 0:HD], vecs[:, 0:HD], 1.0 - lam_init, None, ALU.mult)


def differential_attention(nc, m, l):
    import math
    lam_init = 0.8 - 0.6 * math.exp(-0.3 * l)
    tiles = range(0 if l < DEPTH - 1 else CT, NT)
    n_t = len(tiles)
    with ExitStack() as st:
        sb = lambda n, s, d=F32: st.enter_context(nc.sbuf_tensor(f"{n}_da{l}", s, d))
        y = sb("y", [P, NT, BR])
        qk = sb("qk", [P, 4, ROWS])
        vecs = sb("vecs", [P, HD + 4 * ROPE])
        lam = sb("lam", [P, 2])
        prod = sb("prod", [P, 2, ROPE])
        project(nc, m, l, T_DIFF, 4, qk, CHUNKS, "pd")
        rotate_columns(nc, m, l, "rd", [qk[:, j] for j in range(4)])
        qs = sb("qs", [P, MAPS, P], F32R)
        kk = sb("kk", [P, MAPS, ROWS], F32R)
        qh = sb("qh", [P, 2, ROWS], F32R)
        ql = sb("ql", [P, 2, ROWS], F32R)
        stack_keys(nc, m, l, qk, qs, kk, qh, ql, vecs, lam, prod, lam_init)

        def q_part(h, t):
            out = []
            for j in (2 * h, 2 * h + 1):
                rows = slice(32 * (j % 4), 32 * (j % 4) + 32)
                out += [(qs[32 * a:32 * a + 32, j], (qh, ql)[a // 2][rows, j // 4, ds(t * P, P)]) for a in range(4)]
            return out
        e = qk[:].rearrange("p (s a) c -> p s a c", s=2)
        for key_tiles, t0, t1 in ((CT, 0, CT), (NT, CT, NT))[l == DEPTH - 1:]:
            attention(nc, m, l, "d", q_part, lambda h, a: kk[:, 2 * h + a], m.dv, y,
                      lambda h, a: qs[:, 2 * h + a], key_tiles, t0, t1, ROPE ** -0.5, 2, lam[:, 1:2],
                      e[:, :, :, 0:key_tiles * P])
        normalise_heads(nc, m, l, "nd", y, tiles, vecs[:, 0:HD])
        store_rows(nc, m, l, 2, y, tiles)


def normalise_heads(nc, m, l, name, y, tiles, gain):
    with ExitStack() as st:
        sb = lambda n, s, d=F32: st.enter_context(nc.sbuf_tensor(f"{n}_{name}{l}", s, d))
        sq = sb("sq", [P, NT, BR])
        ssq = sb("ssq", [P, NT * HEADS])
        std = sb("std", [P, NT * HEADS])
        inv = sb("inv", [P, NT * HEADS])
        a, b = tiles[0], NT
        n = (b - a) * HEADS
        heads = lambda x: x[:, a:b].rearrange("p t (h c) -> p (t h) c", h=HEADS)
        with phase(nc, "dve_step", "rooted") as (block, dve_step, rooted):
            @block.vector
            def _(dve):
                step = Tally(dve_step)
                step.then(dve, dve.tensor_tensor(sq[:, a:b], y[:, a:b], y[:, a:b], ALU.mult))
                step.then(dve, dve.reduce_sum(ssq[:, 0:n], heads(sq), AX.X))
                dve.wait_ge(rooted, 1)
                step.then(dve, dve.reciprocal(inv[:, 0:n], std[:, 0:n]))
                by = inv[:, 0:n].rearrange("p (n a) -> p n a", a=1).to_broadcast([P, n, HD])
                step.then(dve, dve.tensor_tensor(heads(y), heads(y), by, ALU.mult))
                dve.tensor_tensor(heads(y), heads(y), gain.rearrange("p (a c) -> p a c", a=1).to_broadcast([P, n, HD]),
                                  ALU.mult)

            @block.scalar
            def _(act):
                act.wait_ge(dve_step, 2)
                act.activation(std[:, 0:n], ssq[:, 0:n], ACT.Sqrt, bias=m.eps[:, 0:1], scale=1.0 / HD).then_inc(rooted, 1)


def convolve(nc, m, l, qkv):
    with nc.sbuf_tensor(f"acc_cv{l}", [P, 2, ROWS], F32) as acc, phase(nc, "scaled", "convolved", "dve_step", "silu") as (
            block, scaled, convolved, dve_step, silu):
        def taps(j):
            return [m.vec[:, V_CONV + 6 * i + j:V_CONV + 6 * i + j + 1] for i in range(3)]

        @block.vector
        def _(dve):
            step = Tally(dve_step)
            for j in range(6):
                a = acc[:, j % 2]
                tap = taps(j)
                dve.wait_ge(scaled, j + 1)
                for n, (lo, hi) in enumerate(((0, CTX), (CTX, ROWS))):
                    ins = dve.scalar_tensor_tensor(out=a[:, lo + 1:hi], in0=qkv[:, j, lo:hi - 1], scalar=tap[0],
                                                   in1=a[:, lo + 1:hi], op0=ALU.mult, op1=ALU.add)
                step.then(dve, ins)
                for n, (lo, hi) in enumerate(((0, CTX), (CTX, ROWS))):
                    ins = dve.scalar_tensor_tensor(out=a[:, lo:hi - 1], in0=qkv[:, j, lo + 1:hi], scalar=tap[2],
                                                   in1=a[:, lo:hi - 1], op0=ALU.mult, op1=ALU.add)
                ins.then_inc(convolved, 1)

        @block.scalar
        def _(act):
            def scale(j):
                if j >= 2:
                    act.wait_ge(silu, j - 1)
                act.activation(acc[:, j % 2], qkv[:, j], ACT.Copy, scale=taps(j)[1]).then_inc(scaled, 1)
            scale(0)
            scale(1)
            for j in range(6):
                act.wait_ge(convolved, j + 1)
                act.activation(qkv[:, j], acc[:, j % 2], ACT.Silu).then_inc(silu, 1)
                if j + 2 < 6:
                    scale(j + 2)


def turn_keys(nc, m, l, qkv, kv):
    with phase(nc, "turned", "moved_a", "moved_d") as (block, turned, moved_a, moved_d):
        @block.tensor
        def _(pe):
            for t in range(NT):
                if t >= 4:
                    pe.wait_ge(moved_d if t % 2 else moved_a, (t - 4) // 2 + 1)
                for j in range(4):
                    mm = pe.transpose(m.ps[:, t % 4, j * P:(j + 1) * P], qkv[:, 2 + j, t * P:(t + 1) * P], m.ident)
                mm.then_inc(turned, 1)

        @block.scalar
        def _(act):
            for t in range(0, NT, 2):
                act.wait_ge(turned, t + 1)
                act.activation(kv[:, t], m.ps[:, t % 4], ACT.Copy).then_inc(moved_a, 1)

        @block.vector
        def _(dve):
            for t in range(1, NT, 2):
                dve.wait_ge(turned, t + 1)
                dve.tensor_copy(kv[:, t], m.ps[:, t % 4]).then_inc(moved_d, 1)


def decay_gates(nc, m, l, g):
    TERMS = 9
    G_DONE = 2 + 5 + (TERMS - 1) + 4
    with ExitStack() as st:
        sb = lambda n, s, d=F32: st.enter_context(nc.sbuf_tensor(f"{n}_dg{l}", s, d))
        vecs = sb("vecs", [P, 16])
        tri = sb("tri", [P, 2, P])
        x = sb("x", [P, NT, MAPS])
        y = sb("y", [P, NT, MAPS])
        z = sb("z", [P, NT, MAPS])
        z2 = sb("z2", [P, NT, MAPS])
        r = sb("r", [P, NT, MAPS])
        gl = sb("gl", [P, NT, MAPS])
        last = sb("last", [P, NT, MAPS])
        bc = lambda v: v.rearrange("p (a c) -> p a c", a=1).to_broadcast([P, NT, MAPS])
        with phase(nc, "loaded", "dve_step", "act_step", "pe_step") as (block, loaded, dve_step, act_step, pe_step):
            @block.sync
            def _(sp):
                sp.dma_start(vecs[:], m.d_bvec[l:l + 1, B_ALOG:B_ALOG + 16].to_broadcast([P, 16])).then_inc(loaded, 16)
                sp.dma_start(tri[:], m.d_const[:, C_TRIF:C_TRIF + 2]).then_inc(loaded, 16)

            @block.vector
            def _(dve):
                step = Tally(dve_step)
                then = lambda ins: step.then(dve, ins)
                dve.wait_ge(loaded, 32)
                then(dve.tensor_tensor(x[:], m.ab[:, :, 0:8], bc(vecs[:, 8:16]), ALU.add))
                then(dve.scalar_tensor_tensor(out=y[:], in0=x[:], scalar=-1.0, in1=x[:], op0=ALU.mult, op1=ALU.min))
                dve.wait_ge(act_step, 1)
                then(dve.tensor_scalar(z[:], y[:], 2.0, None, ALU.add))
                then(dve.reciprocal(z[:], z[:]))
                then(dve.tensor_tensor(z[:], z[:], y[:], ALU.mult))
                then(dve.tensor_tensor(z2[:], z[:], z[:], ALU.mult))
                then(dve.tensor_scalar(r[:], z2[:], 1.0 / (2 * TERMS + 1), None, ALU.mult))
                for n in range(TERMS - 1, 0, -1):
                    then(dve.scalar_tensor_tensor(out=r[:], in0=r[:], scalar=1.0 / (2 * n + 1), in1=z2[:],
                                                  op0=ALU.add, op1=ALU.mult))
                then(dve.scalar_tensor_tensor(out=r[:], in0=r[:], scalar=1.0, in1=z[:], op0=ALU.add, op1=ALU.mult))
                then(dve.tensor_scalar(x[:], x[:], 0.0, None, ALU.max))
                then(dve.scalar_tensor_tensor(out=r[:], in0=r[:], scalar=2.0, in1=x[:], op0=ALU.mult, op1=ALU.add))
                then(dve.scalar_tensor_tensor(out=gl[:], in0=r[:], scalar=-1.0, in1=bc(vecs[:, 0:8]),
                                              op0=ALU.mult, op1=ALU.mult))
                dve.wait_ge(pe_step, 1)
                for d in range(2):
                    dve.tensor_copy(g.gam[:, :, 4 * d:4 * d + 4],
                                    m.ps[:, d, 0:NT * 4].rearrange("p (t h) -> p t h", h=4))
                then(dve.tensor_copy(last[:], m.ps[:, 2, 0:NT * 8].rearrange("p (t h) -> p t h", h=8)))
                then(dve.tensor_tensor(g.kd[:], last[:], g.gam[:], ALU.subtract))
                dve.wait_ge(act_step, 4)
                dve.tensor_tensor(g.be[:], g.beta[:], g.eg[:], ALU.mult)
                for par in range(2):
                    rows = slice(64 * par, 64 * par + 64)
                    for d in range(2):
                        dve.tensor_copy(g.last[rows, :, d], last[rows, :, 4 * d + par:4 * d + 4:2])

            @block.scalar
            def _(act):
                act.wait_ge(dve_step, 2)
                act.activation(vecs[:, 0:8], vecs[:, 0:8], ACT.Exp)
                act.activation(y[:], y[:], ACT.Exp).then_inc(act_step, 1)
                act.wait_ge(dve_step, G_DONE + 2)
                act.activation(last[:], last[:], ACT.Exp).then_inc(act_step, 1)
                act.activation(g.kd[:], g.kd[:], ACT.Exp)
                act.activation(g.eg[:], g.gam[:], ACT.Exp).then_inc(act_step, 1)
                act.activation(g.beta[:], m.ab[:, :, 8:16], ACT.Sigmoid).then_inc(act_step, 1)

            @block.tensor
            def _(pe):
                pe.wait_ge(dve_step, G_DONE)
                for d in range(2):
                    pe.matmul(m.ps[:, d, 0:NT * 4], tri[:, d], gl[:, :, 4 * d:4 * d + 4], start=True, stop=True)
                pe.matmul(m.ps[:, 2, 0:NT * 8], m.ones, gl[:], start=True, stop=True).then_inc(pe_step, 1)


def delta_rule(nc, m, l, qkv, kv, o, g):
    with ExitStack() as st:
        sb = lambda n, s, d=F32: st.enter_context(nc.sbuf_tensor(f"{n}_dr{l}", s, d))
        lv = sb("lv", [P, 2, LEVELS, P])
        inc = sb("inc", [P, 2, P])
        quad = lambda n: [sb(f"{n}{d}", [P, HEADS, P]) for d in range(2)]
        staged_t, joins, E, A, AT, T, TT, V, PT = (quad(n) for n in (
            "st", "joins", "E", "A", "AT", "T", "TT", "V", "PT"))
        half = lambda n: [sb(f"{n}{d}", [P, HEADS, HD]) for d in range(2)]
        xk, xv, kdec, vn = (half(n) for n in ("xk", "xv", "kdec", "vn"))
        qd = [sb(f"qd{d}", [P, 2, P]) for d in range(2)]
        wt = [sb(f"wt{d}", [P, 2, P]) for d in range(2)]
        kz = [sb(f"kz{d}", [P, HEADS, P]) for d in range(2)]
        EG = V
        S = [sb(f"S{d}", [P, 2, 2, HD]) for d in range(2)]
        names = ("staged", "kz_ready", "diag", "grams", "qk_made", "e_in", "e_exp", "eg_done", "a_ready", "pt_ready", "at_turned", "at_ready",
                 "t_ready", "t_turned", "tt_ready", "join_ready", "v_made", "v_ready", "x_made", "t_new", "tt_new", "pt_made",
                 "rows_ready", "w_made", "w_ready",
                 "qd_ready", "vn_made", "vn_ready", "o_made", "o_added", "s_made", "s_scaled", "s_new", "dve_step")
        all_names = [f"{n}{'fb'[d]}" for n in names for d in range(2)]
        SEGMENTS = ((0, CT, 0, l < DEPTH - 1), (CT, NT - CT, CT, True))
        with phase(nc, "loaded", "cleared", *all_names) as (block, loaded, cleared, *rest):
            sem = {n: rest[2 * a:2 * a + 2] for a, n in enumerate(names)}
            bank = lambda d, b: m.ps[:, 4 * d + b]
            wide = lambda x: x.rearrange("p (h c) -> p h c", h=HEADS)
            own = lambda h: slice(64 * (h % 2), 64 * (h % 2) + 64)
            LV = LEVELS - 1

            def steps(eng, between, inverse):
                for t0, n, s0, wants in SEGMENTS:
                    def at(i):
                        if isinstance(i, int):
                            return i + s0, [i + t0, t0 + n - 1 - i], wants
                        return i + s0, [eng.snap(i + t0), eng.snap(i * -1 + (t0 + n - 1))], wants
                    between(at(0), None)
                    inverse(at(0))
                    with eng.Fori(1, n) as i:
                        between(at(i), at(i - 1))
                        inverse(at(i))
                    between(None, at(n - 1))

            def per_head(x, tile, d, width):
                v = x[:, ds(tile, 1), 4 * d:4 * d + 4].rearrange("p t h -> p h t")
                return v.to_broadcast([P, HEADS, width])

            @block.sync
            def _(sp):
                sp.dma_start(lv[:], m.d_const[:, C_LVF:C_LVF + 2 * LEVELS].rearrange(
                    "p (d v) c -> p d v c", d=2)).then_inc(loaded, 16)
                sp.dma_start(inc[:], m.d_const[:, C_TRIF:C_TRIF + 2]).then_inc(loaded, 16)

            @block.gpsimd
            def _(pool):
                pool.wait_ge(loaded, 32)

                def inverse(step):
                    s, tiles, _ = step
                    for d in range(2):
                        t = tiles[d]
                        pool.tensor_copy(staged_t[d][:], qkv[:, 0:4, ds(t * P, P)]).then_inc(sem["staged"][d], 1)
                        pool.wait_ge(sem["v_made"][d], s * LV + 1)
                        pool.tensor_tensor(joins[d][:], m.ident.rearrange("p (a c) -> p a c", a=1).to_broadcast(
                            [P, HEADS, P]), per_head(g.gam, t, d, P), ALU.mult).then_inc(sem["diag"][d], 1)
                    for b in range(LV):
                        for d in range(2):
                            if b == 0:
                                pool.wait_ge(sem["at_ready"][d], s + 1)
                            else:
                                pool.wait_ge(sem["v_made"][d], s * LV + (b + 1))
                            pool.tensor_tensor(joins[d][:], AT[d][:], lv[:, 1 - d, b + 1:b + 2].to_broadcast(
                                [P, HEADS, P]), ALU.mult).then_inc(sem["join_ready"][d], 1)
                        if b == 0:
                            for d in range(2):
                                t = tiles[d]
                                k = wide(kv[:, ds(t, 1), 0:BR].rearrange("p a c -> p (a c)"))
                                v = wide(kv[:, ds(t, 1), BR:2 * BR].rearrange("p a c -> p (a c)"))
                                pool.wait_ge(sem["s_made"][d], s + 1)
                                pool.tensor_tensor(xk[d][:], k, per_head(g.be, t, d, HD), ALU.mult)
                                pool.tensor_tensor(xv[d][:], v, per_head(g.beta, t, d, HD), ALU.mult)
                                pool.tensor_tensor(kdec[d][:], k, per_head(g.kd, t, d, HD), ALU.mult
                                                   ).then_inc(sem["rows_ready"][d], 1)
                        if b == 1:
                            for d in range(2):
                                pool.wait_ge(sem["pt_made"][d], s + 1)
                                pool.tensor_tensor(PT[d][:], PT[d][:], inc[:, d:d + 1].to_broadcast([P, HEADS, P]),
                                                   ALU.mult).then_inc(sem["pt_ready"][d], 1)
                steps(pool, lambda step, last: None, inverse)

            @block.tensor
            def _(pe):
                for d in range(2):
                    pe.sem_inc(sem["s_made"][d], 1)
                    pe.sem_inc(sem["qk_made"][d], 1)
                    pe.sem_inc(sem["v_made"][d], 1)
                pe.wait_ge(cleared, 5)

                def scores(s):
                    for d in range(2):
                        pe.wait_ge(sem["staged"][d], s + 1)
                        pe.wait_ge(sem["kz_ready"][d], s + 1)
                        pe.wait_ge(sem["diag"][d], s + 1)
                        for h in range(HEADS):
                            pe.matmul(bank(d, 0)[:, h * P:(h + 1) * P], kz[d][:, h], staged_t[d][:, 2 + h // 2],
                                      start=True, stop=True)
                        pe.matmul(bank(d, 3), m.ones, joins[d][:], start=True, stop=True).then_inc(sem["grams"][d], 1)
                    for d in range(2):
                        if not (isinstance(s, int) and s == 0):
                            pe.wait_ge(sem["tt_new"][d], s + 0)
                        for h in range(HEADS):
                            mm = pe.matmul(bank(d, 1)[:, h * P:(h + 1) * P], kz[d][:, h], staged_t[d][:, h // 2],
                                           start=True, stop=True)
                        mm.then_inc(sem["qk_made"][d], 1)

                def turn_a(s):
                    for d in range(2):
                        pe.wait_ge(sem["a_ready"][d], s + 1)
                        pe.wait_ge(sem["eg_done"][d], s + 1)
                        for h in range(HEADS):
                            mm = pe.transpose(bank(d, 3)[:, h * P:(h + 1) * P], A[d][:, h], m.ident)
                        mm.then_inc(sem["at_turned"][d], 1)

                def inverse(step):
                    s = step[0]
                    for b in range(LV):
                        for d in range(2):
                            if b == 0:
                                pe.wait_ge(sem["t_ready"][d], s + 1)
                            else:
                                pe.wait_ge(sem["t_new"][d], s * (LV - 1) + b)
                            pe.wait_ge(sem["join_ready"][d], s * LV + (b + 1))
                            for h in range(HEADS):
                                mm = pe.matmul(bank(d, 3)[:, h * P:(h + 1) * P], joins[d][:, h], T[d][:, h],
                                               start=True, stop=True)
                            mm.then_inc(sem["v_made"][d], 1)
                            if b == 0:
                                pe.wait_ge(sem["pt_made"][d], s + 1)
                            for h in range(HEADS):
                                mm = pe.transpose(bank(d, 1)[:, h * P:(h + 1) * P], T[d][:, h], m.ident)
                            mm.then_inc(sem["t_turned"][d], 1)
                        for d in range(2):
                            pe.wait_ge(sem["v_ready"][d], s * LV + (b + 1))
                            pe.wait_ge(sem["tt_ready"][d], s * LV + (b + 1))
                            for h in range(HEADS):
                                if b < LV - 1:
                                    mm = pe.matmul(bank(d, 0)[:, h * P:(h + 1) * P], TT[d][:, h], V[d][:, h],
                                                   start=True, stop=True)
                                else:
                                    mm = pe.matmul(bank(d, 1)[:, h * P:(h + 1) * P], V[d][:, h], TT[d][:, h],
                                                   start=True, stop=True)
                            mm.then_inc(sem["x_made"][d], 1)

                def new_values(step):
                    s = step[0]
                    for d in range(2):
                        pe.wait_ge(sem["tt_new"][d], s + 1)
                        pe.wait_ge(sem["rows_ready"][d], s + 1)
                        pe.wait_ge(sem["s_new"][d], s + 1)
                        pe.wait_ge(sem["o_added"][d], s + 1)
                        for h in range(HEADS):
                            mm = pe.matmul(bank(d, 2)[own(h), (h // 2) * P:(h // 2 + 1) * P], xk[d][:, h], TT[d][:, h],
                                           start=True, stop=True)
                        mm.then_inc(sem["w_made"][d], 1)
                    for d in range(2):
                        pe.wait_ge(sem["w_ready"][d], s + 1)
                        for hp in range(2):
                            cols = slice(BR + hp * P, BR + (hp + 1) * P)
                            pe.matmul(bank(d, 2)[:, cols], wt[d][:, hp], S[d][:, hp], start=True, stop=True,
                                      skip_group_check=True)
                            for h in (2 * hp, 2 * hp + 1):
                                cols = slice(BR + h * HD, BR + (h + 1) * HD)
                                mm = pe.matmul(bank(d, 2)[:, cols], TT[d][:, h], xv[d][:, h], start=False,
                                               stop=True, skip_group_check=True)
                        mm.then_inc(sem["vn_made"][d], 1)

                def finish(step):
                    s, _, wants = step
                    for d in range(2):
                        pe.wait_ge(sem["vn_ready"][d], s + 1)
                        pe.wait_ge(sem["qd_ready"][d], s + 1)
                        pe.wait_ge(sem["pt_ready"][d], s + 1)
                        if wants:
                            for hp in range(2):
                                cols = slice(hp * P, (hp + 1) * P)
                                pe.matmul(bank(d, 2)[:, cols], qd[d][:, hp], S[d][:, hp], start=True, stop=True,
                                      skip_group_check=True)
                                for h in (2 * hp, 2 * hp + 1):
                                    cols = slice(h * HD, (h + 1) * HD)
                                    mm = pe.matmul(bank(d, 2)[:, cols], PT[d][:, h], vn[d][:, h], start=False,
                                                   stop=True, skip_group_check=True)
                            mm.then_inc(sem["o_made"][d], 1)
                        else:
                            pe.sem_inc(sem["o_made"][d], 1)
                        for h in range(HEADS):
                            mm = pe.matmul(bank(d, 2)[own(h), BR + (h // 2) * HD:BR + (h // 2 + 1) * HD], kdec[d][:, h],
                                           vn[d][:, h], start=True, stop=True)
                        mm.then_inc(sem["s_made"][d], 1)

                def between(step, last):
                    if step:
                        scores(step[0])
                    if last:
                        new_values(last)
                    if step:
                        turn_a(step[0])
                    if last:
                        finish(last)
                steps(pe, between, inverse)

            @block.scalar
            def _(act):
                act.wait_ge(cleared, 5)

                def between(step, last):
                    for d in range(2):
                        if step:
                            act.wait_ge(sem["qk_made"][d], step[0] + 1)
                            for par in range(2):
                                rows = slice(64 * par, 64 * par + 64)
                                ins = act.activation(kz[d][rows, par:HEADS:2],
                                                     qkv[rows, 2:4, ds(step[1][d] * P, P)], ACT.Copy)
                            ins.then_inc(sem["kz_ready"][d], 1)
                    for d in range(2):
                        if last:
                            act.wait_ge(sem["w_made"][d], last[0] + 1)
                            act.activation(wt[d][:], bank(d, 2)[:, 0:2 * P].rearrange("p (h c) -> p h c", h=2), ACT.Copy,
                                           scale=-1.0).then_inc(sem["w_ready"][d], 1)
                    for d in range(2):
                        if step:
                            act.wait_ge(sem["e_in"][d], step[0] + 1)
                            act.activation(E[d][:], E[d][:], ACT.Exp).then_inc(sem["e_exp"][d], 1)
                            act.activation(EG[d][:], wide(bank(d, 3)), ACT.Exp).then_inc(sem["eg_done"][d], 1)
                    for d in range(2):
                        if last:
                            act.wait_ge(sem["vn_made"][d], last[0] + 1)
                            act.activation(vn[d][:], wide(bank(d, 2)[:, BR:2 * BR]), ACT.Copy
                                           ).then_inc(sem["vn_ready"][d], 1)
                    for d in range(2):
                        if step:
                            act.wait_ge(sem["at_turned"][d], step[0] + 1)
                            act.activation(AT[d][:], wide(bank(d, 3)), ACT.Copy).then_inc(sem["at_ready"][d], 1)

                def inverse(step):
                    s = step[0]
                    for b in range(LV):
                        for d in range(2):
                            act.wait_ge(sem["v_made"][d], s * LV + (b + 2))
                            if b == 0:
                                act.wait_ge(sem["qd_ready"][d], s + 1)
                            act.activation(V[d][:], wide(bank(d, 3)), ACT.Copy).then_inc(sem["v_ready"][d], 1)
                            act.wait_ge(sem["t_turned"][d], s * LV + (b + 1))
                            act.activation(TT[d][:], wide(bank(d, 1)), ACT.Copy).then_inc(sem["tt_ready"][d], 1)
                steps(act, between, inverse)

            @block.vector
            def _(dve):
                for x in (S[0][:], S[1][:], kz[0][:], kz[1][:], o):
                    dve.memset(x, 0.0).then_inc(cleared, 1)
                for d in range(2):
                    dve.sem_inc(sem["s_new"][d], 1)
                    dve.sem_inc(sem["o_added"][d], 1)
                dve.wait_ge(loaded, 32)
                dve.wait_ge(cleared, 5)
                PER = 3
                ident4 = m.ident.rearrange("p (a c) -> p a c", a=1).to_broadcast([P, HEADS, P])

                def start(s, tiles):
                    step = [Tally(sem["dve_step"][d], 0, s, PER) for d in range(2)]
                    for d in range(2):
                        dve.wait_ge(sem["grams"][d], s + 1)
                        ins = dve.tensor_tensor(E[d][:], wide(bank(d, 3)), per_head(g.gam, tiles[d], d, P), ALU.subtract)
                        step[d].did(ins)
                    for d in range(2):
                        step[d].wait(dve)
                        dve.scalar_tensor_tensor(out=E[d][:], in0=E[d][:], scalar=-1.0, in1=E[d][:], op0=ALU.mult,
                                                 op1=ALU.min).then_inc(sem["e_in"][d], 1)
                    for d in range(2):
                        dve.wait_ge(sem["e_exp"][d], s + 1)
                        step[d].did(dve.tensor_tensor(A[d][:], wide(bank(d, 0)), E[d][:], ALU.mult))
                    for d in range(2):
                        step[d].wait(dve)
                        dve.tensor_tensor(A[d][:], A[d][:], per_head(g.beta, tiles[d], d, P), ALU.mult
                                          ).then_inc(sem["a_ready"][d], 1)
                    for d in range(2):
                        dve.wait_ge(sem["a_ready"][d], s + 1)
                        step[d].did(dve.tensor_tensor(T[d][:], A[d][:], lv[:, d, 0:1].to_broadcast([P, HEADS, P]), ALU.mult))
                    for d in range(2):
                        step[d].wait(dve)
                        dve.scalar_tensor_tensor(out=T[d][:], in0=T[d][:], scalar=-1.0, in1=ident4, op0=ALU.mult,
                                                 op1=ALU.add).then_inc(sem["t_ready"][d], 1)
                    for d in range(2):
                        step[d].close()

                def queries(s):
                    for d in range(2):
                        dve.wait_ge(sem["eg_done"][d], s + 1)
                        dve.wait_ge(sem["s_made"][d], s + 1)
                        dve.wait_ge(sem["staged"][d], s + 1)
                        for par in range(2):
                            rows = slice(64 * par, 64 * par + 64)
                            ins = dve.tensor_tensor(qd[d][rows], staged_t[d][rows, 0:2], EG[d][rows, par:HEADS:2],
                                                    ALU.mult)
                        ins.then_inc(sem["qd_ready"][d], 1)
                    for d in range(2):
                        dve.wait_ge(sem["qk_made"][d], s + 2)
                        dve.tensor_tensor(PT[d][:], wide(bank(d, 1)), E[d][:], ALU.mult).then_inc(sem["pt_made"][d], 1)

                def inverse(step):
                    s = step[0]
                    for b in range(LV):
                        for d in range(2):
                            dve.wait_ge(sem["x_made"][d], s * LV + (b + 1))
                            if b < LV - 1:
                                if b == 0:
                                    dve.wait_ge(sem["t_ready"][d], s + 1)
                                else:
                                    dve.wait_ge(sem["t_new"][d], s * (LV - 1) + b)
                                dve.tensor_tensor(T[d][:], T[d][:], wide(bank(d, 0)), ALU.subtract
                                                  ).then_inc(sem["t_new"][d], 1)
                            else:
                                dve.tensor_tensor(TT[d][:], TT[d][:], wide(bank(d, 1)), ALU.subtract
                                                  ).then_inc(sem["tt_new"][d], 1)

                def finish(step):
                    s, tiles, wants = step
                    for d in range(2):
                        dve.wait_ge(sem["s_made"][d], s + 2)
                        for par in range(2):
                            rows = slice(64 * par, 64 * par + 64)
                            by = g.last[rows, ds(tiles[d], 1), d].rearrange("p a h -> p h a").to_broadcast([64, 2, HD])
                            ins = dve.tensor_tensor(S[d][rows, :, par], S[d][rows, :, par], by, ALU.mult)
                        ins.then_inc(sem["s_scaled"][d], 1)
                        dve.wait_ge(sem["s_scaled"][d], s + 1)
                        for par in range(2):
                            rows = slice(64 * par, 64 * par + 64)
                            ins = dve.tensor_tensor(S[d][rows, :, par], S[d][rows, :, par],
                                                    bank(d, 2)[rows, BR:BR + 2 * HD].rearrange("p (h c) -> p h c", h=2), ALU.add)
                        ins.then_inc(sem["s_new"][d], 1)
                        if wants:
                            dve.wait_ge(sem["o_made"][d], s + 1)
                            row = o[:, ds(tiles[d], 1)].rearrange("p a c -> p (a c)")
                            ins = dve.tensor_tensor(row, row, bank(d, 2)[:, 0:BR], ALU.add)
                            ins.then_inc(sem["o_added"][d], 1)
                            dve.wait_ge(sem["o_added"][d], s + 2)
                        else:
                            dve.sem_inc(sem["o_added"][d], 1)

                def between(step, last):
                    if step:
                        start(step[0], step[1])
                    if step:
                        queries(step[0])
                    if last:
                        finish(last)
                steps(dve, between, inverse)


class Gates:
    pass


def delta_net(nc, m, l):
    tiles = range(0 if l < DEPTH - 1 else CT, NT)
    with ExitStack() as st:
        sb = lambda n, s, d=F32: st.enter_context(nc.sbuf_tensor(f"{n}_dn{l}", s, d))
        g = Gates()
        g.gam, g.eg, g.kd, g.beta, g.be = (sb(n, [P, NT, MAPS]) for n in ("gam", "eg", "kd", "beta", "be"))
        g.last = sb("glast", [P, NT, 2, 2])
        vecs = sb("vecs", [P, HD])
        qkv = sb("qkv", [P, 6, ROWS])
        kv = sb("kv", [P, NT, 2 * BR])
        o = qkv[:, 4:6].rearrange("p j c -> p (j c)").rearrange("p (t c) -> p t c", t=NT)
        project(nc, m, l, T_DN, 6, qkv, CHUNKS, "pn")
        convolve(nc, m, l, qkv)
        normalise_columns(nc, m, l, "nn", qkv, [[0], [1], [2], [3]], m.blocks, lambda j: HD ** -0.5 if j < 2 else 1.0,
                          lambda g: 1, None)
        turn_keys(nc, m, l, qkv, kv)
        decay_gates(nc, m, l, g)
        delta_rule(nc, m, l, qkv, kv, o, g)
        with phase(nc, "loaded") as (block, loaded):
            @block.sync
            def _(sp):
                sp.dma_start(vecs[:], m.d_bvec[l:l + 1, B_DNN:B_DNN + HD].to_broadcast([P, HD])).then_inc(loaded, 16)
                sp.wait_ge(loaded, 16)
        normalise_heads(nc, m, l, "nh", o, tiles, vecs[:])
        store_rows(nc, m, l, 3, o, tiles)


def gate_branches(nc, m, l, yh, yl, chunks):
    n = len(chunks)
    lo = chunks[0][0]
    tiles = 2 * 4
    with ExitStack() as st:
        sb = lambda n, s, d=F32: st.enter_context(nc.sbuf_tensor(f"{n}_gb{l}", s, d))
        w = sb("w", [P, 2, KD, P])
        wh = sb("wh", [P, 2, KD, P], F32R)
        wl = sb("wl", [P, 2, KD, P], F32R)
        gate = sb("gate", [P, 2, ROWS])
        y = m.dv[:].rearrange("p t c -> p (t c)").rearrange("p (s c) -> p s c", s=2)
        with phase(nc, "y_in0", "y_in1", "w_in0", "w_in1", "w_high", "w_low", "made", "silu", "gated", "y_high",
                   "y_low") as (block, y_in0, y_in1, w_in0, w_in1, w_high, w_low, made, silu, gated, y_high, y_low):
            w_in, y_in = [w_in0, w_in1], [y_in0, y_in1]

            @block.sync
            def _(sp):
                for s in range(2):
                    sp.dma_start(w[:, s], m.d_win[l, T_GATE + s]).then_inc(w_in[s], 16)
                    sp.dma_start(y[:, s, lo:], m.d_y[:, s, lo:]).then_inc(y_in[s], 16)
                with sp.Fori(1, tiles // 2) as i:
                    for s in range(2):
                        sp.wait_ge(w_low, i * 2 + (s - 1))
                        sp.dma_start(w[:, s], m.d_win[l, i * 2 + (T_GATE + s)]).then_inc(w_in[s], 16)
                        sp.wait_ge(y_low, i * (2 * n) + (s + 1 - 2) * n)
                        sp.dma_start(y[:, s, lo:], m.d_y[:, ds(i * 2 + s, 1), lo:].rearrange("p a c -> p (a c)")
                                     ).then_inc(y_in[s], 16)

            def stages(eng, cut, move):
                def body(i, last):
                    for s in range(2):
                        for c, (at, width) in enumerate(chunks):
                            if c == 1 and not (last and s == 1):
                                cut(i + s, 1 - s)
                            move(i, s, s * n + c, at, width)
                cut(0, 0)
                with eng.Fori(0, tiles // 2 - 1) as i:
                    body(i, False)
                body(tiles // 2 - 1, True)

            @block.scalar
            def _(act):
                act.sem_inc(silu, 2 * n)

                def cut(i, s):
                    act.wait_ge(w_in[s], i * 16 + 16)
                    act.wait_ge(made, i * (2 * n) + (s + 1) * n)
                    act.activation(wh[:, s], w[:, s], ACT.Copy).then_inc(w_high, 1)

                def move(i, s, u, at, width):
                    act.wait_ge(made, i * (2 * n) + (2 * n + u + 1))
                    act.wait_ge(gated, i * (2 * n) + (u + 1))
                    act.activation(gate[:, s, at:at + width], m.ps[:, u, 0:width], ACT.Silu).then_inc(silu, 1)
                    act.wait_ge(gated, i * (2 * n) + (2 * n + u + 1))
                    act.activation(yh[:, ds(i * 2 + s, 1), at:at + width].rearrange("p a c -> p (a c)"),
                                   y[:, s, at:at + width], ACT.Copy).then_inc(y_high, 1)
                stages(act, cut, move)

            @block.vector
            def _(dve):
                dve.sem_inc(gated, 2 * n)

                def cut(i, s):
                    dve.wait_ge(w_high, i * 2 + (s + 1))
                    dve.tensor_tensor(wl[:, s], w[:, s], wh[:, s].bitcast(F32), ALU.subtract).then_inc(w_low, 1)

                def move(i, s, u, at, width):
                    dve.wait_ge(silu, i * (2 * n) + (2 * n + u + 1))
                    dve.wait_ge(y_in[s], i * 16 + 16)
                    own = y[:, s, at:at + width]
                    dve.tensor_tensor(own, own, gate[:, s, at:at + width], ALU.mult).then_inc(gated, 1)
                    dve.wait_ge(y_high, i * (2 * n) + (u + 1))
                    high, low = (x[:, ds(i * 2 + s, 1), at:at + width].rearrange("p a c -> p (a c)") for x in (yh, yl))
                    dve.tensor_tensor(low, own, high.bitcast(F32), ALU.subtract).then_inc(y_low, 1)
                stages(dve, cut, move)

            @block.tensor
            def _(pe):
                pe.sem_inc(made, 2 * n)
                with pe.Fori(0, tiles // 2) as i:
                    for s in range(2):
                        pe.wait_ge(w_low, i * 2 + (s + 1))
                        for c, (at, width) in enumerate(chunks):
                            u = s * n + c
                            pe.wait_ge(silu, i * (2 * n) + (u + 1))
                            for k in range(KD):
                                mm = split_products(pe, m.ps[:, u, 0:width], wh[:, s, k], wl[:, s, k],
                                                    m.hh[:, k, at:at + width], m.hl[:, k, at:at + width],
                                                    k == 0, k == KD - 1)
                            mm.then_inc(made, 1)


def merge(nc, m, l):
    chunks = list(enumerate(CHUNKS))[0 if l < DEPTH - 1 else 1:]
    n_c = len(chunks)
    lo = chunks[0][1][0]
    with ExitStack() as st:
        sb = lambda n, s, d=F32: st.enter_context(nc.sbuf_tensor(f"{n}_mg{l}", s, d))
        yh = sb("yh", [P, 2 * 4, ROWS], F32R)
        yl = sb("yl", [P, 2 * 4, ROWS], F32R)
        gate_branches(nc, m, l, yh, yl, [c for _, c in chunks])
        w = sb("w", [P, 2, KD + 2, P])
        wh = sb("wh", [P, 2, KD + 2, P], F32R)
        wl = sb("wl", [P, 2, KD + 2, P], F32R)
        sg = sb("sg", [P, 2, 512])
        spare = m.dv[:].rearrange("p t c -> p (t c)")
        acc = spare[:, 0:ROWS]
        term = spare[:, ROWS:ROWS + 2 * 512].rearrange("p (a c) -> p a c", a=2)
        N = 4 * n_c
        with phase(nc, "w_in0", "w_in1", "w_high", "w_low", "gated", "branched", "sigm",
                   "multiplied", "added", "stored") as (
                block, w_in0, w_in1, w_high, w_low, gated, branched, sigm, multiplied, added, stored):
            w_in = [w_in0, w_in1]

            @block.sync
            def _(sp):
                sp.sem_inc(stored, 16)
                for s in range(2):
                    sp.dma_start(w[:, s], m.d_wmerge[l, s]).then_inc(w_in[s], 16)

                def body(f, loads):
                    for b in range(loads):
                        s = b % 2
                        sp.wait_ge(branched, f * N + (b + 3) * n_c)
                        sp.dma_start(w[:, s], m.d_wmerge[l, f * 4 + (b + 2)]).then_inc(w_in[s], 16)
                    sp.wait_ge(added, f * N + N)
                    sp.dma_start(m.d_acc[:, ds(f, 1), lo:], acc[:, lo:].rearrange("p (a c) -> p a c", a=1)
                                 ).then_inc(stored, 16)
                with sp.Fori(0, KD - 1) as f:
                    body(f, 4)
                body(KD - 1, 2)
                sp.wait_ge(stored, 16 * KD + 16)

            @block.scalar
            def _(act):
                def cut(f, b):
                    act.wait_ge(w_in[b % 2], f * 32 + 16 * (b // 2 + 1))
                    act.wait_ge(branched, f * N + (b + 1) * n_c)
                    act.activation(wh[:, b % 2], w[:, b % 2], ACT.Copy).then_inc(w_high, 1)

                def body(f, last):
                    for b in range(4):
                        for n, (c, (at, width)) in enumerate(chunks):
                            if n == 1 and not (last and b == 3):
                                cut(f + b // 3, (b + 1) % 4)
                            u = b * n_c + n
                            act.wait_ge(gated, f * N + (u + 1))
                            act.wait_ge(multiplied, f * N + (u + 3))
                            act.activation(sg[:, u % 2, 0:width], m.ps[:, u % 4, 0:width], ACT.Sigmoid
                                           ).then_inc(sigm, 1)
                cut(0, 0)
                with act.Fori(0, KD - 1) as f:
                    body(f, False)
                body(KD - 1, True)

            @block.tensor
            def _(pe):
                pe.sem_inc(branched, 2 * n_c)
                with pe.Fori(0, KD) as f:
                    for b in range(4):
                        s = b % 2
                        pe.wait_ge(w_low, f * 4 + (b + 1))
                        for n, (c, (at, width)) in enumerate(chunks):
                            u = b * n_c + n
                            pe.wait_ge(multiplied, f * N + (u + 1))
                            for k in range(KD):
                                mm = split_products(pe, m.ps[:, u % 4, 0:width], wh[:, s, k], wl[:, s, k],
                                                    m.hh[:, k, at:at + width], m.hl[:, k, at:at + width],
                                                    k == 0, k == KD - 1)
                            mm.then_inc(gated, 1)
                            for k in range(2):
                                mm = split_products(pe, m.ps[:, 4 + u % 4, 0:width], wh[:, s, KD + k],
                                                    wl[:, s, KD + k], yh[:, 2 * b + k, at:at + width],
                                                    yl[:, 2 * b + k, at:at + width], k == 0, k == 1)
                            mm.then_inc(branched, 1)

            @block.vector
            def _(dve):
                dve.sem_inc(multiplied, 4)

                def cut(f, b):
                    dve.wait_ge(w_high, f * 4 + (b + 1))
                    dve.tensor_tensor(wl[:, b % 2], w[:, b % 2], wh[:, b % 2].bitcast(F32), ALU.subtract
                                      ).then_inc(w_low, 1)

                def body(f, last):
                    for b in range(4):
                        for n, (c, (at, width)) in enumerate(chunks):
                            if n == 1 and not (last and b == 3):
                                cut(f + b // 3, (b + 1) % 4)
                            u = b * n_c + n
                            dve.wait_ge(sigm, f * N + (u + 1))
                            dve.wait_ge(branched, f * N + (u + 1 + 2 * n_c))
                            if b == 0:
                                if n == 0:
                                    dve.wait_ge(stored, f * 16 + 16)
                                dst = acc[:, at:at + width]
                            else:
                                dst = term[:, u % 2, 0:width]
                            dve.tensor_tensor(dst, sg[:, u % 2, 0:width], m.ps[:, 4 + u % 4, 0:width], ALU.mult
                                              ).then_inc(multiplied, 1)
                            dve.wait_ge(multiplied, f * N + (u + 5))
                            if b:
                                dve.tensor_tensor(acc[:, at:at + width], acc[:, at:at + width], dst, ALU.add
                                                  ).then_inc(added, 1)
                                dve.wait_ge(added, f * N + (u + 1))
                            else:
                                dve.sem_inc(added, 1)
                cut(0, 0)
                with dve.Fori(0, KD - 1) as f:
                    body(f, False)
                body(KD - 1, True)


def output(nc, m, l, out):
    tiles = range(0 if l < DEPTH - 1 else CT, NT)
    src = m.d_x if l == 0 else m.d_x1
    wo_h, wo_l = m.hh[:, :, 0:D], m.hl[:, :, 0:D]
    with ExitStack() as st:
        sb = lambda n, s, d=F32: st.enter_context(nc.sbuf_tensor(f"{n}_ou{l}", s, d))
        w = sb("w", [P, KD, D])
        x = sb("x", [P, 2, D])
        r = sb("r", [P, 2, D])
        acc = sb("acc", [P, 2, KD, P])
        ah = sb("ah", [P, 2, KD, P], F32R)
        al = sb("al", [P, 2, KD, P], F32R)
        gate = sb("gate", [P, 2, D])
        lng = sb("lng", [P, 2, D])
        stats = sb("stats", [P, NT, 2, 6])
        mv = sb("mv", [P, NT, 2])
        std = sb("std", [P, NT])
        rstd = sb("rstd", [P, NT])
        with phase(nc, "small_in", "w_in0", "w_in1", "w_in2", "w_in3", "w_high", "w_low", "a_in0", "a_in1", "a_high", "a_low", "made",
                   "x_in0", "x_in1", "var_done", "std_done", "dve_step", "row_done", "stored0", "stored1", "used") as (
                block, small_in, w_in0, w_in1, w_in2, w_in3, w_high, w_low, a_in0, a_in1, a_high, a_low, made,
                x_in0, x_in1, var_done, std_done, dve_step, row_done, stored0, stored1, used):
            w_in, a_in, x_in, stored = [w_in0, w_in1, w_in2, w_in3], [a_in0, a_in1], [x_in0, x_in1], [stored0, stored1]

            def rows_out(t):
                if l < DEPTH - 1:
                    return m.d_x1[t * P:(t + 1) * P, :]
                return out[(t - CT) * P:(t - CT + 1) * P, :]

            @block.sync
            def _(sp):
                def rows_in(n):
                    t = tiles[n]
                    sp.dma_start(acc[:, n % 2], m.d_acc[:, :, t * P:(t + 1) * P]).then_inc(a_in[n % 2], 16)
                    sp.dma_start(x[:, n % 2], src[t * P:(t + 1) * P, :]).then_inc(x_in[n % 2], 16)

                for j in range(4):
                    sp.dma_start(w[:, 2 * j:2 * j + 2], m.d_wout[l, 2 * j:2 * j + 2].rearrange("k p d -> p k d")
                                 ).then_inc(w_in[j], 16)
                    if j < 2:
                        rows_in(j)
                sp.dma_start(gate[:], m.d_gate.rearrange("(c t) p -> c (t p)", c=2).rearrange(
                    "(a c) n -> a c n", a=1).to_broadcast([P, 2, D])).then_inc(small_in, 16)
                sp.dma_start(lng[:], m.d_bvec[l:l + 1, 0:2 * D].rearrange("a (c n) -> a c n", c=2
                                                                          ).to_broadcast([P, 2, D])).then_inc(small_in, 16)
                for n, t in enumerate(tiles):
                    if n >= 2:
                        sp.wait_ge(a_low, n - 1)
                        sp.wait_ge(used, n - 1)
                        rows_in(n)
                    if n >= 1:
                        sp.wait_ge(row_done, n)
                        sp.dma_start(rows_out(tiles[n - 1]), r[:, (n - 1) % 2]).then_inc(stored[(n - 1) % 2], 16)
                n = len(tiles)
                sp.wait_ge(row_done, n)
                sp.dma_start(rows_out(tiles[-1]), r[:, (n - 1) % 2]).then_inc(stored[(n - 1) % 2], 16)
                for s in range(2):
                    sp.wait_ge(stored[s], 16 * len(range(s, n, 2)))

            @block.scalar
            def _(act):
                def high(n):
                    act.wait_ge(a_in[n % 2], 16 * (n // 2 + 1))
                    if n >= 2:
                        act.wait_ge(made, n - 1)
                    act.activation(ah[:, n % 2], acc[:, n % 2], ACT.Copy).then_inc(a_high, 1)

                for k in range(KD):
                    act.wait_ge(w_in[k // 2], 16)
                    act.activation(wo_h[:, k], w[:, k], ACT.Copy).then_inc(w_high, 1)
                    if k == 0:
                        high(0)
                for n, t in enumerate(tiles):
                    if n >= 1:
                        high(n)
                    if n >= 1:
                        act.wait_ge(var_done, n)
                        act.activation(std[:, n - 1:n], mv[:, n - 1, 1:2], ACT.Sqrt, bias=m.eps[:, 0:1]
                                       ).then_inc(std_done, 1)
                n = len(tiles)
                act.wait_ge(var_done, n)
                act.activation(std[:, n - 1:n], mv[:, n - 1, 1:2], ACT.Sqrt, bias=m.eps[:, 0:1]).then_inc(std_done, 1)

            @block.tensor
            def _(pe):
                for n, t in enumerate(tiles):
                    pe.wait_ge(a_low, n + 1)
                    if n >= 2:
                        pe.wait_ge(used, n - 1)
                    for k in range(KD):
                        if n == 0:
                            pe.wait_ge(w_low, k + 1)
                        for c in range(2):
                            mm = split_products(pe, m.ps[:, 2 * (n % 2) + c], ah[:, n % 2, k], al[:, n % 2, k],
                                                wo_h[:, k, 512 * c:512 * c + 512], wo_l[:, k, 512 * c:512 * c + 512],
                                                k == 0, k == KD - 1)
                    mm.then_inc(made, 1)

            @block.vector
            def _(dve):
                step = Tally(dve_step)
                then = lambda ins: step.then(dve, ins)
                def low(n):
                    dve.wait_ge(a_high, n + 1)
                    dve.tensor_tensor(al[:, n % 2], acc[:, n % 2], ah[:, n % 2].bitcast(F32), ALU.subtract
                                      ).then_inc(a_low, 1)
                for k in range(KD):
                    dve.wait_ge(w_high, k + 1)
                    dve.tensor_tensor(wo_l[:, k], w[:, k], wo_h[:, k].bitcast(F32), ALU.subtract).then_inc(w_low, 1)
                    if k == 0:
                        low(0)
                dve.wait_ge(small_in, 32)
                for n, t in enumerate(tiles):
                    s = n % 2
                    if n + 1 < len(tiles):
                        low(n + 1)
                    g = 0 if t >= CT else 1
                    dve.wait_ge(made, n + 1)
                    dve.wait_ge(x_in[s], 16 * (n // 2 + 1))
                    if n >= 2:
                        dve.wait_ge(stored[s], 16 * (n // 2))
                    row = r[:, s].rearrange("p (c n) -> p c n", c=2)
                    then(dve.tensor_tensor(row, m.ps[:, 2 * s:2 * s + 2], gate[:, g].rearrange("p (c n) -> p c n", c=2),
                                           ALU.mult))
                    ins = dve.scalar_tensor_tensor(out=r[:, s], in0=x[:, s], scalar=ALPHA, in1=r[:, s], op0=ALU.mult,
                                                   op1=ALU.add)
                    ins.then_inc(used, 1)
                    dve.wait_ge(used, n + 1)
                    for j in range(2):
                        ins = dve.bn_stats(stats[:, n, j], r[:, s, 512 * j:512 * j + 512])
                    then(ins)
                    dve.bn_aggr(mv[:, n], stats[:, n]).then_inc(var_done, 1)
                    dve.wait_ge(std_done, n + 1)
                    then(dve.reciprocal(rstd[:, n:n + 1], std[:, n:n + 1]))
                    then(dve.tensor_scalar(r[:, s], r[:, s], mv[:, n, 0:1], rstd[:, n:n + 1], ALU.subtract, ALU.mult))
                    then(dve.tensor_tensor(r[:, s], r[:, s], lng[:, 0], ALU.mult))
                    dve.tensor_tensor(r[:, s], r[:, s], lng[:, 1], ALU.add).then_inc(row_done, 1)


def build(nc, d_x, d_c, d_const, d_rope, d_vec, d_bvec, d_wmod, d_win, d_winr, d_ws, d_bs, d_wuq, d_wukv,
          d_wmerge, d_wout, out, only=None, kind="Internal"):
    m = Mem()
    m.d_x, m.cvec, m.d_const, m.d_rope, m.d_vec, m.d_bvec, m.d_wmod = d_x, d_c, d_const, d_rope, d_vec, d_bvec, d_wmod
    m.d_win, m.d_winr, m.d_ws, m.d_bs, m.d_wuq, m.d_wukv = d_win, d_winr, d_ws, d_bs, d_wuq, d_wukv
    m.d_wmerge, m.d_wout = d_wmerge, d_wout
    m.d_x1 = nc.dram_tensor("x1", [ROWS, D], F32, kind=kind).ap()
    m.d_gate = nc.dram_tensor("gate_rows", [16, P], F32, kind=kind).ap()
    m.d_y = nc.dram_tensor("branches", [P, 8, ROWS], F32, kind=kind).ap()
    m.d_acc = nc.dram_tensor("merged", [P, KD, ROWS], F32, kind=kind).ap()
    with ExitStack() as st:
        sb = lambda n, s, d=F32: st.enter_context(nc.sbuf_tensor(n, s, d))
        m.ps = st.enter_context(nc.psum_tensor("ps", [P, 8, 512], F32))
        const = sb("const", [P, 3, P])
        m.ident, m.ones, m.blocks = const[:, 0], const[:, 1], const[:, 2]
        m.eps = sb("eps", [P, 1])
        m.vec = sb("vec", [P, V_COLS])
        m.shift = sb("shift", [P, KD, 2])
        m.scale = sb("scale", [P, KD, 2])
        m.gate_c = sb("gate_c", [P, 16])
        m.dv = sb("dv", [P, NT, BR])
        m.ab = sb("ab", [P, NT, 16])
        m.hh = sb("hh", [P, KD, ROWS], F32R)
        m.hl = sb("hl", [P, KD, ROWS], F32R)
        with phase(nc, "loaded") as (block, loaded):
            @block.sync
            def _(sp):
                sp.dma_start(const[:, 0:2], d_const[:, C_ID:C_ID + 2]).then_inc(loaded, 16)
                sp.dma_start(const[:, 2], d_const[:, C_BLK]).then_inc(loaded, 16)
                sp.wait_ge(loaded, 32)

            @block.vector
            def _(dve):
                dve.memset(m.eps[:], EPS)
        for l in range(DEPTH):
            for name, part in (("mod", modulation), ("ln", normalise_rows), ("gmlp", gating_mlp),
                               ("mla", latent_attention), ("diff", differential_attention), ("dn", delta_net),
                               ("merge", merge)):
                if only is None or (l, name) in only:
                    part(nc, m, l)
            if only is None or (l, "out") in only:
                output(nc, m, l, out)
        return m


def layouts(x, c, ctx, c_ctx, w_mod, b_mod, w_in, mla_q_norm, mla_w_uq, mla_kv_norm, mla_w_ukv, gmlp_ln_g, gmlp_w_s,
            gmlp_b_s, diff_lq1, diff_lk1, diff_lq2, diff_lk2, diff_norm_g, dn_conv_w, dn_a_log, dn_dt_bias, dn_norm_g,
            w_gate, w_branch, w_out, ln_g, ln_b):
    import numpy as np
    L = DEPTH
    A = np.asarray
    w_in, w_mod, w_gate, w_branch = A(w_in), A(w_mod), A(w_gate), A(w_branch)

    def blocks(w):
        n, k, c = w.shape
        return np.ascontiguousarray(w.reshape(n, k // P, P, c // P, P).transpose(0, 3, 2, 1, 4))

    def columns(v):
        return v.reshape(L, -1, P).transpose(0, 2, 1)

    dn0 = 416 + 512 + 768
    zero = np.zeros((L, D, P - ROPE), np.float32)
    w_t = np.concatenate([w_in[:, :, 0:416], zero, w_in[:, :, 928:928 + 512], w_in[:, :, dn0:dn0 + 768],
                          w_in[:, :, dn0 + 784:]], axis=2)
    w_r = np.concatenate([w_in[:, :, 416:928], w_in[:, :, 928 + 512:928 + 768],
                          w_in[:, :, dn0 + 768:dn0 + 784]], axis=2)
    uq = A(mla_w_uq).reshape(L, 2, P, HEADS, QK)
    uq = np.concatenate([uq[..., NOPE:].reshape(L, 2, P, HEADS * ROPE), uq[..., :NOPE].reshape(L, 2, P, HEADS * NOPE)],
                        axis=3).transpose(0, 2, 1, 3)
    ukv = A(mla_w_ukv).reshape(L, P, HEADS, 2, HD).transpose(0, 1, 3, 2, 4).reshape(L, P, 2 * HEADS * HD)
    gate_t = np.stack([blocks(w_gate[:, b]) for b in range(4)], axis=2)
    branch_t = np.stack([blocks(w_branch[:, b]) for b in range(4)], axis=2)
    merge_t = np.concatenate([gate_t, branch_t], axis=4).reshape(L, KD * 4, P, KD + 2, P)
    pad = np.zeros((L, 2, P, KD + 2, P), np.float32)
    conv = A(dn_conv_w).reshape(L, 3, 6, P).transpose(0, 3, 1, 2).reshape(L, P, 18)
    vec = np.concatenate([columns(A(b_mod)), columns(A(mla_q_norm)), columns(A(mla_kv_norm)), conv], axis=2)
    bvec = np.concatenate([A(ln_g), A(ln_b), A(gmlp_ln_g), A(diff_norm_g), A(dn_norm_g), A(diff_lq1), A(diff_lk1),
                           A(diff_lq2), A(diff_lk2), A(dn_a_log).reshape(L, 8), A(dn_dt_bias).reshape(L, 8)], axis=1)
    const = np.zeros((C_N, P, P), np.float32)
    i, j = np.arange(P)[:, None], np.arange(P)[None, :]
    const[C_ID] = i == j
    const[C_ONE] = 1
    const[C_PERM] = (i ^ 8) == j
    const[C_BLK] = i // HD == j // HD
    const[C_TRIF] = i <= j
    const[C_TRIB] = i >= j
    for r in range(4):
        source, high = i == 32 * r + j % 32, j // 32 % 2 == 0
        const[C_REP + r], const[C_REP + 4 + r] = source & high, source & ~high
    for v in range(LEVELS):
        b = 1 << v
        joins = (i // (2 * b) == j // (2 * b)) & (i // b % 2 == 1) & (j // b % 2 == 0)
        const[C_LVF + v], const[C_LVB + v] = joins, joins.T
    at = np.arange(SEQ, dtype=np.float32)
    line, col = np.floor(at / 64).astype(np.float32), at % 64
    freq = (np.float32(10000.0) ** (-np.arange(0, 16, 2, dtype=np.float32) / np.float32(16))).astype(np.float32)
    angle = np.concatenate([np.tile(freq[:, None] * line[None], (2, 1)), np.tile(freq[:, None] * col[None], (2, 1))])
    sign = np.where(np.arange(32) % 16 < 8, -1.0, 1.0).astype(np.float32)[:, None]
    rope = np.stack([np.tile(np.cos(angle), (4, 1)), np.tile(np.sin(angle) * sign, (4, 1))], axis=1)
    f = lambda a: np.ascontiguousarray(a, dtype=np.float32)
    cv = np.stack([A(c)[0], A(c_ctx)], axis=1).reshape(KD, P, 2).transpose(1, 0, 2)
    return {
        "d_x": f(np.concatenate([A(ctx)[0], A(x)[0]], axis=0)), "d_c": f(cv), "d_const": f(const.transpose(1, 0, 2)),
        "d_rope": f(rope), "d_vec": f(vec), "d_bvec": f(bvec), "d_wmod": f(blocks(w_mod)), "d_win": f(blocks(w_t)),
        "d_winr": f(w_r.reshape(L, KD, P, R_COLS)), "d_ws": f(A(gmlp_w_s).transpose(0, 3, 1, 2)),
        "d_bs": f(A(gmlp_b_s).transpose(0, 2, 1)), "d_wuq": f(uq), "d_wukv": f(ukv),
        "d_wmerge": f(np.concatenate([merge_t, pad], axis=1)), "d_wout": f(A(w_out).reshape(L, KD, P, D)),
    }


def kernel(**inputs):
    import numpy as np
    import concourse.bacc as bacc
    from concourse.bass_utils import run_bass_kernel_spmd

    nc = bacc.Bacc("TRN2", target_bir_lowering=False, num_devices=1)
    arrays = layouts(**inputs)
    aps = {n: nc.dram_tensor(f"in_{n}", list(a.shape), mybir.dt.from_np(a.dtype), kind="ExternalInput").ap()
           for n, a in arrays.items()}
    out = nc.dram_tensor("out_x", [SEQ, D], F32, kind="ExternalOutput").ap()
    build(nc, out=out, **aps)
    r = run_bass_kernel_spmd(nc, [{f"in_{n}": a for n, a in arrays.items()}], core_ids=[0])
    return r.results[0]["out_x"].reshape(1, SEQ, D)
```
